# Optimizing a Trainium2 kernel written in Bass

```python
import jax, jax.numpy as jnp
from jax import lax
import numpy as np

D_MODEL = 1024
BATCH = 1
SEQ = 512
DEPTH = 1

N_META = 16
MIX_WIDTH = D_MODEL
ATTN_WIDTH = MIX_WIDTH // 2
CONV_WIDTH = MIX_WIDTH - ATTN_WIDTH
HEAD_DIM = 64
N_ATTN_HEADS = ATTN_WIDTH // HEAD_DIM
Q_BLOCK = 128
CONV_K = 3
N_EXPERTS = 32
TOP_K = 4
D_FF = D_MODEL
SWIGLU_LIMIT = 7.0
SWIGLU_ALPHA = 1.702
MOE_BLOCK = 128
RMS_EPS = 1e-6
PROJ_WIDTH = 3 * ATTN_WIDTH + 3 * CONV_WIDTH

kernel_name = "hymba_stickbreak_shortconv_moe"

def rms_norm(x, g):
    xf = x.astype(jnp.float32)
    y = xf * lax.rsqrt(jnp.mean(xf * xf, axis=-1, keepdims=True) + RMS_EPS)
    return (y * g.astype(jnp.float32)).astype(x.dtype)

def stick_breaking_attention(q, k, v):
    b, h, t, d = q.shape
    pad = (-N_META) % Q_BLOCK
    n_blocks = -(-(pad + t) // Q_BLOCK)
    tail = n_blocks * Q_BLOCK - pad - t
    padw = ((0, 0), (0, 0), (pad, tail), (0, 0))
    qp, kp, vp = [jnp.pad(a, padw) for a in (q, k, v)]
    scale = d ** -0.5
    outs = []
    for i in range(n_blocks):
        q0, q1 = i * Q_BLOCK, (i + 1) * Q_BLOCK
        qb = qp[:, :, q0:q1]
        kb = kp[:, :, :q1]
        vb = vp[:, :, :q1]
        z = jnp.einsum('bhqd,bhkd->bhqk', qb, kb).astype(jnp.float32) * scale
        qpos = jnp.arange(q0, q1)[:, None]
        kpos = jnp.arange(q1)[None, :]
        valid = (kpos < qpos) & (kpos >= pad)
        log_keep = jnp.where(valid, -jax.nn.softplus(z), 0.0)
        later = lax.cumsum(log_keep, axis=3, reverse=True) - log_keep
        log_w = jax.nn.log_sigmoid(z) + later
        w = jnp.where(valid, jnp.exp(log_w), 0.0)
        outs.append(jnp.einsum('bhqk,bhkd->bhqd', w.astype(vb.dtype), vb))
    out = jnp.concatenate(outs, axis=2)
    return out[:, :, pad:pad + t]

def short_conv_mixer(xin, gate_b, gate_c, conv_w, conv_b):
    u = gate_c * xin
    y = lax.conv_general_dilated(
        u, conv_w[:, None, :].astype(u.dtype), window_strides=(1,),
        padding=[(CONV_K - 1, 0)], dimension_numbers=('NWC', 'WIO', 'NWC'),
        feature_group_count=u.shape[-1])
    return gate_b * (y + conv_b)

def clamped_swiglu(gu):
    gate, lin = jnp.split(gu, 2, axis=-1)
    gate = jnp.minimum(gate, SWIGLU_LIMIT)
    lin = jnp.clip(lin, -SWIGLU_LIMIT, SWIGLU_LIMIT)
    return (lin + 1.0) * (gate * jax.nn.sigmoid(SWIGLU_ALPHA * gate))

def moe(x, w_router, b_router, w_gu, b_gu, w_down, b_down):
    d = x.shape[-1]
    xf = x.reshape(-1, d)
    n = xf.shape[0]
    logits = (xf @ w_router).astype(jnp.float32) + b_router.astype(jnp.float32)
    top_logit, top_e = lax.top_k(logits, TOP_K)
    gates = jax.nn.softmax(top_logit, axis=-1)
    a = n * TOP_K
    e_flat = top_e.reshape(-1)
    order = jnp.argsort(e_flat)
    e_sorted = e_flat[order]
    counts = jnp.zeros((N_EXPERTS,), jnp.int32).at[e_flat].add(1)
    padded = (counts + MOE_BLOCK - 1) // MOE_BLOCK * MOE_BLOCK
    start = jnp.cumsum(counts) - counts
    pend = jnp.cumsum(padded)
    pstart = pend - padded
    dest = pstart[e_sorted] + (jnp.arange(a, dtype=jnp.int32) - start[e_sorted])
    n_blocks = -(-a // MOE_BLOCK) + N_EXPERTS
    cap = n_blocks * MOE_BLOCK
    slot_src = jnp.full((cap,), a, jnp.int32).at[dest].set(order.astype(jnp.int32))
    slot_tok = slot_src // TOP_K
    slot_gate = jnp.concatenate([gates.reshape(-1), jnp.zeros((1,), jnp.float32)])[slot_src]
    x_pad = jnp.concatenate([xf, jnp.zeros((1, d), xf.dtype)], axis=0)
    xs = x_pad[slot_tok].reshape(n_blocks, MOE_BLOCK, d)
    block_start = jnp.arange(n_blocks, dtype=jnp.int32) * MOE_BLOCK
    block_expert = jnp.clip(jnp.searchsorted(pend, block_start, side='right'), 0, N_EXPERTS - 1)

    def expert_block(args):
        xb, e = args
        hid = clamped_swiglu(xb @ w_gu[e] + b_gu[e])
        return hid @ w_down[e] + b_down[e]

    ys = lax.map(expert_block, (xs, block_expert)).reshape(cap, d)
    ys = ys * slot_gate[:, None].astype(ys.dtype)
    y = jax.ops.segment_sum(ys, slot_tok, num_segments=n + 1)[:n]
    return y.reshape(x.shape)

def setup_inputs(seed: int = 0) -> dict:
    key = jax.random.key(seed)
    ks = jax.random.split(key, 20)
    f32 = jnp.float32
    nrm = lambda k, s, sc: jax.random.normal(k, s, f32) * sc
    return {
        "x": nrm(ks[0], (BATCH, SEQ, D_MODEL), 1.0),
        "meta_tokens": nrm(ks[1], (N_META, D_MODEL), 1.0),
        "g_mix": 1.0 + nrm(ks[2], (DEPTH, D_MODEL), 0.02),
        "w_in": nrm(ks[3], (DEPTH, D_MODEL, PROJ_WIDTH), D_MODEL ** -0.5),
        "g_attn_out": 1.0 + nrm(ks[4], (DEPTH, ATTN_WIDTH), 0.02),
        "conv_w": nrm(ks[5], (DEPTH, CONV_K, CONV_WIDTH), CONV_K ** -0.5),
        "conv_b": nrm(ks[6], (DEPTH, CONV_WIDTH), 0.02),
        "g_conv_out": 1.0 + nrm(ks[7], (DEPTH, CONV_WIDTH), 0.02),
        "w_out": nrm(ks[8], (DEPTH, MIX_WIDTH, D_MODEL), MIX_WIDTH ** -0.5),
        "g_ffn": 1.0 + nrm(ks[9], (DEPTH, D_MODEL), 0.02),
        "w_router": nrm(ks[10], (DEPTH, D_MODEL, N_EXPERTS), D_MODEL ** -0.5),
        "b_router": nrm(ks[11], (DEPTH, N_EXPERTS), 0.01),
        "w_gu": nrm(ks[12], (DEPTH, N_EXPERTS, D_MODEL, 2 * D_FF), D_MODEL ** -0.5),
        "b_gu": nrm(ks[13], (DEPTH, N_EXPERTS, 2 * D_FF), 0.01),
        "w_down": nrm(ks[14], (DEPTH, N_EXPERTS, D_FF, D_MODEL), D_FF ** -0.5),
        "b_down": nrm(ks[15], (DEPTH, N_EXPERTS, D_MODEL), 0.01),
        "g_final": 1.0 + nrm(ks[16], (D_MODEL,), 0.02),
    }

def reference(x, meta_tokens, g_mix, w_in, g_attn_out, conv_w, conv_b, g_conv_out,
              w_out, g_ffn, w_router, b_router, w_gu, b_gu, w_down, b_down, g_final):
    b = x.shape[0]
    meta = jnp.broadcast_to(meta_tokens[None].astype(x.dtype), (b, N_META, x.shape[-1]))
    h = jnp.concatenate([meta, x], axis=1)
    t = h.shape[1]
    A, C = ATTN_WIDTH, CONV_WIDTH
    cuts = [A, 2 * A, 3 * A, 3 * A + C, 3 * A + 2 * C]
    for l in range(DEPTH):
        n = rms_norm(h, g_mix[l])
        proj = n @ w_in[l]
        q, k, v, cb, cc, cx = jnp.split(proj, cuts, axis=-1)
        to_heads = lambda a: a.reshape(b, t, N_ATTN_HEADS, HEAD_DIM).transpose(0, 2, 1, 3)
        att = stick_breaking_attention(to_heads(q), to_heads(k), to_heads(v))
        att = att.transpose(0, 2, 1, 3).reshape(b, t, A)
        conv = short_conv_mixer(cx, cb, cc, conv_w[l], conv_b[l])
        mixed = jnp.concatenate([rms_norm(att, g_attn_out[l]),
                                 rms_norm(conv, g_conv_out[l])], axis=-1)
        h = h + mixed @ w_out[l]
        h = h + moe(rms_norm(h, g_ffn[l]), w_router[l], b_router[l],
                    w_gu[l], b_gu[l], w_down[l], b_down[l])
    return rms_norm(h, g_final)[:, N_META:]


_drawn_inputs = setup_inputs


def setup_inputs(seed=0):
    import zlib

    import numpy as np

    out = dict(_drawn_inputs(seed))
    spreads = {}
    factors = {'b_gu': 8.0, 'b_down': 8.0, 'g_final': 2.861}
    for name, (base, spread) in spreads.items():
        noise = np.random.default_rng([zlib.crc32(name.encode()), seed]).standard_normal(out[name].shape)
        drawn = base * np.exp(spread * noise) if base else spread * noise
        out[name] = __import__('jax').numpy.asarray(drawn.astype(out[name].dtype))
    for name, factor in factors.items():
        out[name] = (out[name] * factor).astype(out[name].dtype)
    return out
```

```python
from contextlib import ExitStack

import concourse.bass as bass
from concourse import mybir

F32 = mybir.dt.float32
BF16 = mybir.dt.bfloat16
I32 = mybir.dt.int32
U32 = mybir.dt.uint32
ALU = mybir.AluOpType
ACT = mybir.ActivationFunctionType
AX = mybir.AxisListType

P = 128
D = 1024
KD = D // P
T = 512
NT = T // P
META = 16
TM = META + T
AW = 512
HEADS, HD = 8, 64
CW = 512
NC_ = AW // P
TAPS = 3
UT = T + TAPS - 1
E, TOPK = 32, 4
FF = 1024
NF = FF // P
EPS = 1e-6
LIMIT, ALPHA = 7.0, 1.702

SLOTS = 96
BLOCKS = -(-T // SLOTS)
EXTRA = T * TOPK // SLOTS
ITEMS = E + EXTRA + 3
KEYS = 24
assert EXTRA + 3 <= KEYS
SKIP = float(1 << 20)


def build(nc, x, meta_tokens, g_mix, w_in, g_attn_out, conv_w, conv_b, g_conv_out, w_out, g_ffn,
          w_router, b_router, w_gu, b_gu, w_down, b_down, g_final, out):
    with ExitStack() as ctx:
        def sb(name, shape, dt=F32):
            return ctx.enter_context(nc.sbuf_tensor(name, shape, dt))

        def sem(name):
            return ctx.enter_context(nc.semaphore(name))

        ffn_rows = nc.dram_tensor("ffn_rows", [T, D], F32, kind="Internal").ap()
        choice_rows = nc.dram_tensor("choice_rows", [T * TOPK, D], F32, kind="Internal").ap()

        GU_HALF = KD * 2 * (FF // 2)
        ring = sb("ring", [P, 4 * GU_HALF])
        down = sb("down", [P, NF * D])
        MISC = KD * T + NC_ * UT
        misc = sb("misc", [P, MISC])
        res = sb("res", [P, NT, D])

        def view(t, start, *shape, rows=P, dt=None):
            n = 1
            for s in shape:
                n *= s
            v = t[0:rows, start:start + n]
            if len(shape) == 2:
                v = v.rearrange("p (a b) -> p a b", b=shape[1])
            elif len(shape) == 3:
                v = v.rearrange("p (a b c) -> p a b c", b=shape[1], c=shape[2])
            return v

        gu = [[view(ring, (2 * j + h) * GU_HALF, KD, 2, FF // 2) for h in range(2)] for j in range(2)]
        dn = down[:, :].rearrange("p (f d) -> p f d", f=NF)

        GROUP = KD * 512
        win = [view(ring, g * GROUP, KD, 512) for g in range(5)]
        win.append(win[0])
        at = 5 * GROUP
        qT = view(ring, at, NC_, T); at += NC_ * T
        kT = view(ring, at, NC_, TM); at += NC_ * TM
        vN = view(ring, at, NT + 1, AW); at += (NT + 1) * AW
        NA, NSP, NW = 2, 3, 3
        za = [view(ring, at + i * T, T) for i in range(NA)]; at += NA * T
        sp = [view(ring, at + i * T, T) for i in range(NSP)]; at += NSP * T
        wT = [view(ring, at + i * T, T) for i in range(NW)]; at += NW * T
        later = [view(ring, at + i * T, T) for i in range(2)]; at += 2 * T
        neg_tri = view(ring, at, P); at += P
        neg_one = view(ring, at, P); at += P
        causal = view(ring, at, P); at += P
        assert at <= 4 * GU_HALF
        bgu_rows = view(ring, 5 * GROUP + (NC_ * (T + TM)) + (NT + 1) * AW, 2 * FF, rows=E)
        assert NA + NSP + NW + 2 >= 4
        sq = [za[0], za[1], sp[0], sp[1]]
        rstd = [wT[0], wT[1]]
        at = 3 * GU_HALF
        g_ffn_b = view(ring, at, D); at += D
        b_down_sb = view(ring, at, D, rows=E); at += D
        w_router_sb = view(ring, at, KD, E); at += KD * E
        b_router_b = view(ring, at, E); at += E
        rows2 = [view(ring, at + i * D, D) for i in range(2)]; at += 2 * D
        rowsT = [view(ring, at + i * D, KD, P) for i in range(2)]; at += 2 * D
        LATE = at
        hT = view(down, 0, KD, TM)
        xn = [view(down, KD * TM + i * D, D) for i in range(2)]
        meta_rows = view(down, KD * TM + 2 * D, D, rows=META)
        slot_int = misc[:, 0:SLOTS].bitcast(I32)
        cxT = view(down, KD * TM + 3 * D, UT)
        vec_rows = view(down, KD * TM + 3 * D + UT, P, rows=32)
        wo = view(down, 0, KD, D)
        mixT = view(misc, 0, KD, T)
        uT = view(misc, KD * T, NC_, UT)
        at = 0
        xs = view(misc, at, D, rows=SLOTS); at += D
        xsT = view(misc, at, KD, SLOTS); at += KD * SLOTS
        hid = view(misc, at, NF, SLOTS); at += NF * SLOTS
        yT = view(misc, at, KD, SLOTS); at += KD * SLOTS
        ys = view(misc, at, D, rows=SLOTS); at += D
        HC = NF // 2
        gate_t = view(misc, at, HC, SLOTS); at += HC * SLOTS
        lin_t = view(misc, at, HC, SLOTS); at += HC * SLOTS
        sig_t = view(misc, at, HC, SLOTS); at += HC * SLOTS
        assert at <= MISC
        picked = [view(ring, i * TOPK * D, TOPK, D) for i in range(NT)]
        g_final_b = view(ring, NT * TOPK * D, D)
        final_junk = view(ring, (NT * TOPK + 1) * D, D)
        final_rows = [view(ring, (NT * TOPK + 2 + i) * D, D) for i in range(NT)]

        ident = sb("ident", [P, P])
        ones = sb("ones", [P, P])
        eps_t = sb("eps_t", [P, 1])
        before = sb("before", [P, P], BF16)
        ones_h = sb("ones_h", [P, P], BF16)
        vecT = sb("vecT", [P, 32])
        G_MIX, G_ATT, G_CONV, CONV_W, CONV_B = 0, 8, 12, 16, 28
        bguT = sb("bguT", [P, 2 * NF, E])
        ss = sb("ss", [P, 8])
        rs = sb("rs", [P, 8])
        logits = sb("logits", [P, NT, E])
        top = sb("top", [P, NT, 8])
        top_e = sb("top_e", [P, NT, 8], U32)
        gates = sb("gates", [P, NT, TOPK])
        place = sb("place", [P, NT, E])
        choice = sb("choice", [P, NT, E])
        shift = sb("shift", [P, ITEMS])
        item_e = sb("item_e", [1, ITEMS], I32)
        trips = sb("trips", [1, 2], I32)
        slot_no = sb("slot_no", [P, SLOTS])
        onehot = sb("onehot", [P, NT, SLOTS], BF16)
        place_i = sb("place_i", [P, NT])
        ids = sb("ids", [P, NT, 4], BF16)
        slot_f = sb("slot_f", [SLOTS, 4])
        slot_g = sb("slot_g", [SLOTS, 4])
        tok_idx = sb("tok_idx", [SLOTS, 1], U32)
        row_idx_next = sb("row_idx_next", [SLOTS, 2], U32)
        row_idx = sb("row_idx", [SLOTS, 2], U32)
        b_item = sb("b_item", [P, 2, 2 * NF])

        banks = [ctx.enter_context(nc.psum_tensor(f"bank{i}", [P, 512], F32)) for i in range(8)]

        x_in = [sem(f"x_in{i}") for i in range(NT + 1)]
        vec_in, bgu_in, late_in, wo_in = sem("vec_in"), sem("bgu_in"), sem("late_in"), sem("wo_in")
        win_in = [sem(f"win_in{g}") for g in range(6)]
        gu_in = [[sem(f"gu_in{j}{h}") for h in range(2)] for j in range(2)]
        dn_in = [sem(f"dn_in{h}") for h in range(2)]
        ident_ready, ones_ready, masks_ready, slots_ready, eps_ready = (
            sem("ident_ready"), sem("ones_ready"), sem("masks_ready"), sem("slots_ready"), sem("eps_ready"))
        const_step, glu_part, glu_read, row_moved, final_step = sem("const_step"), sem("glu_part"), sem("glu_read"), sem("row_moved"), sem("final_step")
        squares, sq_dve, rms_act = sem("squares"), sem("sq_dve"), sem("rms_act")
        xn_ready, xn_turned = sem("xn_ready"), sem("xn_turned")
        hT_act, hT_dve = sem("hT_act"), sem("hT_dve")
        vec_turned, vec_ready, bgu_turned, bgu_ready = sem("vec_turned"), sem("vec_ready"), sem("bgu_turned"), sem("bgu_ready")
        proj_done, proj_act, proj_dve = sem("proj_done"), sem("proj_act"), sem("proj_dve")
        conv_step = sem("conv_step")
        z_done, abs_done, exp_done, ln_done, sp_done, masked = (sem("z_done"), sem("abs_done"), sem("exp_done"), sem("ln_done"), sem("sp_done"), sem("masked"))
        later_done, logw_done, w_done, w_masked, av_done, att_copied = (sem("later_done"), sem("logw_done"), sem("w_done"), sem("w_masked"), sem("av_done"), sem("att_copied"))
        nsq, nsum, nroot, nscaled = sem("nsq"), sem("nsum"), sem("nroot"), sem("nscaled")
        outp, res_added, row_sq, row_var, row_root, row_ready, row_turned, rowT_ready = (
            sem("outp"), sem("res_added"), sem("row_sq"), sem("row_var"), sem("row_root"), sem("row_ready"), sem("row_turned"), sem("rowT_ready"))
        row_stored = [sem(f"row_stored{i}") for i in range(NT)]
        logit_done, route, gate_exp, mask_ready, pos_done, dense_turned, dense_ready, bias_done, base_ready = (
            sem("logit_done"), sem("route"), sem("gate_exp"), sem("mask_ready"), sem("pos_done"), sem("dense_turned"), sem("dense_ready"), sem("bias_done"), sem("base_ready"))
        table_ready, bufs_clear = sem("table_ready"), sem("bufs_clear")
        onehot_ready, idx_summed, idx_copied, idx_step, idx_ready, prep_step = (
            sem("onehot_ready"), sem("idx_summed"), sem("idx_copied"), sem("idx_step"), sem("idx_ready"), sem("prep_step"))
        xs_in, xs_turned, xsT_ready = sem("xs_in"), sem("xs_turned"), sem("xsT_ready")
        gu_done, gate_ready, sig_done, hid_ready, dn_done = (
            sem("gu_done"), sem("gate_ready"), sem("sig_done"), sem("hid_ready"), sem("dn_done"))
        yT_ready, y_turned, ys_ready, y_out = sem("yT_ready"), sem("y_turned"), sem("ys_ready"), sem("y_out")
        picked_in = [sem(f"picked_in{i}") for i in range(NT)]
        final_in, final_sum, final_sq, final_rt, final_ready, stored = (
            sem("final_in"), sem("final_sum"), sem("final_sq"), sem("final_rt"), sem("final_ready"), sem("stored"))

        HALF_K, HALF_U = TM // 2, UT // 2
        jobs = [("k", c, h) for c in range(NC_) for h in range(2)]
        jobs += [("q", c, 0) for c in range(NC_)]
        jobs += [("v", m, 0) for m in range(NT + 1)]
        jobs += [(kind, c, h) for c in range(NC_) for kind in ("cx", "cc") for h in range(2)]
        jobs += [("cb", c, 0) for c in range(NC_)]
        GROUP_OF = {"q": 0, "k": 1, "v": 2, "cb": 3, "cc": 4, "cx": 5}
        LOADS = ["k", "q", "v", "cx", "cc", "cb"]
        SLOT_OF = {kind: n for n, kind in enumerate(LOADS)}
        PROJ_BANKS = 4

        def evac_by_act(n):
            return jobs[n][0] in ("k", "q", "v", "cx") and n % 2 == 0

        def evac_wait(eng, n):
            by = [evac_by_act(m) for m in range(n + 1)]
            if by[n]:
                eng.wait_ge(proj_act, sum(by))
            else:
                eng.wait_ge(proj_dve, n + 1 - sum(by))

        def jobs_until(kind):
            return max(n for n, j in enumerate(jobs) if j[0] == kind) + 1

        att_items = [(2 * c + hh, b) for c in range(HEADS // 2) for b in (3, 2, 1, 0, -1) for hh in range(2)]
        NI = len(att_items)
        LB = 6

        def span(b):
            return (P * b, P) if b >= 0 else (0, META)

        masks_before = [sum(1 for h, b in att_items[:i] if b >= 0) for i in range(NI + 1)]

        block = ctx.enter_context(nc.Block())

        @block.sync
        def _(sp_):
            def load_gu(e, j, h):
                for s in range(2):
                    src = w_gu[0, e, :, s * FF + h * (FF // 2):s * FF + (h + 1) * (FF // 2)] if isinstance(e, int) else \
                        w_gu[0, bass.ds(e, 1), :, s * FF + h * (FF // 2):s * FF + (h + 1) * (FF // 2)].rearrange("o r f -> (o r) f")
                    sp_.dma_start(gu[j][h][:, :, s, :], src.rearrange("(k p) f -> p k f", p=P)).then_inc(gu_in[j][h], 16)

            def load_dn(e, h):
                src = w_down[0, e, h * (FF // 2):(h + 1) * (FF // 2), :] if isinstance(e, int) else \
                    w_down[0, bass.ds(e, 1), h * (FF // 2):(h + 1) * (FF // 2), :].rearrange("o r d -> (o r) d")
                sp_.dma_start(dn[:, h * HC:(h + 1) * HC, :], src.rearrange("(f p) d -> p f d", p=P)).then_inc(dn_in[h], 16)

            sp_.dma_start(meta_rows, meta_tokens[:, :]).then_inc(x_in[NT], 16)
            for i in range(NT):
                sp_.dma_start(res[:, i, :], x[0, i * P:(i + 1) * P, :]).then_inc(x_in[i], 16)
            for src, at_, n in ((g_mix[0], G_MIX, 8), (g_attn_out[0], G_ATT, 4), (g_conv_out[0], G_CONV, 4), (conv_b[0], CONV_B, 4)):
                sp_.dma_start(vec_rows[at_:at_ + n, :], src.rearrange("(a b) -> a b", b=P)).then_inc(vec_in, 16)
            sp_.dma_start(vec_rows[CONV_W:CONV_W + 12, :], conv_w[0].rearrange("t (a b) -> (t a) b", b=P)).then_inc(vec_in, 16)
            sp_.dma_start(bgu_rows, b_gu[0]).then_inc(bgu_in, 16)
            for n, kind in enumerate(LOADS):
                g = GROUP_OF[kind]
                if n == 5:
                    sp_.wait_ge(proj_done, jobs_until("k"))
                sp_.dma_start(win[n], w_in[0, :, g * 512:(g + 1) * 512].rearrange("(k p) f -> p k f", p=P)).then_inc(win_in[n], 16)
            sp_.wait_ge(proj_done, len(jobs))
            sp_.dma_start(wo, w_out[0].rearrange("(k p) f -> p k f", p=P)).then_inc(wo_in, 16)
            load_gu(0, 0, 0)
            load_gu(0, 0, 1)
            sp_.wait_ge(nscaled, 2 * NC_)
            sp_.dma_start(g_ffn_b, g_ffn[0:1, :].to_broadcast([P, D])).then_inc(late_in, 16)
            sp_.dma_start(b_router_b, b_router[0:1, :].to_broadcast([P, E])).then_inc(late_in, 16)
            sp_.dma_start(w_router_sb, w_router[0].rearrange("(k p) e -> p k e", p=P)).then_inc(late_in, 16)
            sp_.dma_start(b_down_sb, b_down[0]).then_inc(late_in, 16)
            load_gu(1, 1, 0)
            for i in range(NT):
                sp_.wait_ge(row_ready, i + 1)
                sp_.dma_start(ffn_rows[i * P:(i + 1) * P, :], rows2[i % 2]).then_inc(row_stored[i], 16)
            sp_.wait_ge(outp, 2 * NT)
            load_dn(0, 0)
            load_dn(0, 1)
            sp_.wait_ge(base_ready, NT * 2)
            sp_.wait_ge(table_ready, 2)
            for i in range(NT):
                sp_.wait_ge(row_stored[i], 16)
            load_gu(1, 1, 1)
            full = sp_.value_load(trips[0:1, 1:2], min_val=E // 2 - 1, max_val=(E + EXTRA + 1) // 2 - 1)
            with sp_.Fori(0, full) as it:
                for j in range(2):
                    i = it * 2 + j
                    e1 = sp_.value_load(item_e[0:1, bass.ds(it * 2 + (j + 1), 1)], min_val=0, max_val=E - 1)
                    e2 = sp_.value_load(item_e[0:1, bass.ds(it * 2 + (j + 2), 1)], min_val=0, max_val=E - 1)
                    for h in range(2):
                        sp_.wait_ge(gu_done, i * 2 + (h + 1))
                        load_gu(e2, j, h)
                    for h in range(2):
                        sp_.wait_ge(dn_done, i * 2 + (h + 1))
                        load_dn(e1, h)
            e1 = sp_.value_load(item_e[0:1, bass.ds(full * 2 + 1, 1)], min_val=0, max_val=E - 1)
            for h in range(2):
                sp_.wait_ge(dn_done, full * 4 + (h + 1))
                load_dn(e1, h)
            sp_.wait_ge(gu_done, full * 4 + 4)
            sp_.dma_start(g_final_b, g_final.rearrange("(a d) -> a d", a=1).to_broadcast([P, D])).then_inc(final_in, 16)
            sp_.wait_ge(y_out, full * 32 + 64)
            for i in range(NT):
                sp_.dma_start(picked[i], choice_rows[i * P * TOPK:(i + 1) * P * TOPK, :].rearrange("(p k) d -> p k d", k=TOPK)).then_inc(picked_in[i], 16)
            for i in range(NT):
                sp_.wait_ge(final_ready, i + 1)
                sp_.dma_start(out[0, i * P:(i + 1) * P, :], final_rows[i]).then_inc(stored, 16)
            sp_.wait_ge(stored, 16 * NT)

        @block.tensor
        def _(pe):
            pe.wait_ge(ident_ready, 1)
            pe.wait_ge(vec_in, 5 * 16)
            pe.transpose(banks[4][:, 0:32], vec_rows[:, :], ident[0:32, 0:32]).then_inc(vec_turned, 1)
            pe.wait_ge(bgu_in, 16)
            for f in range(2 * NF):
                mm = pe.transpose(banks[5][:, f * E:(f + 1) * E], bgu_rows[:, f * P:(f + 1) * P], ident[0:E, 0:E])
            mm.then_inc(bgu_turned, 1)
            for n in range(NT + 1):
                rows = META if n == 0 else P
                pe.wait_ge(xn_ready, n + 1)
                if n >= 2:
                    pe.wait_ge(hT_act, n - 1)
                    pe.wait_ge(hT_dve, n - 1)
                src = xn[n % 2]
                for c in range(KD):
                    b = banks[2 * (n % 2) + c // 4]
                    mm = pe.transpose(b[:, (c % 4) * P:(c % 4) * P + rows], src[0:rows, c * P:(c + 1) * P], ident[0:rows, 0:rows])
                mm.then_inc(xn_turned, 1)
            pe.wait_ge(hT_act, NT + 1)
            pe.wait_ge(hT_dve, NT + 1)
            for n, (kind, c, h) in enumerate(jobs):
                if n >= PROJ_BANKS:
                    evac_wait(pe, n - PROJ_BANKS)
                pe.wait_ge(win_in[SLOT_OF[kind]], 16)
                b = banks[n % PROJ_BANKS]
                w = win[SLOT_OF[kind]]
                for k in range(KD):
                    if kind == "v":
                        lo, rows = (0, META) if c == 0 else (META + (c - 1) * P, P)
                        o, lhs, rhs = b[0:rows, :], hT[:, k, lo:lo + rows], w[:, k, :]
                    else:
                        lo, cols = {"k": (h * HALF_K, HALF_K), "cx": (TM - UT + h * HALF_U, HALF_U),
                                    "cc": (TM - UT + h * HALF_U, HALF_U)}.get(kind, (META, T))
                        o, lhs, rhs = b[:, 0:cols], w[:, k, c * P:(c + 1) * P], hT[:, k, lo:lo + cols]
                    mm = pe.matmul(o, lhs, rhs, start=(k == 0), stop=(k == KD - 1))
                mm.then_inc(proj_done, 1)
            def width_norm(part):
                for c in range(NC_):
                    pe.wait_ge(nsq, part * NC_ + c + 1)
                    mm = pe.matmul(banks[4 + part][:, :], ones[:, :], sq[c], start=(c == 0), stop=(c == NC_ - 1))
                mm.then_inc(nsum, 1)

            for n in range(len(jobs) - PROJ_BANKS, len(jobs)):
                evac_wait(pe, n)
            pe.wait_ge(ones_ready, 1)
            width_norm(0)
            pe.wait_ge(nscaled, NC_)
            pe.wait_ge(masks_ready, 3)
            for s in range(NI + 4):
                if s < NI:
                    h, b = att_items[s]
                    t0, keys = span(b)
                    k0 = META + t0 if b >= 0 else 0
                    r = HD * (h % 2)
                    if s >= LB:
                        pe.wait_ge(w_done, s - LB + 1)
                    pe.matmul(banks[s % LB][0:keys, 0:T - t0], kT[r:r + HD, h // 2, k0:k0 + keys],
                              qT[r:r + HD, h // 2, t0:T], start=True, stop=True).then_inc(z_done, 1)
                if 2 <= s < NI + 2:
                    i = s - 2
                    h, b = att_items[i]
                    t0, keys = span(b)
                    L = banks[i % LB]
                    if b >= 0:
                        pe.wait_ge(masked, masks_before[i + 1])
                    else:
                        pe.wait_ge(sp_done, i + 1)
                    mm = pe.matmul(L[0:keys, 0:T - t0], neg_tri[0:keys, 0:keys], sp[i % NSP][0:keys, 0:T - t0],
                                   start=False, stop=True, skip_group_check=True)
                    if b != 3:
                        t1 = P * (b + 1)
                        pe.wait_ge(later_done, masks_before[i - 1])
                        mm = pe.matmul(L[0:keys, t1 - t0:T - t0], neg_one[:, 0:keys], later[h % 2][:, t1:T],
                                       start=False, stop=True, skip_group_check=True)
                    mm.then_inc(logw_done, 1)
                if 4 <= s < NI + 4:
                    i = s - 4
                    h, b = att_items[i]
                    t0, keys = span(b)
                    r = HD * (h % 2)
                    if b >= 0:
                        pe.wait_ge(w_masked, masks_before[i + 1])
                    else:
                        pe.wait_ge(w_done, i + 1)
                    if b == 3 and h % 2 == 0 and h >= 4:
                        pe.wait_ge(att_copied, h // 2 - 1)
                    pe.matmul(banks[LB + (h // 2) % 2][r:r + HD, t0:T], vN[0:keys, b + 1, HD * h:HD * (h + 1)],
                              wT[i % NW][0:keys, 0:T - t0], start=(b == 3), stop=True,
                              skip_group_check=True).then_inc(av_done, 1)
            width_norm(1)
            pe.wait_ge(wo_in, 16)
            pe.wait_ge(nscaled, 2 * NC_)
            def route_tile(i):
                pe.wait_ge(row_ready, i + 1)
                if i >= 1:
                    pe.wait_ge(rowT_ready, 2 * i)
                for c in range(KD):
                    mm = pe.transpose(banks[4 + c // 4][:, (c % 4) * P:(c % 4 + 1) * P], rows2[i % 2][:, c * P:(c + 1) * P], ident[:, :])
                mm.then_inc(row_turned, 1)
                pe.wait_ge(rowT_ready, 2 * (i + 1))
                if i == 0:
                    pe.wait_ge(late_in, 64)
                if i >= 1:
                    pe.wait_ge(route, i)
                for k in range(KD):
                    mm = pe.matmul(banks[6][:, 0:E], rowsT[i % 2][:, k, :], w_router_sb[:, k, :], start=(k == 0), stop=(k == KD - 1))
                mm.then_inc(logit_done, 1)

            for i in range(NT):
                for n in range(2):
                    m = 2 * i + n
                    if m >= 4:
                        pe.wait_ge(res_added, m - 3)
                    for k in range(KD):
                        mm = pe.matmul(banks[m % 4][:, :], mixT[:, k, i * P:(i + 1) * P], wo[:, k, n * 512:(n + 1) * 512],
                                       start=(k == 0), stop=(k == KD - 1))
                    mm.then_inc(outp, 1)
                if i >= 1:
                    route_tile(i - 1)
            route_tile(NT - 1)
            pe.wait_ge(mask_ready, 1)
            pe.wait_ge(slots_ready, 1)
            for i in range(NT):
                for m in range(i + 1):
                    pe.matmul(banks[7][:, i * E:(i + 1) * E], (before if m == i else ones_h)[:, :], onehot[:, m, 0:E],
                              start=(m == 0), stop=(m == i))
            for m in range(NT):
                mm = pe.matmul(banks[7][:, NT * E:(NT + 1) * E], ones_h[:, :], onehot[:, m, 0:E], start=(m == 0), stop=(m == NT - 1))
            mm.then_inc(pos_done, 1)
            pe.wait_ge(mask_ready, 2)
            for i in range(NT):
                mm = pe.transpose(banks[6][0:E, i * P:(i + 1) * P], rowsT[0][:, i, 0:E], ident[:, :])
            mm.then_inc(dense_turned, 1)
            pe.wait_ge(dense_ready, 1)
            for m in range(2 * NT):
                if m >= 4:
                    pe.wait_ge(base_ready, m - 3)
                pe.matmul(banks[m % 4][:, :], rowsT[1][0:E, m // 2, :], b_down_sb[:, (m % 2) * 512:(m % 2 + 1) * 512],
                          start=True, stop=True).then_inc(bias_done, 1)
            pe.wait_ge(base_ready, 2 * NT)

            def sum_ids(i):
                pe.wait_ge(onehot_ready, i + 1)
                for m in range(NT):
                    mm = pe.matmul(banks[4][0:SLOTS, 504:508], onehot[:, m, :], ids[:, m, :], start=(m == 0), stop=(m == NT - 1))
                mm.then_inc(idx_summed, 1)

            def turn_rows(i):
                pe.wait_ge(xs_in, i * 16 + 16)
                pe.wait_ge(ys_ready, i)
                for c in range(KD):
                    mm = pe.transpose(banks[6 + c // 4][:, (c % 4) * SLOTS:(c % 4 + 1) * SLOTS], xs[:, c * P:(c + 1) * P], ident[0:SLOTS, 0:SLOTS])
                mm.then_inc(xs_turned, 1)

            def turn_outputs(n):
                pe.wait_ge(yT_ready, n + 1)
                pe.wait_ge(xsT_ready, n + 1)
                for c in range(KD):
                    mm = pe.transpose(banks[6 + c // 4][0:SLOTS, (c % 4) * P:(c % 4 + 1) * P], yT[:, c, :], ident[:, :])
                mm.then_inc(y_turned, 1)

            def gate_and_up(i, it, j, h):
                pe.wait_ge(gu_in[j][h], it * 32 + 32)
                if h == 0:
                    pe.wait_ge(xsT_ready, i + 1)
                pe.wait_ge(glu_read, i * 2 + (h + 1))
                for s in range(2):
                    for f in range(HC):
                        for k in range(KD):
                            mm = pe.matmul(banks[2 * h + s][:, f * SLOTS:(f + 1) * SLOTS], gu[j][h][:, k, s, f * P:(f + 1) * P],
                                           xsT[:, k, :], start=(k == 0), stop=(k == KD - 1))
                mm.then_inc(gu_done, 1)

            sum_ids(0)
            pe.wait_ge(xs_in, 16)
            for c in range(KD):
                mm = pe.transpose(banks[6 + c // 4][:, (c % 4) * SLOTS:(c % 4 + 1) * SLOTS], xs[:, c * P:(c + 1) * P], ident[0:SLOTS, 0:SLOTS])
            mm.then_inc(xs_turned, 1)
            n_trips = pe.value_load(trips[0:1, 0:1], min_val=E // 2, max_val=(E + EXTRA + 1) // 2)
            with pe.Fori(0, n_trips) as it:
                for j in range(2):
                    i = it * 2 + j
                    gate_and_up(i, it, j, 0)
                    turn_outputs(i)
                    sum_ids(i + 1)
                    gate_and_up(i, it, j, 1)
                    turn_rows(i + 1)
                    pe.wait_ge(idx_copied, i + 2)
                    for h in range(2):
                        pe.wait_ge(dn_in[h], i * 16 + 16)
                        pe.wait_ge(hid_ready, i * 2 + (h + 2))
                        for f in range(h * HC, (h + 1) * HC):
                            for c in range(KD):
                                mm = pe.matmul(banks[4 + c // 4][:, (c % 4) * SLOTS:(c % 4 + 1) * SLOTS], dn[:, f, c * P:(c + 1) * P],
                                               hid[:, f, :], start=(f == 0 and c % 4 == 0), stop=(f == NF - 1), skip_group_check=True)
                        mm.then_inc(dn_done, 1)
            turn_outputs(n_trips * 2)

        @block.scalar
        def _(act):
            act.wait_ge(eps_ready, 1)
            for n in range(NT + 1):
                act.wait_ge(x_in[NT if n == 0 else n - 1], 16)
                src = meta_rows if n == 0 else res[:, n - 1, :]
                rows = META if n == 0 else P
                if n >= 2:
                    act.wait_ge(squares, n - 1)
                act.activation(xn[n % 2][0:rows, :], src, ACT.Square, accum_out=ss[0:rows, n:n + 1]).then_inc(squares, 1)
            act.wait_ge(squares, NT + 1)
            act.activation(rs[:, 0:5], ss[:, 0:5], ACT.Sqrt, scale=1.0 / D, bias=eps_t[:, :]).then_inc(rms_act, 1)
            act.wait_ge(vec_ready, 1)
            for n in range(NT + 1):
                lo, rows = (0, META) if n == 0 else (META + (n - 1) * P, P)
                act.wait_ge(xn_turned, n + 1)
                for c in range(4):
                    ins = act.activation(hT[:, c, lo:lo + rows], banks[2 * (n % 2)][:, c * P:c * P + rows], ACT.Copy,
                                         scale=vecT[:, G_MIX + c:G_MIX + c + 1])
                ins.then_inc(hT_act, 1)
            for n, (kind, c, h) in enumerate(jobs):
                if evac_by_act(n):
                    act.wait_ge(proj_done, n + 1)
                    b = banks[n % PROJ_BANKS]
                    if kind == "k":
                        ins = act.activation(kT[:, c, h * HALF_K:(h + 1) * HALF_K], b[:, 0:HALF_K], ACT.Copy)
                    elif kind == "q":
                        ins = act.activation(qT[:, c, :], b[:, :], ACT.Copy, scale=HD ** -0.5)
                    elif kind == "v":
                        rows = META if c == 0 else P
                        ins = act.activation(vN[0:rows, c, :], b[0:rows, :], ACT.Copy)
                    else:
                        if c >= 1:
                            evac_wait(act, jobs.index(("cc", c - 1, 1)))
                        ins = act.activation(cxT[:, h * HALF_U:(h + 1) * HALF_U], b[:, 0:HALF_U], ACT.Copy)
                    ins.then_inc(proj_act, 1)

            def width_norm(part):
                for c in range(NC_):
                    if part:
                        act.wait_ge(att_copied, c + 1)
                    else:
                        evac_wait(act, jobs.index(("cb", c, 0)))
                    src = mixT[:, c + (0 if part else NC_), :]
                    act.activation(sq[c], src, ACT.Square).then_inc(nsq, 1)
                act.wait_ge(nsum, part + 1)
                act.activation(rstd[0], banks[4 + part][:, :], ACT.Sqrt, scale=1.0 / AW, bias=eps_t[:, :]).then_inc(nroot, 1)

            act.wait_ge(bgu_turned, 1)
            width_norm(0)
            act.wait_ge(nscaled, NC_)
            act.preload_act_table_set("natural_log_exp_and_others")
            for s in range(NI + 3):
                if s < NI:
                    h, b = att_items[s]
                    t0, keys = span(b)
                    a = za[s % NA][0:keys, 0:T - t0]
                    act.wait_ge(abs_done, s + 1)
                    act.activation(a, a, ACT.Exp, scale=-1.0).then_inc(exp_done, 1)
                    act.wait_ge(exp_done, s + 1)
                    act.activation(a, a, ACT.Ln, bias=1.0).then_inc(ln_done, 1)
                if s >= 3:
                    i = s - 3
                    h, b = att_items[i]
                    t0, keys = span(b)
                    act.wait_ge(logw_done, i + 1)
                    if i >= NW:
                        act.wait_ge(av_done, i - NW + 1)
                    act.activation(wT[i % NW][0:keys, 0:T - t0], banks[i % LB][0:keys, 0:T - t0], ACT.Exp).then_inc(w_done, 1)
            act.wait_ge(av_done, NI)
            width_norm(1)
            for i in range(NT):
                act.wait_ge(res_added, 2 * (i + 1))
                if i >= 1:
                    act.wait_ge(row_ready, i)
                if i >= 2:
                    act.wait_ge(row_stored[i - 2], 16)
                    act.wait_ge(row_turned, i - 1)
                act.activation(rows2[i % 2], res[:, i, :], ACT.Square, accum_out=ss[:, i:i + 1]).then_inc(row_sq, 1)
                act.wait_ge(row_sq, i + 1)
                act.activation(rs[:, i:i + 1], ss[:, i:i + 1], ACT.Sqrt, scale=1.0 / D, bias=eps_t[:, :]).then_inc(row_root, 1)
                act.wait_ge(row_turned, i + 1)
                if i >= 2:
                    act.wait_ge(logit_done, i - 1)
                for c in range(2):
                    act.activation(rowsT[i % 2][:, 4 * c:4 * c + 4, :], banks[4 + c][:, :].rearrange("p (a b) -> p a b", b=P), ACT.Copy).then_inc(rowT_ready, 1)
            act.wait_ge(gate_exp, 1)
            act.activation(gates[:, :, :], gates[:, :, :], ACT.Exp).then_inc(gate_exp, 1)

            def sigmoid(i, h):
                act.wait_ge(gate_ready, i * 2 + (h + 1))
                act.activation(sig_t, gate_t, ACT.Sigmoid, scale=ALPHA).then_inc(sig_done, 1)

            def outputs_out(n):
                act.wait_ge(y_turned, n + 1)
                act.wait_ge(y_out, n * 16 + 16)
                for c in range(2):
                    ins = act.activation(ys[:, 512 * c:512 * (c + 1)], banks[6 + c][0:SLOTS, :], ACT.Copy)
                ins.then_inc(ys_ready, 1)

            act.wait_ge(xs_turned, 1)
            for c in range(2):
                ins = act.activation(xsT[:, 4 * c:4 * c + 4, :], banks[6 + c][:, 0:4 * SLOTS].rearrange("p (a b) -> p a b", b=SLOTS), ACT.Copy)
            ins.then_inc(xsT_ready, 1)
            act.wait_ge(table_ready, 2)
            n_trips = act.value_load(trips[0:1, 0:1], min_val=E // 2, max_val=(E + EXTRA + 1) // 2)
            with act.Fori(0, n_trips) as it:
                for j in range(2):
                    i = it * 2 + j
                    sigmoid(i, 0)
                    act.wait_ge(y_turned, i + 1)
                    act.wait_ge(y_out, i * 16 + 16)
                    for c in range(2):
                        ins = act.activation(ys[:, 512 * c:512 * (c + 1)], banks[6 + c][0:SLOTS, :], ACT.Copy)
                    ins.then_inc(ys_ready, 1)
                    sigmoid(i, 1)
                    act.wait_ge(xs_turned, i + 2)
                    act.wait_ge(gu_done, i * 2 + 2)
                    for c in range(2):
                        ins = act.activation(xsT[:, 4 * c:4 * c + 4, :], banks[6 + c][:, 0:4 * SLOTS].rearrange("p (a b) -> p a b", b=SLOTS), ACT.Copy)
                    ins.then_inc(xsT_ready, 1)
                    act.wait_ge(dn_done, i * 2 + 2)
                    for c in range(2):
                        ins = act.activation(yT[:, 4 * c:4 * c + 4, :], banks[4 + c][:, 0:4 * SLOTS].rearrange("p (a b) -> p a b", b=SLOTS), ACT.Copy)
                    ins.then_inc(yT_ready, 1)
            outputs_out(n_trips * 2)
            for i in range(NT):
                act.wait_ge(final_sum, TOPK * (i + 1))
                if i >= 1:
                    act.wait_ge(final_sq, i)
                act.activation(final_junk, res[:, i, :], ACT.Square, accum_out=ss[:, i:i + 1]).then_inc(final_sq, 1)
                act.wait_ge(final_sq, i + 1)
                act.activation(rs[:, i:i + 1], ss[:, i:i + 1], ACT.Sqrt, scale=1.0 / D, bias=eps_t[:, :]).then_inc(final_rt, 1)

        @block.vector
        def _(v):
            v.memset(eps_t[:, :], EPS)
            v.memset(ss[:, :], 1.0).then_inc(eps_ready, 1)
            v.wait_ge(rms_act, 1)
            v.reciprocal(rs[:, 0:5], rs[:, 0:5]).then_inc(sq_dve, 1)
            v.wait_ge(sq_dve, 1)

            def scale_rows(n):
                src = meta_rows if n == 0 else res[:, n - 1, :]
                rows = META if n == 0 else P
                if n >= 2:
                    v.wait_ge(xn_turned, n - 1)
                v.tensor_scalar(xn[n % 2][0:rows, :], src, rs[0:rows, n:n + 1], None, ALU.mult).then_inc(xn_ready, 1)

            def gain_rows(n):
                lo, rows = (0, META) if n == 0 else (META + (n - 1) * P, P)
                v.wait_ge(xn_turned, n + 1)
                for c in range(4, 8):
                    ins = v.tensor_scalar(hT[:, c, lo:lo + rows], banks[2 * (n % 2) + 1][:, (c - 4) * P:(c - 4) * P + rows],
                                          vecT[:, G_MIX + c:G_MIX + c + 1], None, ALU.mult)
                ins.then_inc(hT_dve, 1)

            scale_rows(0)
            v.wait_ge(vec_turned, 1)
            v.tensor_copy(vecT[:, :], banks[4][:, 0:32]).then_inc(vec_ready, 1)
            v.wait_ge(bgu_turned, 1)
            v.tensor_copy(bguT[:, :, :], banks[5][:, :].rearrange("p (a b) -> p a b", b=E)).then_inc(bgu_ready, 1)
            v.wait_ge(vec_ready, 1)
            for n in range(NT + 1):
                if n < NT:
                    scale_rows(n + 1)
                gain_rows(n)

            def vec(col):
                return vecT[:, col:col + 1]

            steps = [0]

            def conv(ins):
                steps[0] += 1
                ins.then_inc(conv_step, 1)

            for n, (kind, c, h) in enumerate(jobs):
                b = banks[n % PROJ_BANKS]
                if kind == "cb" and c == 0:
                    evac_wait(v, n - 1)
                    for m in range(NC_):
                        o = mixT[:, NC_ + m, :]
                        conv(v.tensor_scalar(o, uT[:, m, 0:T], vec(CONV_W + m), vec(CONV_B + m), ALU.mult, ALU.add))
                    for tap in (1, 2):
                        for m in range(NC_):
                            o = mixT[:, NC_ + m, :]
                            v.wait_ge(conv_step, (tap - 1) * NC_ + m + 1)
                            conv(v.scalar_tensor_tensor(out=o, in0=uT[:, m, tap:tap + T], scalar=vec(CONV_W + 4 * tap + m),
                                                        in1=o, op0=ALU.mult, op1=ALU.add))
                if evac_by_act(n):
                    continue
                v.wait_ge(proj_done, n + 1)
                if kind == "k":
                    ins = v.tensor_copy(kT[:, c, h * HALF_K:(h + 1) * HALF_K], b[:, 0:HALF_K])
                elif kind == "q":
                    ins = v.tensor_scalar(qT[:, c, :], b[:, :], HD ** -0.5, None, ALU.mult)
                elif kind == "v":
                    rows = META if c == 0 else P
                    ins = v.tensor_copy(vN[0:rows, c, :], b[0:rows, :])
                elif kind == "cx":
                    if c >= 1:
                        evac_wait(v, jobs.index(("cc", c - 1, 1)))
                    ins = v.tensor_copy(cxT[:, h * HALF_U:(h + 1) * HALF_U], b[:, 0:HALF_U])
                elif kind == "cc":
                    evac_wait(v, jobs.index(("cx", c, h)))
                    ins = v.tensor_tensor(uT[:, c, h * HALF_U:(h + 1) * HALF_U], b[:, 0:HALF_U], cxT[:, h * HALF_U:(h + 1) * HALF_U], ALU.mult)
                else:
                    o = mixT[:, NC_ + c, :]
                    v.wait_ge(conv_step, 2 * NC_ + c + 1)
                    ins = v.tensor_tensor(o, b[:, :], o, ALU.mult)
                ins.then_inc(proj_dve, 1)

            def width_norm(part):
                v.wait_ge(nroot, part + 1)
                v.reciprocal(rstd[1], rstd[0]).then_inc(conv_step, 1)
                steps[0] += 1
                v.wait_ge(conv_step, steps[0])
                for c in range(NC_):
                    o = mixT[:, c + (0 if part else NC_), :]
                    g = vec((G_ATT if part else G_CONV) + c)
                    v.scalar_tensor_tensor(out=o, in0=o, scalar=g, in1=rstd[1], op0=ALU.mult, op1=ALU.mult).then_inc(nscaled, 1)

            width_norm(0)
            v.wait_ge(nscaled, NC_)
            v.wait_ge(masks_ready, 3)
            for s in range(NI + 1):
                if s < NI:
                    h, b = att_items[s]
                    t0, keys = span(b)
                    v.wait_ge(z_done, s + 1)
                    if s >= NA:
                        v.wait_ge(sp_done, s - NA + 1)
                    v.tensor_scalar(za[s % NA][0:keys, 0:T - t0].bitcast(I32), banks[s % LB][0:keys, 0:T - t0].bitcast(I32),
                                    0x7FFFFFFF, None, ALU.bitwise_and).then_inc(abs_done, 1)
                if s >= 1:
                    i = s - 1
                    h, b = att_items[i]
                    t0, keys = span(b)
                    v.wait_ge(ln_done, i + 1)
                    if i >= NSP:
                        v.wait_ge(logw_done, i - NSP + 1)
                        v.wait_ge(later_done, masks_before[i - NSP + 1])
                    v.scalar_tensor_tensor(out=sp[i % NSP][0:keys, 0:T - t0], in0=banks[i % LB][0:keys, 0:T - t0], scalar=0.0,
                                           in1=za[i % NA][0:keys, 0:T - t0], op0=ALU.max, op1=ALU.add).then_inc(sp_done, 1)
                    if b >= 0:
                        v.wait_ge(sp_done, i + 1)
                        v.tensor_tensor(sp[i % NSP][:, 0:P], sp[i % NSP][:, 0:P], causal, ALU.mult).then_inc(masked, 1)
                if s >= 15 and (s - 15) % 10 == 0 and s < NI:
                    c = (s - 15) // 10
                    v.wait_ge(av_done, 10 * (c + 1))
                    v.tensor_copy(mixT[:, c, :], banks[LB + c % 2][:, :]).then_inc(att_copied, 1)
            v.wait_ge(av_done, NI)
            v.tensor_copy(mixT[:, NC_ - 1, :], banks[LB + (NC_ - 1) % 2][:, :]).then_inc(att_copied, 1)
            v.wait_ge(att_copied, NC_)
            width_norm(1)
            at_ = LATE

            def late(*shape, dt=None):
                nonlocal at_
                n = 1
                for q in shape:
                    n *= q
                r = view(ring, at_, *shape)
                at_ += n
                return r

            v.wait_ge(late_in, 64)
            for i in range(NT):
                for n in range(2):
                    v.wait_ge(outp, 2 * i + n + 1)
                    o = res[:, i, n * 512:(n + 1) * 512]
                    v.tensor_tensor(o, banks[(2 * i + n) % 4][:, :], o, ALU.add).then_inc(res_added, 1)
                if i >= 1:
                    v.wait_ge(logit_done, i)
                    v.tensor_tensor(logits[:, i - 1, :], banks[6][:, 0:E], b_router_b, ALU.add).then_inc(route, 1)
                v.wait_ge(row_root, i + 1)
                v.reciprocal(rs[:, i:i + 1], rs[:, i:i + 1]).then_inc(row_var, 1)
                v.wait_ge(row_var, i + 1)
                v.wait_ge(res_added, 2 * (i + 1))
                v.scalar_tensor_tensor(out=rows2[i % 2], in0=res[:, i, :], scalar=rs[:, i:i + 1], in1=g_ffn_b,
                                       op0=ALU.mult, op1=ALU.mult).then_inc(row_ready, 1)
            v.wait_ge(logit_done, NT)
            v.tensor_tensor(logits[:, NT - 1, :], banks[6][:, 0:E], b_router_b, ALU.add).then_inc(route, 1)
            v.wait_ge(route, NT)
            chain = [NT]

            def step(ins):
                chain[0] += 1
                ins.then_inc(route, 1)
                v.wait_ge(route, chain[0])

            for i in range(NT):
                v.max(top[:, i, :], logits[:, i, :]).then_inc(route, 1)
            chain[0] += NT
            v.wait_ge(route, chain[0])
            for i in range(NT):
                v.max_index(top_e[:, i, :], top[:, i, :], logits[:, i, :]).then_inc(route, 1)
            chain[0] += NT
            v.wait_ge(route, chain[0])
            v.tensor_tensor(gates[:, :, :], top[:, :, 0:TOPK], top[:, :, 0:1].to_broadcast([P, NT, TOPK]), ALU.subtract).then_inc(gate_exp, 1)
            chosen = late(NT, 8)
            step(v.tensor_copy(chosen, top_e[:, :, :]))
            e_no = late(E)
            v.wait_ge(slots_ready, 1)
            step(v.tensor_copy(e_no, slot_no[:, 0:E]))
            picks = [late(NT, E) for _ in range(TOPK)]
            e_all = e_no.rearrange("p (a e) -> p a e", a=1).to_broadcast([P, NT, E])
            for k in range(TOPK):
                ins = v.tensor_tensor(picks[k], e_all, chosen[:, :, k:k + 1].to_broadcast([P, NT, E]), ALU.is_equal)
                ins.then_inc(route, 1)
            chain[0] += TOPK
            v.wait_ge(route, chain[0])
            mask = late(NT, E)
            step(v.tensor_tensor(mask, picks[0], picks[1], ALU.add))
            step(v.tensor_tensor(mask, mask, picks[2], ALU.add))
            step(v.tensor_tensor(mask, mask, picks[3], ALU.add))
            v.tensor_copy(onehot[:, :, 0:E], mask).then_inc(mask_ready, 1)
            step(v.scalar_tensor_tensor(out=choice[:, :, :], in0=picks[2], scalar=2.0, in1=picks[1], op0=ALU.mult, op1=ALU.add))
            step(v.scalar_tensor_tensor(out=choice[:, :, :], in0=picks[3], scalar=3.0, in1=choice[:, :, :], op0=ALU.mult, op1=ALU.add))
            v.wait_ge(pos_done, 1)
            step(v.scalar_tensor_tensor(out=place[:, :, :], in0=banks[7][:, 0:NT * E].rearrange("p (a e) -> p a e", e=E), scalar=4096.0,
                                        in1=mask, op0=ALU.add, op1=ALU.mult))
            step(v.tensor_scalar(place[:, :, :], place[:, :, :], -4096.0, None, ALU.add))
            counts, extra, cum, one_e = late(E), late(E), late(E), late(E)
            step(v.tensor_copy(counts, banks[7][:, NT * E:(NT + 1) * E]))
            step(v.memset(one_e, 1.0))
            step(v.tensor_scalar(extra, counts, float(SLOTS), None, ALU.is_gt))
            for b in range(2, BLOCKS):
                step(v.scalar_tensor_tensor(out=extra, in0=counts, scalar=float(SLOTS * b), in1=extra, op0=ALU.is_gt, op1=ALU.add))
            step(v.tensor_tensor_scan(cum, one_e, extra, 0.0, ALU.mult, ALU.add))
            done = view(ring, 3 * GU_HALF, KEYS, E)
            key_e, key_b, key_end, key_no = late(KEYS), late(KEYS), late(KEYS), late(KEYS)
            step(v.tensor_copy(key_no, slot_no[:, 0:KEYS]))
            step(v.tensor_tensor(done, cum.rearrange("p (a e) -> p a e", a=1).to_broadcast([P, KEYS, E]),
                                 key_no.rearrange("p (k a) -> p k a", a=1).to_broadcast([P, KEYS, E]), ALU.is_le))
            step(v.tensor_reduce(key_e, done, AX.X, ALU.add))
            step(v.tensor_tensor(done, done, extra.rearrange("p (a e) -> p a e", a=1).to_broadcast([P, KEYS, E]), ALU.mult))
            step(v.tensor_reduce(key_b, done, AX.X, ALU.add))
            step(v.tensor_scalar(key_end, key_e, float(E), None, ALU.is_equal))
            step(v.tensor_tensor(key_b, key_no, key_b, ALU.subtract))
            step(v.scalar_tensor_tensor(out=key_b, in0=key_end, scalar=float(BLOCKS), in1=key_b, op0=ALU.mult, op1=ALU.add))
            step(v.memset(shift[:, 0:E], 0.0))
            step(v.tensor_scalar(shift[:, E:ITEMS], key_b[:, 0:ITEMS - E], 1.0, -float(SLOTS), ALU.add, ALU.mult))
            step(v.tensor_scalar(key_e, key_e, float(E - 1), None, ALU.min))
            step(v.tensor_copy(item_e[:, 0:E], slot_no[0:1, 0:E]))
            v.tensor_copy(item_e[:, E:ITEMS], key_e[0:1, 0:ITEMS - E]).then_inc(table_ready, 1)
            evens, below = late(KEYS), late(KEYS)
            step(v.tensor_scalar(evens, key_no, 2.0, None, ALU.mult))
            step(v.tensor_scalar(below, evens, cum[:, E - 1:E], None, ALU.is_lt))
            step(v.tensor_reduce(key_end[:, 0:1], below, AX.X, ALU.add))
            step(v.tensor_scalar(trips[:, 0:1], key_end[0:1, 0:1], float(E // 2), None, ALU.add))
            v.tensor_scalar(trips[:, 1:2], key_end[0:1, 0:1], float(E // 2 - 1), None, ALU.add).then_inc(table_ready, 1)
            gsum = late(NT)
            v.wait_ge(gate_exp, 2)
            step(v.tensor_reduce(gsum, gates[:, :, :], AX.X, ALU.add))
            step(v.reciprocal(gsum, gsum))
            step(v.tensor_tensor(gates[:, :, :], gates[:, :, :], gsum.rearrange("p (a b) -> p a b", b=1).to_broadcast([P, NT, TOPK]), ALU.mult))
            for k in range(TOPK):
                v.tensor_tensor(picks[k], picks[k], gates[:, :, k:k + 1].to_broadcast([P, NT, E]), ALU.mult).then_inc(route, 1)
            chain[0] += TOPK
            v.wait_ge(route, chain[0])
            v.wait_ge(logit_done, NT)
            step(v.tensor_tensor(mask, picks[0], picks[1], ALU.add))
            step(v.tensor_tensor(mask, mask, picks[2], ALU.add))
            dense = rowsT[0][:, 0:NT, 0:E]
            v.tensor_tensor(dense, mask, picks[3], ALU.add).then_inc(mask_ready, 1)
            v.wait_ge(dense_turned, 1)
            v.tensor_copy(rowsT[1][0:E, 0:NT, :], banks[6][0:E, :].rearrange("p (a b) -> p a b", b=P)).then_inc(dense_ready, 1)
            for m in range(2 * NT):
                v.wait_ge(bias_done, m + 1)
                o = res[:, m // 2, (m % 2) * 512:(m % 2 + 1) * 512]
                v.tensor_tensor(o, banks[m % 4][:, :], o, ALU.add).then_inc(base_ready, 1)
            assert at_ <= 4 * GU_HALF

            def prepare(i, par, number):
                e = v.value_load(item_e[0:1, number], min_val=0, max_val=E - 1)
                v.wait_ge(idx_summed, i)
                v.tensor_copy(ids[:, :, 3:4], choice[:, :, bass.ds(e, 1)]).then_inc(prep_step, 1)
                v.tensor_copy(b_item[:, par, :].rearrange("p (a b) -> p a b", b=1), bguT[:, :, bass.ds(e, 1)]).then_inc(prep_step, 1)
                v.tensor_scalar(place_i[:, :].rearrange("p (a b) -> p a b", b=1), place[:, :, bass.ds(e, 1)], shift[:, number], None, ALU.add).then_inc(prep_step, 1)
                v.wait_ge(prep_step, i * 3 + 3)
                v.tensor_tensor(onehot[:, :, :], slot_no[:, :].rearrange("p (a s) -> p a s", a=1).to_broadcast([P, NT, SLOTS]),
                                place_i[:, :].rearrange("p (a b) -> p a b", b=1).to_broadcast([P, NT, SLOTS]), ALU.is_equal).then_inc(onehot_ready, 1)

            def indices(i, par):
                v.wait_ge(idx_summed, i + 1)
                v.tensor_copy(slot_f[:, :], banks[4][0:SLOTS, 504:508]).then_inc(idx_copied, 1)
                v.wait_ge(idx_copied, i + 1)
                v.tensor_scalar(slot_g[:, 0:1], slot_f[:, 2:3], -SKIP, SKIP, ALU.mult, ALU.add).then_inc(idx_step, 1)
                v.wait_ge(idx_step, i * 3 + 1)
                v.scalar_tensor_tensor(out=slot_g[:, 1:2], in0=slot_f[:, 0:1], scalar=slot_f[:, 1:2], in1=slot_g[:, 0:1], op0=ALU.add, op1=ALU.add).then_inc(idx_step, 1)
                v.wait_ge(idx_step, i * 3 + 2)
                v.tensor_tensor(row_idx_next[:, par:par + 1], slot_g[:, 1:2], slot_f[:, 3:4], ALU.add).then_inc(idx_step, 1)
                v.wait_ge(xs_in, i * 16)
                v.tensor_scalar(tok_idx[:, :], slot_g[:, 1:2], 0.25, None, ALU.mult).then_inc(idx_ready, 1)

            def swiglu(i, j, h):
                bias = [b_item[:, j, s * NF + h * HC:s * NF + (h + 1) * HC].rearrange("p (a b) -> p a b", b=1).to_broadcast([P, HC, SLOTS]) for s in range(2)]
                raw = [banks[2 * h + s][:, 0:HC * SLOTS].rearrange("p (a b) -> p a b", b=SLOTS) for s in range(2)]
                n = i * 6 + 3 * h
                v.wait_ge(gu_done, i * 2 + (h + 1))
                v.wait_ge(hid_ready, i * 2 + (h + 1))
                v.tensor_tensor(gate_t, raw[0], bias[0], ALU.add).then_inc(glu_part, 1)
                v.wait_ge(glu_part, n + 1)
                v.tensor_scalar(gate_t, gate_t, LIMIT, None, ALU.min).then_inc(gate_ready, 1)
                v.tensor_tensor(lin_t, raw[1], bias[1], ALU.add).then_inc(glu_read, 1)
                v.wait_ge(glu_read, i * 2 + (h + 3))
                v.tensor_scalar(lin_t, lin_t, LIMIT, -LIMIT, ALU.min, ALU.max).then_inc(glu_part, 1)
                v.wait_ge(sig_done, i * 2 + (h + 1))
                v.wait_ge(gate_ready, i * 2 + (h + 1))
                v.tensor_tensor(gate_t, gate_t, sig_t, ALU.mult).then_inc(glu_part, 1)
                v.wait_ge(glu_part, n + 3)
                v.scalar_tensor_tensor(out=hid[:, h * HC:(h + 1) * HC, :], in0=lin_t, scalar=1.0, in1=gate_t, op0=ALU.add, op1=ALU.mult).then_inc(hid_ready, 1)

            v.memset(slot_g[:, 0:1], 0.0).then_inc(glu_read, 2)
            v.memset(slot_g[:, 1:2], 0.0).then_inc(hid_ready, 1)
            v.memset(slot_g[:, 2:3], 0.0).then_inc(row_moved, 1)
            v.memset(row_idx[:, :], int(SKIP)).then_inc(bufs_clear, 1)
            v.memset(ys, 0.0).then_inc(bufs_clear, 1)
            v.memset(yT, 0.0).then_inc(yT_ready, 1)
            v.memset(xs, 0.0).then_inc(bufs_clear, 1)
            v.wait_ge(table_ready, 2)
            prepare(0, 0, slice(0, 1))
            indices(0, 0)
            n_trips = v.value_load(trips[0:1, 0:1], min_val=E // 2, max_val=(E + EXTRA + 1) // 2)
            with v.Fori(0, n_trips) as it:
                for j in range(2):
                    i = it * 2 + j
                    v.wait_ge(y_out, i * 16 + 16)
                    v.wait_ge(idx_step, i * 3 + 3)
                    if j == 0:
                        v.wait_ge(bufs_clear, 3)
                    v.tensor_copy(row_idx[:, j:j + 1], row_idx_next[:, j:j + 1]).then_inc(row_moved, 1)
                    prepare(i + 1, 1 - j, bass.ds(it * 2 + (j + 1), 1))
                    swiglu(i, j, 0)
                    indices(i + 1, 1 - j)
                    swiglu(i, j, 1)
            def combine(i):
                v.wait_ge(picked_in[i], 16)
                for k in range(TOPK):
                    if k:
                        v.wait_ge(final_sum, TOPK * i + k)
                    v.scalar_tensor_tensor(out=res[:, i, :], in0=picked[i][:, k, :], scalar=gates[:, i, k:k + 1], in1=res[:, i, :],
                                           op0=ALU.mult, op1=ALU.add).then_inc(final_sum, 1)

            def finish(i):
                v.wait_ge(final_rt, i + 1)
                v.reciprocal(rs[:, i:i + 1], rs[:, i:i + 1]).then_inc(final_step, 1)
                v.wait_ge(final_step, i + 1)
                v.scalar_tensor_tensor(out=final_rows[i], in0=res[:, i, :], scalar=rs[:, i:i + 1], in1=g_final_b,
                                       op0=ALU.mult, op1=ALU.mult).then_inc(final_ready, 1)

            v.wait_ge(final_in, 16)
            for i in range(NT):
                combine(i)
                if i >= 1:
                    finish(i - 1)
            finish(NT - 1)

        @block.gpsimd
        def _(g):
            steps = [0]

            def step(ins):
                steps[0] += 1
                ins.then_inc(const_step, 1)
                g.wait_ge(const_step, steps[0])

            def triangle(t, compare, base, fill):
                return g.affine_select(out=t, in_=t, compare_op=compare, fill=fill, base=base, pattern=[[1, P]], channel_multiplier=-1)

            step(g.memset(ident[:, :], 0.0))
            triangle(ident[:, :], ALU.not_equal, 0, 1.0).then_inc(ident_ready, 1)
            g.memset(ones[:, :], 1.0).then_inc(ones_ready, 1)
            step(g.memset(ones_h[:, :], 1.0))
            step(g.memset(before[:, :], 1.0))
            step(triangle(before[:, :], ALU.is_gt, 0, 0.0))
            step(g.iota(slot_int, pattern=[[1, SLOTS]], base=0, channel_multiplier=0))
            step(g.tensor_copy(slot_no[:, :], slot_int))
            step(g.memset(ids[:, :, :], 1.0))
            step(g.iota(slot_int[:, 0:NT], pattern=[[0, NT]], base=0, channel_multiplier=TOPK))
            step(g.tensor_copy(ids[:, :, 0:1], slot_int[:, 0:NT].rearrange("p (a b) -> p a b", b=1)))
            step(g.iota(slot_int[:, 0:NT], pattern=[[TOPK * P, NT]], base=0, channel_multiplier=0))
            g.tensor_copy(ids[:, :, 1:2], slot_int[:, 0:NT].rearrange("p (a b) -> p a b", b=1)).then_inc(slots_ready, 1)
            step(g.memset(neg_tri, -1.0))
            g.affine_select(out=neg_tri, in_=neg_tri, compare_op=ALU.is_ge, fill=0.0, base=0, pattern=[[-1, P]], channel_multiplier=1).then_inc(masks_ready, 1)
            g.memset(neg_one, -1.0).then_inc(masks_ready, 1)
            step(g.memset(causal, 1.0))
            triangle(causal, ALU.is_gt, 0, 0.0).then_inc(masks_ready, 1)
            g.wait_ge(nscaled, NC_)
            g.wait_ge(masks_ready, 3)
            for s in range(NI + 2):
                if s < NI:
                    h, b = att_items[s]
                    t0, keys = span(b)
                    acc = later[h % 2]
                    if b >= 0:
                        g.wait_ge(masked, masks_before[s + 1])
                        if b == 3:
                            if s >= 2:
                                g.wait_ge(logw_done, s - 1)
                            g.memset(acc[:, 0:t0], 0.0)
                            g.tensor_copy(acc[:, t0:T], sp[s % NSP][:, 0:T - t0]).then_inc(later_done, 1)
                        else:
                            g.wait_ge(logw_done, s + 1)
                            g.wait_ge(later_done, masks_before[s - 1])
                            g.tensor_tensor(acc[:, t0:T], acc[:, t0:T], sp[s % NSP][:, 0:T - t0], ALU.add).then_inc(later_done, 1)
                if s >= 2:
                    i = s - 2
                    if att_items[i][1] >= 0:
                        g.wait_ge(w_done, i + 1)
                        w = wT[i % NW][:, 0:P]
                        g.affine_select(out=w, in_=w, compare_op=ALU.is_gt, fill=0.0, base=0, pattern=[[1, P]], channel_multiplier=-1).then_inc(w_masked, 1)

            last_token, last_row = g.to_reg(T - 1), g.to_reg(T * TOPK - 1)

            def gather(before_, upto):
                g.wait_ge(bufs_clear, 3)
                g.wait_ge(idx_ready, upto)
                g.wait_ge(xs_turned, before_)
                g.indirect_dma_start(xs, None, ffn_rows, bass.IndirectOffsetOnAxis(ap=tok_idx[:, 0:1], axis=0),
                                     bounds_check=last_token, oob_is_err=False).then_inc(xs_in, 16)

            def scatter(before_, upto, par):
                g.wait_ge(bufs_clear, 3)
                g.wait_ge(ys_ready, upto)
                g.wait_ge(row_moved, upto)
                g.indirect_dma_start(choice_rows, bass.IndirectOffsetOnAxis(ap=row_idx[:, par:par + 1], axis=0), ys, None,
                                     bounds_check=last_row, oob_is_err=False).then_inc(y_out, 16)

            even, odd, second = (g.alloc_register(n) for n in ("even", "odd", "second"))
            g.wait_ge(bufs_clear, 3)
            for i in range(NT):
                g.wait_ge(row_stored[i], 16)
            g.wait_ge(table_ready, 2)
            gather(0, 1)
            g.indirect_dma_start(choice_rows, bass.IndirectOffsetOnAxis(ap=row_idx[:, 0:1], axis=0), ys, None,
                                 bounds_check=last_row, oob_is_err=False).then_inc(y_out, 16)
            n_trips = g.value_load(trips[0:1, 0:1], min_val=E // 2, max_val=(E + EXTRA + 1) // 2)
            g.reg_mov(even, 0)
            g.reg_mov(odd, 1)
            g.reg_mov(second, 2)
            with g.Fori(0, n_trips) as it:
                scatter(even, odd, 1)
                gather(odd, second)
                scatter(odd, second, 0)
                g.reg_add(even, even, 2)
                g.reg_add(odd, odd, 2)
                g.reg_add(second, second, 2)
                gather(even, odd)
            scatter(even, odd, 1)


_INS = ['x', 'meta_tokens', 'g_mix', 'w_in', 'g_attn_out', 'conv_w', 'conv_b', 'g_conv_out', 'w_out', 'g_ffn',
        'w_router', 'b_router', 'w_gu', 'b_gu', 'w_down', 'b_down', 'g_final']


def kernel(**inputs):
    import numpy as _np
    import concourse.bacc as _bacc
    from concourse import mybir as _mybir
    from concourse.bass_utils import run_bass_kernel_spmd as _run

    nc = _bacc.Bacc("TRN2", target_bir_lowering=False, num_devices=1)
    arrays, args = {}, []
    for name in _INS:
        a = _np.ascontiguousarray(inputs[name])
        arrays[f"in_{name}_dram"] = a
        args.append(nc.dram_tensor(f"in_{name}_dram", a.shape, _mybir.dt.from_np(a.dtype), kind="ExternalInput").ap())
    args.append(nc.dram_tensor("out_dram", (1, T, D), F32, kind="ExternalOutput").ap())
    build(nc, *args)
    r = _run(nc, [arrays], core_ids=[0])
    return r.results[0]["out_dram"]
```

```python
from contextlib import ExitStack

import concourse.bass as bass
from concourse import mybir

F32 = mybir.dt.float32
F32R = mybir.dt.float32r
BF16 = mybir.dt.bfloat16
I32 = mybir.dt.int32
U32 = mybir.dt.uint32
ALU = mybir.AluOpType
ACT = mybir.ActivationFunctionType
AX = mybir.AxisListType

P = 128
D = 1024
KD = D // P
T = 512
NT = T // P
META = 16
TM = META + T
AW = 512
HEADS, HD = 8, 64
CW = 512
NC_ = AW // P
TAPS = 3
UT = T + TAPS - 1
E, TOPK = 32, 4
FF = 1024
NF = FF // P
EPS = 1e-6
LIMIT, ALPHA = 7.0, 1.702

SLOTS = 96
BLOCKS = -(-T // SLOTS)
EXTRA = T * TOPK // SLOTS
ITEMS = E + EXTRA + 3
KEYS = 24
assert EXTRA + 3 <= KEYS
SKIP = float(1 << 20)

GU_UNITS = 2 * KD
UNITS = GU_UNITS + NF
BY_ALL = range(UNITS)
BY_POOL = (3, 7, 11, 15, 20, 22)
BY_DVE = tuple(u for u in BY_ALL if u not in BY_POOL)
STAGES = 4
assert GU_UNITS % STAGES == 0 and UNITS % STAGES == 0


def through(by, it, u, skip=0):
    c = sum(1 for m in by if skip <= m <= u)
    return c if it is None else it * len(by) + (len(by) + c)


def free_again(it, u, skip=0):
    c = u - STAGES + 1 - skip
    if it is None:
        return c if c > 0 else None
    return it * UNITS + (UNITS + c)


def step_of(by, it, u):
    mine = [m for m in by if m < GU_UNITS]
    return 1 + (len(by) - len(mine) if it is None and u == mine[-1] else 0)


def build(nc, x, meta_tokens, g_mix, w_in, g_attn_out, conv_w, conv_b, g_conv_out, w_out, g_ffn,
          w_router, b_router, w_gu, b_gu, w_down, b_down, g_final, out):
    with ExitStack() as ctx:
        def sb(name, shape, dt=F32):
            return ctx.enter_context(nc.sbuf_tensor(name, shape, dt))

        def sem(name):
            return ctx.enter_context(nc.semaphore(name))

        ffn_rows = nc.dram_tensor("ffn_rows", [T, D], F32, kind="Internal").ap()
        choice_rows = nc.dram_tensor("choice_rows", [T * TOPK, D], F32, kind="Internal").ap()

        WIN_SLOTS = 3
        GROUP = KD * 512
        TEMPS = 5120
        MIX = WIN_SLOTS * GROUP
        HEADS_AT = MIX + KD * TM + 3 * D + UT + P
        LATE_AT = 6 * 2048 + TEMPS + KD * D
        RING = LATE_AT + 2400
        ring = sb("ring", [P, RING])
        MISC = KD * T + NC_ * UT
        misc = sb("misc", [P, MISC])
        res = sb("res", [P, NT, D])

        def view(t, start, *shape, rows=P, dt=None):
            n = 1
            for s in shape:
                n *= s
            v = t[0:rows, start:start + n]
            if len(shape) == 2:
                v = v.rearrange("p (a b) -> p a b", b=shape[1])
            elif len(shape) == 3:
                v = v.rearrange("p (a b c) -> p a b c", b=shape[1], c=shape[2])
            return v

        PAIR = 2 * FF
        gu_pair = [view(ring, TEMPS + KD * D + g * PAIR if g < 6 else (g - 6) * PAIR, 2, FF) for g in range(KD)]
        dn_pair = [view(ring, (2 + g) * PAIR, 2, D) for g in range(NF // 2)]
        assert (2 + NF // 2) * PAIR <= TEMPS + KD * D
        stage = sb("stage", [P, STAGES, 2, FF], F32R)

        win = [view(ring, (g % WIN_SLOTS) * GROUP, KD, 512) for g in range(6)]
        at = HEADS_AT
        qT = view(ring, at, NC_, T); at += NC_ * T
        kT = view(ring, at, NC_, TM); at += NC_ * TM
        vN = view(ring, at, NT + 1, AW); at += (NT + 1) * AW
        neg_tri = view(ring, at, P); at += P
        neg_one = view(ring, at, P); at += P
        causal = view(ring, at, P); at += P
        assert at <= RING
        at = 0
        NA, NSP, NW = 2, 3, 3
        za = [view(ring, at + i * T, T) for i in range(NA)]; at += NA * T
        sp = [view(ring, at + i * T, T) for i in range(NSP)]; at += NSP * T
        wT = [view(ring, at + i * T, T) for i in range(NW)]; at += NW * T
        later = [view(ring, at + i * T, T) for i in range(2)]; at += 2 * T
        assert at <= TEMPS
        assert NA + NSP + NW + 2 >= 4
        sq = [za[0], za[1], sp[0], sp[1]]
        rstd = [wT[0], wT[1]]
        at = 0
        rows2 = [view(ring, at + i * D, D) for i in range(2)]; at += 2 * D
        rowsT = [view(ring, at + i * D, KD, P) for i in range(2)]; at += 2 * D
        b_down_sb = view(ring, at, D, rows=E); at += D
        assert at <= TEMPS
        at = LATE_AT
        g_ffn_b = view(ring, at, D); at += D
        w_router_sb = view(ring, at, KD, E); at += KD * E
        b_router_b = view(ring, at, E); at += E
        LATE = at
        wo = view(ring, TEMPS, KD, D)
        hT = view(ring, MIX, KD, TM)
        xn = [view(ring, MIX + KD * TM + i * D, D) for i in range(2)]
        meta_rows = view(ring, MIX + KD * TM + 2 * D, D, rows=META)
        cxT = view(ring, MIX + KD * TM + 3 * D, UT)
        vec_rows = view(ring, MIX + KD * TM + 3 * D + UT, P, rows=32)
        bgu_rows = view(misc, 0, 2 * FF, rows=2 * E)
        slot_int = misc[:, 2 * FF:2 * FF + SLOTS].bitcast(I32)
        mixT = view(misc, 0, KD, T)
        uT = view(misc, KD * T, NC_, UT)
        at = 0
        xs = view(misc, at, D, rows=SLOTS); at += D
        hid = view(misc, at, FF, rows=SLOTS); at += FF
        ys = view(misc, at, D, rows=SLOTS); at += D
        gate_t = view(misc, at, FF, rows=SLOTS); at += FF
        lin_t = view(misc, at, FF, rows=SLOTS); at += FF
        sig_t = view(misc, at, FF, rows=SLOTS); at += FF
        assert at <= MISC
        picked = [view(ring, i * TOPK * D, TOPK, D) for i in range(NT)]
        g_final_b = view(ring, NT * TOPK * D, D)
        final_junk = view(ring, (NT * TOPK + 1) * D, D)
        final_rows = [view(ring, (NT * TOPK + 2 + i) * D, D) for i in range(NT)]

        ident = sb("ident", [P, P])
        ones = sb("ones", [P, P])
        eps_t = sb("eps_t", [P, 1])
        before = sb("before", [P, P], BF16)
        ones_h = sb("ones_h", [P, P], BF16)
        vecT = sb("vecT", [P, 32])
        G_MIX, G_ATT, G_CONV, CONV_W, CONV_B = 0, 8, 12, 16, 28
        bgu = sb("bgu", [P, 2 * FF], F32R)
        bgu_row = sb("bgu_row", [P, 1])
        bgu_past = view(misc, 2 * FF + SLOTS, 1)
        sel = sb("sel", [P, SLOTS], F32R)
        xsT = sb("xsT", [P, 2, KD, SLOTS], F32R)
        hidT = sb("hidT", [P, 2, NF, SLOTS], F32R)
        ss = sb("ss", [P, 8])
        rs = sb("rs", [P, 8])
        logits = sb("logits", [P, NT, E])
        top = sb("top", [P, NT, 8])
        top_e = sb("top_e", [P, NT, 8], U32)
        gates = sb("gates", [P, NT, TOPK])
        place = sb("place", [P, NT, E])
        choice = sb("choice", [P, NT, E])
        shift = sb("shift", [P, ITEMS])
        item_e = sb("item_e", [1, ITEMS], I32)
        item_all = sb("item_all", [P, ITEMS])
        trips = sb("trips", [1, 1], I32)
        slot_no = sb("slot_no", [P, SLOTS])
        onehot = sb("onehot", [P, NT, SLOTS], BF16)
        place_i = sb("place_i", [P, NT])
        ids = sb("ids", [P, NT, 4], BF16)
        slot_f = sb("slot_f", [SLOTS, 4])
        slot_g = sb("slot_g", [SLOTS, 4])
        tok_idx = sb("tok_idx", [SLOTS, 1], U32)
        row_tab = sb("row_tab", [SLOTS, ITEMS + 1], U32)
        row_idx = sb("row_idx", [SLOTS, 1], U32)

        banks = [ctx.enter_context(nc.psum_tensor(f"bank{i}", [P, 512], F32)) for i in range(8)]

        x_in = [sem(f"x_in{i}") for i in range(NT + 1)]
        vec_in, bgu_in, late_in, wo_in = sem("vec_in"), sem("bgu_in"), sem("late_in"), sem("wo_in")
        win_in = [sem(f"win_in{g}") for g in range(6)]
        gu_in = [sem(f"gu_in{g}") for g in range(KD)]
        dn_in = [sem(f"dn_in{g}") for g in range(NF // 2)]
        rows_ready = sem("rows_ready")
        hi_done, lo_dve, lo_pool, unit_used = sem("hi_done"), sem("lo_dve"), sem("lo_pool"), sem("unit_used")
        ident_ready, ones_ready, masks_ready, slots_ready, eps_ready = (
            sem("ident_ready"), sem("ones_ready"), sem("masks_ready"), sem("slots_ready"), sem("eps_ready"))
        const_step, glu_part, glu_read, row_moved, final_step = sem("const_step"), sem("glu_part"), sem("glu_read"), sem("row_moved"), sem("final_step")
        squares, sq_dve, rms_act = sem("squares"), sem("sq_dve"), sem("rms_act")
        xn_ready, xn_turned = sem("xn_ready"), sem("xn_turned")
        hT_act, hT_dve = sem("hT_act"), sem("hT_dve")
        vec_turned, vec_ready, bgu_hi, bgu_ready = sem("vec_turned"), sem("vec_ready"), sem("bgu_hi"), sem("bgu_ready")
        proj_done, proj_act, proj_dve = sem("proj_done"), sem("proj_act"), sem("proj_dve")
        conv_step = sem("conv_step")
        z_done, abs_done, exp_done, ln_done, sp_done, masked = (sem("z_done"), sem("abs_done"), sem("exp_done"), sem("ln_done"), sem("sp_done"), sem("masked"))
        later_done, logw_done, w_done, w_masked, av_done, att_copied = (sem("later_done"), sem("logw_done"), sem("w_done"), sem("w_masked"), sem("av_done"), sem("att_copied"))
        nsq, nsum, nroot, nscaled = sem("nsq"), sem("nsum"), sem("nroot"), sem("nscaled")
        outp, res_added, row_sq, row_var, row_root, row_ready, row_turned, rowT_ready = (
            sem("outp"), sem("res_added"), sem("row_sq"), sem("row_var"), sem("row_root"), sem("row_ready"), sem("row_turned"), sem("rowT_ready"))
        row_stored = [sem(f"row_stored{i}") for i in range(NT)]
        logit_done, route, gate_exp, mask_ready, pos_done, dense_turned, dense_ready, bias_done, base_ready = (
            sem("logit_done"), sem("route"), sem("gate_exp"), sem("mask_ready"), sem("pos_done"), sem("dense_turned"), sem("dense_ready"), sem("bias_done"), sem("base_ready"))
        table_ready, bufs_clear = sem("table_ready"), sem("bufs_clear")
        onehot_ready, idx_summed, idx_copied, idx_step, idx_ready, prep_step = (
            sem("onehot_ready"), sem("idx_summed"), sem("idx_copied"), sem("idx_step"), sem("idx_ready"), sem("prep_step"))
        xs_in, xs_turned, xsT_hi, xsT_lo = sem("xs_in"), sem("xs_turned"), sem("xsT_hi"), sem("xsT_lo")
        hid_turned, hidT_hi, hidT_lo = sem("hid_turned"), sem("hidT_hi"), sem("hidT_lo")
        gate_ready, sig_done, hid_ready, sel_ready = (
            sem("gate_ready"), sem("sig_done"), sem("hid_ready"), sem("sel_ready"))
        ys_ready, y_out = sem("ys_ready"), sem("y_out")
        picked_in = [sem(f"picked_in{i}") for i in range(NT)]
        final_in, final_sum, final_sq, final_rt, final_ready, stored = (
            sem("final_in"), sem("final_sum"), sem("final_sq"), sem("final_rt"), sem("final_ready"), sem("stored"))

        HALF_K, HALF_U = TM // 2, UT // 2
        jobs = [("k", c, h) for c in range(NC_) for h in range(2)]
        jobs += [("q", c, 0) for c in range(NC_)]
        jobs += [("v", m, 0) for m in range(NT + 1)]
        jobs += [(kind, c, h) for c in range(NC_) for kind in ("cx", "cc") for h in range(2)]
        jobs += [("cb", c, 0) for c in range(NC_)]
        GROUP_OF = {"q": 0, "k": 1, "v": 2, "cb": 3, "cc": 4, "cx": 5}
        LOADS = ["k", "q", "v", "cx", "cc", "cb"]
        SLOT_OF = {kind: n for n, kind in enumerate(LOADS)}
        PROJ_BANKS = 4

        def evac_by_act(n):
            return jobs[n][0] in ("k", "q", "v", "cx") and n % 2 == 0

        def evac_wait(eng, n):
            by = [evac_by_act(m) for m in range(n + 1)]
            if by[n]:
                eng.wait_ge(proj_act, sum(by))
            else:
                eng.wait_ge(proj_dve, n + 1 - sum(by))

        def jobs_until(kind):
            return max(n for n, j in enumerate(jobs) if j[0] == kind) + 1

        att_items = [(2 * c + hh, b) for c in range(HEADS // 2) for b in (3, 2, 1, 0, -1) for hh in range(2)]
        NI = len(att_items)
        LB = 6

        def span(b):
            return (P * b, P) if b >= 0 else (0, META)

        masks_before = [sum(1 for h, b in att_items[:i] if b >= 0) for i in range(NI + 1)]

        block = ctx.enter_context(nc.Block())

        @block.sync
        def _(sp_):
            def load_gu(e, g):
                src = w_gu[0, e, g * P:(g + 1) * P, :] if isinstance(e, int) else \
                    w_gu[0, bass.ds(e, 1), g * P:(g + 1) * P, :].rearrange("o r f -> (o r) f")
                sp_.dma_start(gu_pair[g], src.rearrange("p (s f) -> p s f", s=2)).then_inc(gu_in[g], 16)

            def load_dn(e, g):
                src = w_down[0, e, 2 * g * P:2 * (g + 1) * P, :] if isinstance(e, int) else \
                    w_down[0, bass.ds(e, 1), 2 * g * P:2 * (g + 1) * P, :].rearrange("o r d -> (o r) d")
                sp_.dma_start(dn_pair[g], src.rearrange("(f p) d -> p f d", p=P)).then_inc(dn_in[g], 16)

            sp_.dma_start(meta_rows, meta_tokens[:, :]).then_inc(x_in[NT], 16)
            for i in range(NT):
                sp_.dma_start(res[:, i, :], x[0, i * P:(i + 1) * P, :]).then_inc(x_in[i], 16)
            for src, at_, n in ((g_mix[0], G_MIX, 8), (g_attn_out[0], G_ATT, 4), (g_conv_out[0], G_CONV, 4), (conv_b[0], CONV_B, 4)):
                sp_.dma_start(vec_rows[at_:at_ + n, :], src.rearrange("(a b) -> a b", b=P)).then_inc(vec_in, 16)
            sp_.dma_start(vec_rows[CONV_W:CONV_W + 12, :], conv_w[0].rearrange("t (a b) -> (t a) b", b=P)).then_inc(vec_in, 16)
            for r in range(2):
                sp_.dma_start(bgu_rows[r * E:(r + 1) * E, :], b_gu[0]).then_inc(bgu_in, 16)
            for n, kind in enumerate(LOADS):
                g = GROUP_OF[kind]
                if n >= WIN_SLOTS:
                    sp_.wait_ge(proj_done, jobs_until(LOADS[n - WIN_SLOTS]))
                sp_.dma_start(win[n], w_in[0, :, g * 512:(g + 1) * 512].rearrange("(k p) f -> p k f", p=P)).then_inc(win_in[n], 16)
            sp_.wait_ge(proj_done, len(jobs))
            sp_.dma_start(wo, w_out[0].rearrange("(k p) f -> p k f", p=P)).then_inc(wo_in, 16)
            for g in range(3):
                load_gu(0, g)
            sp_.wait_ge(nscaled, 2 * NC_)
            sp_.dma_start(g_ffn_b, g_ffn[0:1, :].to_broadcast([P, D])).then_inc(late_in, 16)
            sp_.dma_start(b_router_b, b_router[0:1, :].to_broadcast([P, E])).then_inc(late_in, 16)
            sp_.dma_start(w_router_sb, w_router[0].rearrange("(k p) e -> p k e", p=P)).then_inc(late_in, 16)
            sp_.dma_start(b_down_sb, b_down[0]).then_inc(late_in, 16)
            for g in range(3, 6):
                load_gu(0, g)
            for i in range(NT):
                sp_.wait_ge(row_ready, i + 1)
                sp_.dma_start(ffn_rows[i * P:(i + 1) * P, :], rows2[i % 2]).then_inc(row_stored[i], 16)
            sp_.wait_ge(outp, 2 * NT)
            sp_.wait_ge(base_ready, NT * 2)
            sp_.wait_ge(table_ready, 2)
            for i in range(NT):
                sp_.wait_ge(row_stored[i], 16)
            for g in range(6, KD):
                load_gu(0, g)

            full = sp_.value_load(trips[0:1, 0:1], min_val=E - 1, max_val=E - 1 + EXTRA)
            with sp_.Fori(0, full) as it:
                e1 = sp_.value_load(item_e[0:1, bass.ds(it + 1, 1)], min_val=0, max_val=E - 1)
                e0 = sp_.value_load(item_e[0:1, bass.ds(it, 1)], min_val=0, max_val=E - 1)
                for g in range(KD):
                    sp_.wait_ge(unit_used, it * UNITS + (2 * g + 2))
                    load_gu(e1, g)
                for g in range(NF // 2):
                    sp_.wait_ge(unit_used, it * UNITS + (GU_UNITS + 2 * g + 2))
                    load_dn(e0, g)
            e0 = sp_.value_load(item_e[0:1, bass.ds(full, 1)], min_val=0, max_val=E - 1)
            for g in range(NF // 2):
                sp_.wait_ge(unit_used, full * UNITS + (GU_UNITS + 2 * g + 2))
                load_dn(e0, g)
            sp_.wait_ge(unit_used, through(BY_ALL, full, UNITS - 1, GU_UNITS))
            sp_.dma_start(g_final_b, g_final.rearrange("(a d) -> a d", a=1).to_broadcast([P, D])).then_inc(final_in, 16)
            sp_.wait_ge(y_out, full * 16 + 48)
            for i in range(NT):
                sp_.dma_start(picked[i], choice_rows[i * P * TOPK:(i + 1) * P * TOPK, :].rearrange("(p k) d -> p k d", k=TOPK)).then_inc(picked_in[i], 16)
            for i in range(NT):
                sp_.wait_ge(final_ready, i + 1)
                sp_.dma_start(out[0, i * P:(i + 1) * P, :], final_rows[i]).then_inc(stored, 16)
            sp_.wait_ge(stored, 16 * NT)

        @block.tensor
        def _(pe):
            pe.wait_ge(ident_ready, 1)
            pe.wait_ge(vec_in, 5 * 16)
            pe.transpose(banks[4][:, 0:32], vec_rows[:, :], ident[0:32, 0:32]).then_inc(vec_turned, 1)
            for n in range(NT + 1):
                rows = META if n == 0 else P
                pe.wait_ge(xn_ready, n + 1)
                if n >= 2:
                    pe.wait_ge(hT_act, n - 1)
                    pe.wait_ge(hT_dve, n - 1)
                src = xn[n % 2]
                for c in range(KD):
                    b = banks[2 * (n % 2) + c // 4]
                    mm = pe.transpose(b[:, (c % 4) * P:(c % 4) * P + rows], src[0:rows, c * P:(c + 1) * P], ident[0:rows, 0:rows])
                mm.then_inc(xn_turned, 1)
            pe.wait_ge(hT_act, NT + 1)
            pe.wait_ge(hT_dve, NT + 1)
            for n, (kind, c, h) in enumerate(jobs):
                if n >= PROJ_BANKS:
                    evac_wait(pe, n - PROJ_BANKS)
                pe.wait_ge(win_in[SLOT_OF[kind]], 16)
                b = banks[n % PROJ_BANKS]
                w = win[SLOT_OF[kind]]
                for k in range(KD):
                    if kind == "v":
                        lo, rows = (0, META) if c == 0 else (META + (c - 1) * P, P)
                        o, lhs, rhs = b[0:rows, :], hT[:, k, lo:lo + rows], w[:, k, :]
                    else:
                        lo, cols = {"k": (h * HALF_K, HALF_K), "cx": (TM - UT + h * HALF_U, HALF_U),
                                    "cc": (TM - UT + h * HALF_U, HALF_U)}.get(kind, (META, T))
                        o, lhs, rhs = b[:, 0:cols], w[:, k, c * P:(c + 1) * P], hT[:, k, lo:lo + cols]
                    mm = pe.matmul(o, lhs, rhs, start=(k == 0), stop=(k == KD - 1))
                mm.then_inc(proj_done, 1)
            def width_norm(part):
                for c in range(NC_):
                    pe.wait_ge(nsq, part * NC_ + c + 1)
                    mm = pe.matmul(banks[4 + part][:, :], ones[:, :], sq[c], start=(c == 0), stop=(c == NC_ - 1))
                mm.then_inc(nsum, 1)

            for n in range(len(jobs) - PROJ_BANKS, len(jobs)):
                evac_wait(pe, n)
            pe.wait_ge(ones_ready, 1)
            width_norm(0)
            pe.wait_ge(nscaled, NC_)
            pe.wait_ge(masks_ready, 3)
            for s in range(NI + 4):
                if s < NI:
                    h, b = att_items[s]
                    t0, keys = span(b)
                    k0 = META + t0 if b >= 0 else 0
                    r = HD * (h % 2)
                    if s >= LB:
                        pe.wait_ge(w_done, s - LB + 1)
                    pe.matmul(banks[s % LB][0:keys, 0:T - t0], kT[r:r + HD, h // 2, k0:k0 + keys],
                              qT[r:r + HD, h // 2, t0:T], start=True, stop=True).then_inc(z_done, 1)
                if 2 <= s < NI + 2:
                    i = s - 2
                    h, b = att_items[i]
                    t0, keys = span(b)
                    L = banks[i % LB]
                    if b >= 0:
                        pe.wait_ge(masked, masks_before[i + 1])
                    else:
                        pe.wait_ge(sp_done, i + 1)
                    mm = pe.matmul(L[0:keys, 0:T - t0], neg_tri[0:keys, 0:keys], sp[i % NSP][0:keys, 0:T - t0],
                                   start=False, stop=True, skip_group_check=True)
                    if b != 3:
                        t1 = P * (b + 1)
                        pe.wait_ge(later_done, masks_before[i - 1])
                        mm = pe.matmul(L[0:keys, t1 - t0:T - t0], neg_one[:, 0:keys], later[h % 2][:, t1:T],
                                       start=False, stop=True, skip_group_check=True)
                    mm.then_inc(logw_done, 1)
                if 4 <= s < NI + 4:
                    i = s - 4
                    h, b = att_items[i]
                    t0, keys = span(b)
                    r = HD * (h % 2)
                    if b >= 0:
                        pe.wait_ge(w_masked, masks_before[i + 1])
                    else:
                        pe.wait_ge(w_done, i + 1)
                    if b == 3 and h % 2 == 0 and h >= 4:
                        pe.wait_ge(att_copied, h // 2 - 1)
                    pe.matmul(banks[LB + (h // 2) % 2][r:r + HD, t0:T], vN[0:keys, b + 1, HD * h:HD * (h + 1)],
                              wT[i % NW][0:keys, 0:T - t0], start=(b == 3), stop=True,
                              skip_group_check=True).then_inc(av_done, 1)
            width_norm(1)
            pe.wait_ge(wo_in, 16)
            pe.wait_ge(nscaled, 2 * NC_)
            def route_tile(i):
                pe.wait_ge(row_ready, i + 1)
                if i >= 1:
                    pe.wait_ge(rowT_ready, 2 * i)
                for c in range(KD):
                    mm = pe.transpose(banks[4 + c // 4][:, (c % 4) * P:(c % 4 + 1) * P], rows2[i % 2][:, c * P:(c + 1) * P], ident[:, :])
                mm.then_inc(row_turned, 1)
                pe.wait_ge(rowT_ready, 2 * (i + 1))
                if i == 0:
                    pe.wait_ge(late_in, 64)
                if i >= 1:
                    pe.wait_ge(route, i)
                for k in range(KD):
                    mm = pe.matmul(banks[6][:, 0:E], rowsT[i % 2][:, k, :], w_router_sb[:, k, :], start=(k == 0), stop=(k == KD - 1))
                mm.then_inc(logit_done, 1)

            for i in range(NT):
                for n in range(2):
                    m = 2 * i + n
                    if m >= 4:
                        pe.wait_ge(res_added, m - 3)
                    for k in range(KD):
                        mm = pe.matmul(banks[m % 4][:, :], mixT[:, k, i * P:(i + 1) * P], wo[:, k, n * 512:(n + 1) * 512],
                                       start=(k == 0), stop=(k == KD - 1))
                    mm.then_inc(outp, 1)
                if i >= 1:
                    route_tile(i - 1)
            route_tile(NT - 1)
            pe.wait_ge(mask_ready, 1)
            pe.wait_ge(slots_ready, 1)
            for i in range(NT):
                for m in range(i + 1):
                    pe.matmul(banks[7][:, i * E:(i + 1) * E], (before if m == i else ones_h)[:, :], onehot[:, m, 0:E],
                              start=(m == 0), stop=(m == i))
            for m in range(NT):
                mm = pe.matmul(banks[7][:, NT * E:(NT + 1) * E], ones_h[:, :], onehot[:, m, 0:E], start=(m == 0), stop=(m == NT - 1))
            mm.then_inc(pos_done, 1)
            pe.wait_ge(mask_ready, 2)
            for i in range(NT):
                mm = pe.transpose(banks[6][0:E, i * P:(i + 1) * P], rowsT[0][:, i, 0:E], ident[:, :])
            mm.then_inc(dense_turned, 1)
            pe.wait_ge(dense_ready, 1)
            for m in range(2 * NT):
                if m >= 4:
                    pe.wait_ge(base_ready, m - 3)
                pe.matmul(banks[m % 4][:, :], rowsT[1][0:E, m // 2, :], b_down_sb[:, (m % 2) * 512:(m % 2 + 1) * 512],
                          start=True, stop=True).then_inc(bias_done, 1)
            pe.wait_ge(base_ready, 2 * NT)

            def sum_ids(n):
                pe.wait_ge(onehot_ready, n + 1)
                for m in range(NT):
                    mm = pe.matmul(banks[7][0:SLOTS, 504:508], onehot[:, m, :], ids[:, m, :], start=(m == 0), stop=(m == NT - 1))
                mm.then_inc(idx_summed, 1)

            def turn(src, turned):
                for c in range(KD):
                    mm = pe.transpose(banks[6 + c // 4][:, (c % 4) * SLOTS:(c % 4 + 1) * SLOTS], src[:, c * P:(c + 1) * P], ident[0:SLOTS, 0:SLOTS])
                mm.then_inc(turned, 1)

            def lower_ready(it, u, skip=0):
                by, done = (BY_POOL, lo_pool) if u in BY_POOL else (BY_DVE, lo_dve)
                pe.wait_ge(done, through(by, it, u, skip))

            def split_product(out_bank, lhs, k, s, q, start, stop):
                for n, (x_half, w_half) in enumerate(((0, 0), (0, 1), (1, 0))):
                    mm = pe.matmul(out_bank[0:SLOTS, :], lhs[:, x_half, k, :], stage[:, s, w_half, q * 512:(q + 1) * 512],
                                   start=(start and n == 0), stop=(stop and n == 2))
                return mm

            def gu_unit(it, u):
                k, s = u // 2, u % 2
                lower_ready(it, u)
                for q in range(2):
                    mm = split_product(banks[2 * s + q], xsT, k, u % STAGES, q, False, k == KD - 1)
                mm.then_inc(unit_used, step_of(BY_ALL, it, u))

            def gate_and_up_biases():
                for b in range(4):
                    pe.matmul(banks[b][0:SLOTS, :], sel[:, :], bgu[:, b * 512:(b + 1) * 512], start=True, stop=False)

            def down_units(it, skip=0):
                for v in range(NF):
                    u = GU_UNITS + v
                    lower_ready(it, u, skip)
                    for q in range(2):
                        mm = split_product(banks[4 + q], hidT, v, u % STAGES, q, v == 0, v == NF - 1)
                    mm.then_inc(unit_used, 1)

            sum_ids(0)
            pe.wait_ge(idx_copied, 1)
            pe.wait_ge(xs_in, 16)
            turn(xs, xs_turned)
            pe.wait_ge(bgu_ready, 1)
            pe.wait_ge(xsT_hi, 1)
            pe.wait_ge(xsT_lo, 1)
            gate_and_up_biases()
            for u in range(GU_UNITS):
                gu_unit(None, u)
                if u == 7:
                    sum_ids(1)
            pe.wait_ge(xs_in, 32)
            turn(xs, xs_turned)
            pe.wait_ge(idx_copied, 2)
            trip = pe.value_load(trips[0:1, 0:1], min_val=E - 1, max_val=E - 1 + EXTRA)
            with pe.Fori(0, trip) as it:
                pe.wait_ge(sel_ready, it + 2)
                pe.wait_ge(xsT_hi, it + 2)
                pe.wait_ge(xsT_lo, it + 2)
                pe.wait_ge(glu_read, it * 2 + 2)
                pe.wait_ge(gate_ready, it * 2 + 2)
                gate_and_up_biases()
                for u in range(GU_UNITS):
                    gu_unit(it, u)
                    if u == 3:
                        pe.wait_ge(hid_ready, it * 2 + 2)
                        turn(hid, hid_turned)
                    if u == 8:
                        pe.wait_ge(hidT_hi, it + 1)
                        pe.wait_ge(hidT_lo, it + 1)
                        sum_ids(it + 2)
                pe.wait_ge(idx_copied, it + 3)
                pe.wait_ge(xs_in, it * 16 + 48)
                turn(xs, xs_turned)
                pe.wait_ge(ys_ready, it + 1)
                down_units(it)
            pe.wait_ge(xsT_hi, trip + 2)
            pe.wait_ge(xsT_lo, trip + 2)
            pe.wait_ge(hid_ready, trip * 2 + 2)
            turn(hid, hid_turned)
            pe.wait_ge(hidT_hi, trip + 1)
            pe.wait_ge(hidT_lo, trip + 1)
            pe.wait_ge(ys_ready, trip + 1)
            down_units(trip, GU_UNITS)

        @block.scalar
        def _(act):
            act.wait_ge(eps_ready, 1)
            for n in range(NT + 1):
                act.wait_ge(x_in[NT if n == 0 else n - 1], 16)
                src = meta_rows if n == 0 else res[:, n - 1, :]
                rows = META if n == 0 else P
                if n >= 2:
                    act.wait_ge(squares, n - 1)
                act.activation(xn[n % 2][0:rows, :], src, ACT.Square, accum_out=ss[0:rows, n:n + 1]).then_inc(squares, 1)
            act.wait_ge(squares, NT + 1)
            act.activation(rs[:, 0:5], ss[:, 0:5], ACT.Sqrt, scale=1.0 / D, bias=eps_t[:, :]).then_inc(rms_act, 1)
            act.wait_ge(vec_ready, 1)
            for n in range(NT + 1):
                lo, rows = (0, META) if n == 0 else (META + (n - 1) * P, P)
                act.wait_ge(xn_turned, n + 1)
                for c in range(4):
                    ins = act.activation(hT[:, c, lo:lo + rows], banks[2 * (n % 2)][:, c * P:c * P + rows], ACT.Copy,
                                         scale=vecT[:, G_MIX + c:G_MIX + c + 1])
                ins.then_inc(hT_act, 1)
            act.wait_ge(bgu_in, 32)
            act.activation(bgu[0:2 * E, :], bgu_rows, ACT.Copy).then_inc(bgu_hi, 1)
            for n, (kind, c, h) in enumerate(jobs):
                if evac_by_act(n):
                    act.wait_ge(proj_done, n + 1)
                    b = banks[n % PROJ_BANKS]
                    if kind == "k":
                        ins = act.activation(kT[:, c, h * HALF_K:(h + 1) * HALF_K], b[:, 0:HALF_K], ACT.Copy)
                    elif kind == "q":
                        ins = act.activation(qT[:, c, :], b[:, :], ACT.Copy, scale=HD ** -0.5)
                    elif kind == "v":
                        rows = META if c == 0 else P
                        ins = act.activation(vN[0:rows, c, :], b[0:rows, :], ACT.Copy)
                    else:
                        if c >= 1:
                            evac_wait(act, jobs.index(("cc", c - 1, 1)))
                        ins = act.activation(cxT[:, h * HALF_U:(h + 1) * HALF_U], b[:, 0:HALF_U], ACT.Copy)
                    ins.then_inc(proj_act, 1)

            def width_norm(part):
                for c in range(NC_):
                    if part:
                        act.wait_ge(att_copied, c + 1)
                    else:
                        evac_wait(act, jobs.index(("cb", c, 0)))
                    src = mixT[:, c + (0 if part else NC_), :]
                    act.activation(sq[c], src, ACT.Square).then_inc(nsq, 1)
                act.wait_ge(nsum, part + 1)
                act.activation(rstd[0], banks[4 + part][:, :], ACT.Sqrt, scale=1.0 / AW, bias=eps_t[:, :]).then_inc(nroot, 1)

            width_norm(0)
            act.wait_ge(nscaled, NC_)
            act.preload_act_table_set("natural_log_exp_and_others")
            for s in range(NI + 3):
                if s < NI:
                    h, b = att_items[s]
                    t0, keys = span(b)
                    a = za[s % NA][0:keys, 0:T - t0]
                    act.wait_ge(abs_done, s + 1)
                    act.activation(a, a, ACT.Exp, scale=-1.0).then_inc(exp_done, 1)
                    act.wait_ge(exp_done, s + 1)
                    act.activation(a, a, ACT.Ln, bias=1.0).then_inc(ln_done, 1)
                if s >= 3:
                    i = s - 3
                    h, b = att_items[i]
                    t0, keys = span(b)
                    act.wait_ge(logw_done, i + 1)
                    if i >= NW:
                        act.wait_ge(av_done, i - NW + 1)
                    act.activation(wT[i % NW][0:keys, 0:T - t0], banks[i % LB][0:keys, 0:T - t0], ACT.Exp).then_inc(w_done, 1)
            act.wait_ge(av_done, NI)
            width_norm(1)
            for i in range(NT):
                act.wait_ge(res_added, 2 * (i + 1))
                if i >= 1:
                    act.wait_ge(row_ready, i)
                if i >= 2:
                    act.wait_ge(row_stored[i - 2], 16)
                    act.wait_ge(row_turned, i - 1)
                act.activation(rows2[i % 2], res[:, i, :], ACT.Square, accum_out=ss[:, i:i + 1]).then_inc(row_sq, 1)
                act.wait_ge(row_sq, i + 1)
                act.activation(rs[:, i:i + 1], ss[:, i:i + 1], ACT.Sqrt, scale=1.0 / D, bias=eps_t[:, :]).then_inc(row_root, 1)
                act.wait_ge(row_turned, i + 1)
                if i >= 2:
                    act.wait_ge(logit_done, i - 1)
                for c in range(2):
                    act.activation(rowsT[i % 2][:, 4 * c:4 * c + 4, :], banks[4 + c][:, :].rearrange("p (a b) -> p a b", b=P), ACT.Copy).then_inc(rowT_ready, 1)
            act.wait_ge(gate_exp, 1)
            act.activation(gates[:, :, :], gates[:, :, :], ACT.Exp).then_inc(gate_exp, 1)

            def upper(it, u, skip=0):
                if u < GU_UNITS:
                    act.wait_ge(gu_in[u // 2], 16 if it is None else it * 16 + 32)
                    src = gu_pair[u // 2][:, u % 2, :]
                else:
                    act.wait_ge(dn_in[(u - GU_UNITS) // 2], it * 16 + 16)
                    src = dn_pair[(u - GU_UNITS) // 2][:, u % 2, :]
                free = free_again(it, u, skip)
                if free is not None:
                    act.wait_ge(unit_used, free)
                act.activation(stage[:, u % STAGES, 0, :], src, ACT.Copy).then_inc(hi_done, step_of(BY_ALL, it, u))

            def upper_turned(dst, done):
                for c in range(2):
                    ins = act.activation(dst[:, 0, 4 * c:4 * c + 4, :], banks[6 + c][:, 0:4 * SLOTS].rearrange("p (a b) -> p a b", b=SLOTS), ACT.Copy)
                ins.then_inc(done, 1)

            def sigmoid(n, q):
                act.wait_ge(gate_ready, n * 2 + (q + 1))
                act.activation(sig_t[:, q * 512:(q + 1) * 512], gate_t[:, q * 512:(q + 1) * 512], ACT.Sigmoid, scale=ALPHA).then_inc(sig_done, 1)

            def outputs_out(it):
                act.wait_ge(unit_used, it * UNITS + UNITS)
                act.wait_ge(y_out, it * 16 + 16)
                for c in range(2):
                    ins = act.activation(ys[:, 512 * c:512 * (c + 1)], banks[4 + c][0:SLOTS, :], ACT.Copy)
                ins.then_inc(ys_ready, 1)

            act.wait_ge(xs_turned, 1)
            upper_turned(xsT, xsT_hi)
            for u in range(GU_UNITS):
                upper(None, u)
            act.wait_ge(table_ready, 2)
            trip = act.value_load(trips[0:1, 0:1], min_val=E - 1, max_val=E - 1 + EXTRA)
            for q in range(2):
                sigmoid(0, q)
            act.wait_ge(xs_turned, 2)
            act.wait_ge(unit_used, GU_UNITS)
            upper_turned(xsT, xsT_hi)
            with act.Fori(0, trip) as it:
                for u in range(UNITS):
                    upper(it, u)
                    if u == 4:
                        outputs_out(it)
                    if u == 8:
                        act.wait_ge(hid_turned, it + 1)
                        act.wait_ge(unit_used, it * UNITS + UNITS)
                        upper_turned(hidT, hidT_hi)
                    if u in (19, 20):
                        q = u - 19
                        act.wait_ge(hid_ready, it * 2 + (q + 1))
                        sigmoid(it + 1, q)
                    if u == 21:
                        act.wait_ge(xs_turned, it + 3)
                        act.wait_ge(unit_used, it * UNITS + (UNITS + GU_UNITS))
                        upper_turned(xsT, xsT_hi)
            for u in range(GU_UNITS, UNITS):
                if u == GU_UNITS + 2:
                    outputs_out(trip)
                    act.wait_ge(hid_turned, trip + 1)
                    upper_turned(hidT, hidT_hi)
                upper(trip, u, GU_UNITS)
            act.wait_ge(unit_used, through(BY_ALL, trip, UNITS - 1, GU_UNITS))
            act.wait_ge(y_out, trip * 16 + 32)
            for c in range(2):
                ins = act.activation(ys[:, 512 * c:512 * (c + 1)], banks[4 + c][0:SLOTS, :], ACT.Copy)
            ins.then_inc(ys_ready, 1)
            for i in range(NT):
                act.wait_ge(final_sum, TOPK * (i + 1))
                if i >= 1:
                    act.wait_ge(final_sq, i)
                act.activation(final_junk, res[:, i, :], ACT.Square, accum_out=ss[:, i:i + 1]).then_inc(final_sq, 1)
                act.wait_ge(final_sq, i + 1)
                act.activation(rs[:, i:i + 1], ss[:, i:i + 1], ACT.Sqrt, scale=1.0 / D, bias=eps_t[:, :]).then_inc(final_rt, 1)

        @block.vector
        def _(v):
            v.memset(eps_t[:, :], EPS)
            v.memset(ss[:, :], 1.0).then_inc(eps_ready, 1)
            v.wait_ge(rms_act, 1)
            v.reciprocal(rs[:, 0:5], rs[:, 0:5]).then_inc(sq_dve, 1)
            v.wait_ge(sq_dve, 1)

            def scale_rows(n):
                src = meta_rows if n == 0 else res[:, n - 1, :]
                rows = META if n == 0 else P
                if n >= 2:
                    v.wait_ge(xn_turned, n - 1)
                v.tensor_scalar(xn[n % 2][0:rows, :], src, rs[0:rows, n:n + 1], None, ALU.mult).then_inc(xn_ready, 1)

            def gain_rows(n):
                lo, rows = (0, META) if n == 0 else (META + (n - 1) * P, P)
                v.wait_ge(xn_turned, n + 1)
                for c in range(4, 8):
                    ins = v.tensor_scalar(hT[:, c, lo:lo + rows], banks[2 * (n % 2) + 1][:, (c - 4) * P:(c - 4) * P + rows],
                                          vecT[:, G_MIX + c:G_MIX + c + 1], None, ALU.mult)
                ins.then_inc(hT_dve, 1)

            scale_rows(0)
            v.wait_ge(vec_turned, 1)
            v.tensor_copy(vecT[:, :], banks[4][:, 0:32]).then_inc(vec_ready, 1)
            v.wait_ge(vec_ready, 1)
            for n in range(NT + 1):
                if n < NT:
                    scale_rows(n + 1)
                gain_rows(n)

            v.memset(bgu[2 * E:P, :].bitcast(F32), 0.0)
            v.wait_ge(bgu_hi, 1)
            v.tensor_tensor(bgu[E:2 * E, :], bgu_rows[E:2 * E, :], bgu[E:2 * E, :].bitcast(F32), ALU.subtract).then_inc(bgu_ready, 1)
            v.wait_ge(bgu_ready, 1)
            v.wait_ge(slots_ready, 1)
            v.wait_ge(rows_ready, 1)
            def vec(col):
                return vecT[:, col:col + 1]

            steps = [0]

            def conv(ins):
                steps[0] += 1
                ins.then_inc(conv_step, 1)

            for n, (kind, c, h) in enumerate(jobs):
                b = banks[n % PROJ_BANKS]
                if kind == "cb" and c == 0:
                    evac_wait(v, n - 1)
                    for m in range(NC_):
                        o = mixT[:, NC_ + m, :]
                        conv(v.tensor_scalar(o, uT[:, m, 0:T], vec(CONV_W + m), vec(CONV_B + m), ALU.mult, ALU.add))
                    for tap in (1, 2):
                        for m in range(NC_):
                            o = mixT[:, NC_ + m, :]
                            v.wait_ge(conv_step, (tap - 1) * NC_ + m + 1)
                            conv(v.scalar_tensor_tensor(out=o, in0=uT[:, m, tap:tap + T], scalar=vec(CONV_W + 4 * tap + m),
                                                        in1=o, op0=ALU.mult, op1=ALU.add))
                if evac_by_act(n):
                    continue
                v.wait_ge(proj_done, n + 1)
                if kind == "k":
                    ins = v.tensor_copy(kT[:, c, h * HALF_K:(h + 1) * HALF_K], b[:, 0:HALF_K])
                elif kind == "q":
                    ins = v.tensor_scalar(qT[:, c, :], b[:, :], HD ** -0.5, None, ALU.mult)
                elif kind == "v":
                    rows = META if c == 0 else P
                    ins = v.tensor_copy(vN[0:rows, c, :], b[0:rows, :])
                elif kind == "cx":
                    if c >= 1:
                        evac_wait(v, jobs.index(("cc", c - 1, 1)))
                    ins = v.tensor_copy(cxT[:, h * HALF_U:(h + 1) * HALF_U], b[:, 0:HALF_U])
                elif kind == "cc":
                    evac_wait(v, jobs.index(("cx", c, h)))
                    ins = v.tensor_tensor(uT[:, c, h * HALF_U:(h + 1) * HALF_U], b[:, 0:HALF_U], cxT[:, h * HALF_U:(h + 1) * HALF_U], ALU.mult)
                else:
                    o = mixT[:, NC_ + c, :]
                    v.wait_ge(conv_step, 2 * NC_ + c + 1)
                    ins = v.tensor_tensor(o, b[:, :], o, ALU.mult)
                ins.then_inc(proj_dve, 1)

            def width_norm(part):
                v.wait_ge(nroot, part + 1)
                v.reciprocal(rstd[1], rstd[0]).then_inc(conv_step, 1)
                steps[0] += 1
                v.wait_ge(conv_step, steps[0])
                for c in range(NC_):
                    o = mixT[:, c + (0 if part else NC_), :]
                    g = vec((G_ATT if part else G_CONV) + c)
                    v.scalar_tensor_tensor(out=o, in0=o, scalar=g, in1=rstd[1], op0=ALU.mult, op1=ALU.mult).then_inc(nscaled, 1)

            width_norm(0)
            v.wait_ge(nscaled, NC_)
            v.wait_ge(masks_ready, 3)
            for s in range(NI + 1):
                if s < NI:
                    h, b = att_items[s]
                    t0, keys = span(b)
                    v.wait_ge(z_done, s + 1)
                    if s >= NA:
                        v.wait_ge(sp_done, s - NA + 1)
                    v.tensor_scalar(za[s % NA][0:keys, 0:T - t0].bitcast(I32), banks[s % LB][0:keys, 0:T - t0].bitcast(I32),
                                    0x7FFFFFFF, None, ALU.bitwise_and).then_inc(abs_done, 1)
                if s >= 1:
                    i = s - 1
                    h, b = att_items[i]
                    t0, keys = span(b)
                    v.wait_ge(ln_done, i + 1)
                    if i >= NSP:
                        v.wait_ge(logw_done, i - NSP + 1)
                        v.wait_ge(later_done, masks_before[i - NSP + 1])
                    v.scalar_tensor_tensor(out=sp[i % NSP][0:keys, 0:T - t0], in0=banks[i % LB][0:keys, 0:T - t0], scalar=0.0,
                                           in1=za[i % NA][0:keys, 0:T - t0], op0=ALU.max, op1=ALU.add).then_inc(sp_done, 1)
                    if b >= 0:
                        v.wait_ge(sp_done, i + 1)
                        v.tensor_tensor(sp[i % NSP][:, 0:P], sp[i % NSP][:, 0:P], causal, ALU.mult).then_inc(masked, 1)
                if s >= 15 and (s - 15) % 10 == 0 and s < NI:
                    c = (s - 15) // 10
                    v.wait_ge(av_done, 10 * (c + 1))
                    v.tensor_copy(mixT[:, c, :], banks[LB + c % 2][:, :]).then_inc(att_copied, 1)
            v.wait_ge(av_done, NI)
            v.tensor_copy(mixT[:, NC_ - 1, :], banks[LB + (NC_ - 1) % 2][:, :]).then_inc(att_copied, 1)
            v.wait_ge(att_copied, NC_)
            width_norm(1)
            at_ = LATE

            def late(*shape, dt=None):
                nonlocal at_
                n = 1
                for q in shape:
                    n *= q
                r = view(ring, at_, *shape)
                at_ += n
                return r

            v.wait_ge(late_in, 64)
            for i in range(NT):
                for n in range(2):
                    v.wait_ge(outp, 2 * i + n + 1)
                    o = res[:, i, n * 512:(n + 1) * 512]
                    v.tensor_tensor(o, banks[(2 * i + n) % 4][:, :], o, ALU.add).then_inc(res_added, 1)
                if i >= 1:
                    v.wait_ge(logit_done, i)
                    v.tensor_tensor(logits[:, i - 1, :], banks[6][:, 0:E], b_router_b, ALU.add).then_inc(route, 1)
                v.wait_ge(row_root, i + 1)
                v.reciprocal(rs[:, i:i + 1], rs[:, i:i + 1]).then_inc(row_var, 1)
                v.wait_ge(row_var, i + 1)
                v.wait_ge(res_added, 2 * (i + 1))
                v.scalar_tensor_tensor(out=rows2[i % 2], in0=res[:, i, :], scalar=rs[:, i:i + 1], in1=g_ffn_b,
                                       op0=ALU.mult, op1=ALU.mult).then_inc(row_ready, 1)
            v.wait_ge(logit_done, NT)
            v.tensor_tensor(logits[:, NT - 1, :], banks[6][:, 0:E], b_router_b, ALU.add).then_inc(route, 1)
            v.wait_ge(route, NT)
            chain = [NT]

            def step(ins):
                chain[0] += 1
                ins.then_inc(route, 1)
                v.wait_ge(route, chain[0])

            for i in range(NT):
                v.max(top[:, i, :], logits[:, i, :]).then_inc(route, 1)
            chain[0] += NT
            v.wait_ge(route, chain[0])
            for i in range(NT):
                v.max_index(top_e[:, i, :], top[:, i, :], logits[:, i, :]).then_inc(route, 1)
            chain[0] += NT
            v.wait_ge(route, chain[0])
            v.tensor_tensor(gates[:, :, :], top[:, :, 0:TOPK], top[:, :, 0:1].to_broadcast([P, NT, TOPK]), ALU.subtract).then_inc(gate_exp, 1)
            chosen = late(NT, 8)
            step(v.tensor_copy(chosen, top_e[:, :, :]))
            e_no = late(E)
            v.wait_ge(slots_ready, 1)
            step(v.tensor_copy(e_no, slot_no[:, 0:E]))
            picks = [late(NT, E) for _ in range(TOPK)]
            e_all = e_no.rearrange("p (a e) -> p a e", a=1).to_broadcast([P, NT, E])
            for k in range(TOPK):
                ins = v.tensor_tensor(picks[k], e_all, chosen[:, :, k:k + 1].to_broadcast([P, NT, E]), ALU.is_equal)
                ins.then_inc(route, 1)
            chain[0] += TOPK
            v.wait_ge(route, chain[0])
            mask = late(NT, E)
            step(v.tensor_tensor(mask, picks[0], picks[1], ALU.add))
            step(v.tensor_tensor(mask, mask, picks[2], ALU.add))
            step(v.tensor_tensor(mask, mask, picks[3], ALU.add))
            v.tensor_copy(onehot[:, :, 0:E], mask).then_inc(mask_ready, 1)
            step(v.scalar_tensor_tensor(out=choice[:, :, :], in0=picks[2], scalar=2.0, in1=picks[1], op0=ALU.mult, op1=ALU.add))
            step(v.scalar_tensor_tensor(out=choice[:, :, :], in0=picks[3], scalar=3.0, in1=choice[:, :, :], op0=ALU.mult, op1=ALU.add))
            v.wait_ge(pos_done, 1)
            step(v.scalar_tensor_tensor(out=place[:, :, :], in0=banks[7][:, 0:NT * E].rearrange("p (a e) -> p a e", e=E), scalar=4096.0,
                                        in1=mask, op0=ALU.add, op1=ALU.mult))
            step(v.tensor_scalar(place[:, :, :], place[:, :, :], -4096.0, None, ALU.add))
            counts, extra, cum, one_e = late(E), late(E), late(E), late(E)
            step(v.tensor_copy(counts, banks[7][:, NT * E:(NT + 1) * E]))
            step(v.memset(one_e, 1.0))
            step(v.tensor_scalar(extra, counts, float(SLOTS), None, ALU.is_gt))
            for b in range(2, BLOCKS):
                step(v.scalar_tensor_tensor(out=extra, in0=counts, scalar=float(SLOTS * b), in1=extra, op0=ALU.is_gt, op1=ALU.add))
            step(v.tensor_tensor_scan(cum, one_e, extra, 0.0, ALU.mult, ALU.add))
            done = view(ring, LATE_AT, KEYS, E)
            key_e, key_b, key_end, key_no = late(KEYS), late(KEYS), late(KEYS), late(KEYS)
            step(v.tensor_copy(key_no, slot_no[:, 0:KEYS]))
            step(v.tensor_tensor(done, cum.rearrange("p (a e) -> p a e", a=1).to_broadcast([P, KEYS, E]),
                                 key_no.rearrange("p (k a) -> p k a", a=1).to_broadcast([P, KEYS, E]), ALU.is_le))
            step(v.tensor_reduce(key_e, done, AX.X, ALU.add))
            step(v.tensor_tensor(done, done, extra.rearrange("p (a e) -> p a e", a=1).to_broadcast([P, KEYS, E]), ALU.mult))
            step(v.tensor_reduce(key_b, done, AX.X, ALU.add))
            step(v.tensor_scalar(key_end, key_e, float(E), None, ALU.is_equal))
            step(v.tensor_tensor(key_b, key_no, key_b, ALU.subtract))
            step(v.scalar_tensor_tensor(out=key_b, in0=key_end, scalar=float(BLOCKS), in1=key_b, op0=ALU.mult, op1=ALU.add))
            step(v.memset(shift[:, 0:E], 0.0))
            step(v.tensor_scalar(shift[:, E:ITEMS], key_b[:, 0:ITEMS - E], 1.0, -float(SLOTS), ALU.add, ALU.mult))
            step(v.tensor_scalar(key_e, key_e, float(E - 1), None, ALU.min))
            step(v.tensor_copy(item_all[:, 0:E], slot_no[:, 0:E]))
            step(v.tensor_copy(item_all[:, E:ITEMS], key_e[:, 0:ITEMS - E]))
            step(v.tensor_copy(item_e[:, 0:E], slot_no[0:1, 0:E]))
            v.tensor_copy(item_e[:, E:ITEMS], key_e[0:1, 0:ITEMS - E]).then_inc(table_ready, 1)
            v.tensor_scalar(trips[:, 0:1], cum[0:1, E - 1:E], float(E - 1), None, ALU.add).then_inc(table_ready, 1)
            gsum = late(NT)
            v.wait_ge(gate_exp, 2)
            step(v.tensor_reduce(gsum, gates[:, :, :], AX.X, ALU.add))
            step(v.reciprocal(gsum, gsum))
            step(v.tensor_tensor(gates[:, :, :], gates[:, :, :], gsum.rearrange("p (a b) -> p a b", b=1).to_broadcast([P, NT, TOPK]), ALU.mult))
            for k in range(TOPK):
                v.tensor_tensor(picks[k], picks[k], gates[:, :, k:k + 1].to_broadcast([P, NT, E]), ALU.mult).then_inc(route, 1)
            chain[0] += TOPK
            v.wait_ge(route, chain[0])
            v.wait_ge(logit_done, NT)
            step(v.tensor_tensor(mask, picks[0], picks[1], ALU.add))
            step(v.tensor_tensor(mask, mask, picks[2], ALU.add))
            dense = rowsT[0][:, 0:NT, 0:E]
            v.tensor_tensor(dense, mask, picks[3], ALU.add).then_inc(mask_ready, 1)
            v.wait_ge(dense_turned, 1)
            v.tensor_copy(rowsT[1][0:E, 0:NT, :], banks[6][0:E, :].rearrange("p (a b) -> p a b", b=P)).then_inc(dense_ready, 1)
            for m in range(2 * NT):
                v.wait_ge(bias_done, m + 1)
                o = res[:, m // 2, (m % 2) * 512:(m % 2 + 1) * 512]
                v.tensor_tensor(o, banks[m % 4][:, :], o, ALU.add).then_inc(base_ready, 1)
            assert at_ <= RING

            def prepare(n, number):
                e = v.value_load(item_e[0:1, number], min_val=0, max_val=E - 1)
                if not isinstance(n, int) or n > 0:
                    v.wait_ge(idx_summed, n)
                v.tensor_copy(ids[:, :, 3:4], choice[:, :, bass.ds(e, 1)]).then_inc(prep_step, 1)
                v.tensor_scalar(sel[:, :], item_all[:, number].to_broadcast([P, SLOTS]), bgu_row[:, 0:1], None, ALU.is_equal).then_inc(sel_ready, 1)
                v.tensor_scalar(place_i[:, :].rearrange("p (a b) -> p a b", b=1), place[:, :, bass.ds(e, 1)], shift[:, number], None, ALU.add).then_inc(prep_step, 1)
                v.wait_ge(prep_step, n * 2 + 2)
                v.tensor_tensor(onehot[:, :, :], slot_no[:, :].rearrange("p (a s) -> p a s", a=1).to_broadcast([P, NT, SLOTS]),
                                place_i[:, :].rearrange("p (a b) -> p a b", b=1).to_broadcast([P, NT, SLOTS]), ALU.is_equal).then_inc(onehot_ready, 1)

            def indices(n, column):
                v.wait_ge(idx_summed, n + 1)
                v.tensor_copy(slot_f[:, :], banks[7][0:SLOTS, 504:508]).then_inc(idx_copied, 1)
                v.wait_ge(idx_copied, n + 1)
                v.tensor_scalar(slot_g[:, 0:1], slot_f[:, 2:3], -SKIP, SKIP, ALU.mult, ALU.add).then_inc(idx_step, 1)
                v.wait_ge(idx_step, n * 3 + 1)
                v.scalar_tensor_tensor(out=slot_g[:, 1:2], in0=slot_f[:, 0:1], scalar=slot_f[:, 1:2], in1=slot_g[:, 0:1], op0=ALU.add, op1=ALU.add).then_inc(idx_step, 1)
                v.wait_ge(idx_step, n * 3 + 2)
                v.tensor_tensor(row_tab[:, column], slot_g[:, 1:2], slot_f[:, 3:4], ALU.add).then_inc(idx_step, 1)
                if not isinstance(n, int) or n > 0:
                    v.wait_ge(xs_in, n * 16)
                v.tensor_scalar(tok_idx[:, :], slot_g[:, 1:2], 0.25, None, ALU.mult).then_inc(idx_ready, 1)

            def lower(it, u, skip=0):
                if u < GU_UNITS:
                    v.wait_ge(gu_in[u // 2], 16 if it is None else it * 16 + 32)
                    src = gu_pair[u // 2][:, u % 2, :]
                else:
                    v.wait_ge(dn_in[(u - GU_UNITS) // 2], it * 16 + 16)
                    src = dn_pair[(u - GU_UNITS) // 2][:, u % 2, :]
                v.wait_ge(hi_done, through(BY_ALL, it, u, skip))
                v.tensor_tensor(stage[:, u % STAGES, 1, :], src, stage[:, u % STAGES, 0, :].bitcast(F32), ALU.subtract).then_inc(lo_dve, step_of(BY_DVE, it, u))

            def lower_turned(dst, upper_done, n, done):
                v.wait_ge(upper_done, n + 1)
                for c in range(2):
                    ins = v.tensor_tensor(dst[:, 1, 4 * c:4 * c + 4, :], banks[6 + c][:, 0:4 * SLOTS].rearrange("p (a b) -> p a b", b=SLOTS),
                                          dst[:, 0, 4 * c:4 * c + 4, :].bitcast(F32), ALU.subtract)
                ins.then_inc(done, 1)

            def half(t, q):
                return t[:, q * 512:(q + 1) * 512]

            def read_gate_and_up(n, used, q):
                v.wait_ge(unit_used, used)
                if not isinstance(n, int):
                    v.wait_ge(hid_ready, n * 2)
                v.tensor_scalar(half(gate_t, q), banks[q][0:SLOTS, :], LIMIT, None, ALU.min).then_inc(gate_ready, 1)
                v.tensor_scalar(half(lin_t, q), banks[2 + q][0:SLOTS, :], LIMIT, -LIMIT, ALU.min, ALU.max).then_inc(glu_read, 1)

            def glu(n, q):
                v.wait_ge(gate_ready, n * 2 + (q + 1))
                v.wait_ge(glu_read, n * 2 + (q + 1))
                v.scalar_tensor_tensor(out=half(lin_t, q), in0=half(lin_t, q), scalar=1.0, in1=half(gate_t, q), op0=ALU.add, op1=ALU.mult).then_inc(glu_part, 1)

            def hidden(n, q):
                v.wait_ge(glu_part, n * 2 + (q + 1))
                v.wait_ge(sig_done, n * 2 + (q + 1))
                if not isinstance(n, int):
                    v.wait_ge(hid_turned, n)
                v.tensor_tensor(half(hid, q), half(lin_t, q), half(sig_t, q), ALU.mult).then_inc(hid_ready, 1)

            v.memset(row_idx[:, :], int(SKIP)).then_inc(bufs_clear, 1)
            v.memset(row_tab[:, 0:1], int(SKIP)).then_inc(bufs_clear, 1)
            v.memset(ys, 0.0).then_inc(bufs_clear, 1)
            v.memset(xs, 0.0).then_inc(bufs_clear, 1)
            v.wait_ge(table_ready, 2)
            prepare(0, slice(0, 1))
            indices(0, slice(1, 2))
            lower_turned(xsT, xsT_hi, 0, xsT_lo)
            for u in range(GU_UNITS):
                if u in BY_DVE:
                    lower(None, u)
                if u == 4:
                    v.wait_ge(unit_used, 1)
                    prepare(1, slice(1, 2))
                if u == 12:
                    indices(1, slice(2, 3))
            for q in range(2):
                read_gate_and_up(0, GU_UNITS, q)
            for q in range(2):
                glu(0, q)
            for q in range(2):
                hidden(0, q)
            lower_turned(xsT, xsT_hi, 1, xsT_lo)
            trip = v.value_load(trips[0:1, 0:1], min_val=E - 1, max_val=E - 1 + EXTRA)
            with v.Fori(0, trip) as it:
                for u in range(UNITS):
                    if u in BY_DVE:
                        lower(it, u)
                    if u == 1:
                        v.wait_ge(y_out, it * 16 + 16)
                        v.wait_ge(idx_step, it * 3 + 3)
                        v.wait_ge(bufs_clear, 4)
                        v.tensor_copy(row_idx[:, :], row_tab[:, bass.ds(it, 1)]).then_inc(row_moved, 1)
                    if u == 4:
                        v.wait_ge(unit_used, it * UNITS + (UNITS + 1))
                        prepare(it + 2, bass.ds(it + 2, 1))
                    if u == 8:
                        lower_turned(hidT, hidT_hi, it, hidT_lo)
                    if u == 13:
                        indices(it + 2, bass.ds(it + 3, 1))
                    if u == 19:
                        for q in range(2):
                            read_gate_and_up(it + 1, it * UNITS + (UNITS + GU_UNITS), q)
                        for q in range(2):
                            glu(it + 1, q)
                    if u == 21:
                        for q in range(2):
                            hidden(it + 1, q)
                        lower_turned(xsT, xsT_hi, it + 2, xsT_lo)
            v.wait_ge(y_out, trip * 16 + 16)
            v.wait_ge(idx_step, trip * 3 + 3)
            v.tensor_copy(row_idx[:, :], row_tab[:, bass.ds(trip, 1)]).then_inc(row_moved, 1)
            lower_turned(hidT, hidT_hi, trip, hidT_lo)
            for u in range(GU_UNITS, UNITS):
                if u in BY_DVE:
                    lower(trip, u, GU_UNITS)
            v.wait_ge(y_out, trip * 16 + 32)
            v.tensor_copy(row_idx[:, :], row_tab[:, bass.ds(trip + 1, 1)]).then_inc(row_moved, 1)
            def combine(i):
                v.wait_ge(picked_in[i], 16)
                for k in range(TOPK):
                    if k:
                        v.wait_ge(final_sum, TOPK * i + k)
                    v.scalar_tensor_tensor(out=res[:, i, :], in0=picked[i][:, k, :], scalar=gates[:, i, k:k + 1], in1=res[:, i, :],
                                           op0=ALU.mult, op1=ALU.add).then_inc(final_sum, 1)

            def finish(i):
                v.wait_ge(final_rt, i + 1)
                v.reciprocal(rs[:, i:i + 1], rs[:, i:i + 1]).then_inc(final_step, 1)
                v.wait_ge(final_step, i + 1)
                v.scalar_tensor_tensor(out=final_rows[i], in0=res[:, i, :], scalar=rs[:, i:i + 1], in1=g_final_b,
                                       op0=ALU.mult, op1=ALU.mult).then_inc(final_ready, 1)

            v.wait_ge(final_in, 16)
            for i in range(NT):
                combine(i)
                if i >= 1:
                    finish(i - 1)
            finish(NT - 1)

        @block.gpsimd
        def _(g):
            steps = [0]

            def step(ins):
                steps[0] += 1
                ins.then_inc(const_step, 1)
                g.wait_ge(const_step, steps[0])

            def triangle(t, compare, base, fill):
                return g.affine_select(out=t, in_=t, compare_op=compare, fill=fill, base=base, pattern=[[1, P]], channel_multiplier=-1)

            step(g.memset(ident[:, :], 0.0))
            triangle(ident[:, :], ALU.not_equal, 0, 1.0).then_inc(ident_ready, 1)
            g.memset(ones[:, :], 1.0).then_inc(ones_ready, 1)
            step(g.memset(ones_h[:, :], 1.0))
            step(g.memset(before[:, :], 1.0))
            step(triangle(before[:, :], ALU.is_gt, 0, 0.0))
            step(g.iota(slot_int, pattern=[[1, SLOTS]], base=0, channel_multiplier=0))
            step(g.tensor_copy(slot_no[:, :], slot_int))
            step(g.memset(ids[:, :, :], 1.0))
            step(g.iota(slot_int[:, 0:NT], pattern=[[0, NT]], base=0, channel_multiplier=TOPK))
            step(g.tensor_copy(ids[:, :, 0:1], slot_int[:, 0:NT].rearrange("p (a b) -> p a b", b=1)))
            step(g.iota(slot_int[:, 0:NT], pattern=[[TOPK * P, NT]], base=0, channel_multiplier=0))
            g.tensor_copy(ids[:, :, 1:2], slot_int[:, 0:NT].rearrange("p (a b) -> p a b", b=1)).then_inc(slots_ready, 1)
            row_no = slot_int[:, 8:9]
            step(g.iota(row_no, pattern=[[0, 1]], base=0, channel_multiplier=1))
            step(g.tensor_copy(bgu_row[:, :], row_no))
            step(g.tensor_scalar(bgu_past, bgu_row[:, :], float(E), -float(E), ALU.is_ge, ALU.mult))
            g.tensor_tensor(bgu_row[:, :], bgu_row[:, :], bgu_past, ALU.add).then_inc(rows_ready, 1)
            step(g.memset(neg_tri, -1.0))
            g.affine_select(out=neg_tri, in_=neg_tri, compare_op=ALU.is_ge, fill=0.0, base=0, pattern=[[-1, P]], channel_multiplier=1).then_inc(masks_ready, 1)
            g.memset(neg_one, -1.0).then_inc(masks_ready, 1)
            step(g.memset(causal, 1.0))
            triangle(causal, ALU.is_gt, 0, 0.0).then_inc(masks_ready, 1)
            g.wait_ge(nscaled, NC_)
            g.wait_ge(masks_ready, 3)
            for s in range(NI + 2):
                if s < NI:
                    h, b = att_items[s]
                    t0, keys = span(b)
                    acc = later[h % 2]
                    if b >= 0:
                        g.wait_ge(masked, masks_before[s + 1])
                        if b == 3:
                            if s >= 2:
                                g.wait_ge(logw_done, s - 1)
                            g.memset(acc[:, 0:t0], 0.0)
                            g.tensor_copy(acc[:, t0:T], sp[s % NSP][:, 0:T - t0]).then_inc(later_done, 1)
                        else:
                            g.wait_ge(logw_done, s + 1)
                            g.wait_ge(later_done, masks_before[s - 1])
                            g.tensor_tensor(acc[:, t0:T], acc[:, t0:T], sp[s % NSP][:, 0:T - t0], ALU.add).then_inc(later_done, 1)
                if s >= 2:
                    i = s - 2
                    if att_items[i][1] >= 0:
                        g.wait_ge(w_done, i + 1)
                        w = wT[i % NW][:, 0:P]
                        g.affine_select(out=w, in_=w, compare_op=ALU.is_gt, fill=0.0, base=0, pattern=[[1, P]], channel_multiplier=-1).then_inc(w_masked, 1)

            last_token, last_row = g.to_reg(T - 1), g.to_reg(T * TOPK - 1)

            def gather(turned, ready):
                g.wait_ge(bufs_clear, 4)
                g.wait_ge(idx_ready, ready)
                g.wait_ge(xs_turned, turned)
                g.indirect_dma_start(xs, None, ffn_rows, bass.IndirectOffsetOnAxis(ap=tok_idx[:, 0:1], axis=0),
                                     bounds_check=last_token, oob_is_err=False).then_inc(xs_in, 16)

            def scatter(ready):
                g.wait_ge(bufs_clear, 4)
                g.wait_ge(ys_ready, ready)
                g.wait_ge(row_moved, ready)
                g.indirect_dma_start(choice_rows, bass.IndirectOffsetOnAxis(ap=row_idx[:, 0:1], axis=0), ys, None,
                                     bounds_check=last_row, oob_is_err=False).then_inc(y_out, 16)

            def lower(it, u, skip=0):
                if u < GU_UNITS:
                    g.wait_ge(gu_in[u // 2], 16 if it is None else it * 16 + 32)
                    src = gu_pair[u // 2][:, u % 2, :]
                else:
                    g.wait_ge(dn_in[(u - GU_UNITS) // 2], it * 16 + 16)
                    src = dn_pair[(u - GU_UNITS) // 2][:, u % 2, :]
                g.wait_ge(hi_done, through(BY_ALL, it, u, skip))
                g.tensor_tensor(stage[:, u % STAGES, 1, :], src, stage[:, u % STAGES, 0, :].bitcast(F32), ALU.subtract).then_inc(lo_pool, step_of(BY_POOL, it, u))

            one, two, three = (g.alloc_register(n) for n in ("one_more", "two_more", "three_more"))
            g.wait_ge(bufs_clear, 4)
            for i in range(NT):
                g.wait_ge(row_stored[i], 16)
            g.wait_ge(table_ready, 2)
            g.wait_ge(idx_ready, 1)
            g.indirect_dma_start(xs, None, ffn_rows, bass.IndirectOffsetOnAxis(ap=tok_idx[:, 0:1], axis=0),
                                 bounds_check=last_token, oob_is_err=False).then_inc(xs_in, 16)
            g.indirect_dma_start(choice_rows, bass.IndirectOffsetOnAxis(ap=row_idx[:, 0:1], axis=0), ys, None,
                                 bounds_check=last_row, oob_is_err=False).then_inc(y_out, 16)
            for u in BY_POOL:
                if u < GU_UNITS:
                    lower(None, u)
                if u == 11:
                    gather(1, 2)
            trip = g.value_load(trips[0:1, 0:1], min_val=E - 1, max_val=E - 1 + EXTRA)
            g.reg_mov(one, 1)
            g.reg_mov(two, 2)
            g.reg_mov(three, 3)
            with g.Fori(0, trip) as it:
                for u in BY_POOL:
                    lower(it, u)
                    if u == 7:
                        scatter(one)
                    if u == 11:
                        gather(two, three)
                g.reg_add(one, one, 1)
                g.reg_add(two, two, 1)
                g.reg_add(three, three, 1)
            scatter(one)
            for u in BY_POOL:
                if u >= GU_UNITS:
                    lower(trip, u, GU_UNITS)
            scatter(two)


_INS = ['x', 'meta_tokens', 'g_mix', 'w_in', 'g_attn_out', 'conv_w', 'conv_b', 'g_conv_out', 'w_out', 'g_ffn',
        'w_router', 'b_router', 'w_gu', 'b_gu', 'w_down', 'b_down', 'g_final']


def kernel(**inputs):
    import numpy as _np
    import concourse.bacc as _bacc
    from concourse import mybir as _mybir
    from concourse.bass_utils import run_bass_kernel_spmd as _run

    nc = _bacc.Bacc("TRN2", target_bir_lowering=False, num_devices=1)
    arrays, args = {}, []
    for name in _INS:
        a = _np.ascontiguousarray(inputs[name])
        arrays[f"in_{name}_dram"] = a
        args.append(nc.dram_tensor(f"in_{name}_dram", a.shape, _mybir.dt.from_np(a.dtype), kind="ExternalInput").ap())
    args.append(nc.dram_tensor("out_dram", (1, T, D), F32, kind="ExternalOutput").ap())
    build(nc, *args)
    r = _run(nc, [arrays], core_ids=[0])
    return r.results[0]["out_dram"]
```

```python
from contextlib import ExitStack

import concourse.bass as bass
from concourse import mybir

F32 = mybir.dt.float32
F32R = mybir.dt.float32r
BF16 = mybir.dt.bfloat16
I32 = mybir.dt.int32
U32 = mybir.dt.uint32
ALU = mybir.AluOpType
ACT = mybir.ActivationFunctionType
AX = mybir.AxisListType

P = 128
D = 1024
KD = D // P
T = 512
NT = T // P
META = 16
TM = META + T
AW = 512
HEADS, HD = 8, 64
CW = 512
NC_ = AW // P
TAPS = 3
UT = T + TAPS - 1
E, TOPK = 32, 4
FF = 1024
NF = FF // P
EPS = 1e-6
LIMIT, ALPHA = 7.0, 1.702

SLOTS = 96
BLOCKS = -(-T // SLOTS)
EXTRA = T * TOPK // SLOTS
ITEMS = E + EXTRA + 3
KEYS = 24
assert EXTRA + 3 <= KEYS
SKIP = float(1 << 20)

GU_UNITS = 2 * KD
UNITS = GU_UNITS + NF
BY_ALL = range(UNITS)
BY_POOL = (3, 7, 11, 15, 20, 22)
BY_DVE = tuple(u for u in BY_ALL if u not in BY_POOL)
TURN_AFTER = 3
STAGES = 4
assert GU_UNITS % STAGES == 0 and UNITS % STAGES == 0


def through(by, it, u, skip=0):
    c = sum(1 for m in by if skip <= m <= u)
    return c if it is None else it * len(by) + (len(by) + c)


def free_again(it, u, skip=0):
    c = u - STAGES + 1 - skip
    if it is None:
        return c if c > 0 else None
    return it * UNITS + (UNITS + c)


def step_of(by, it, u):
    mine = [m for m in by if m < GU_UNITS]
    return 1 + (len(by) - len(mine) if it is None and u == mine[-1] else 0)


def build(nc, x, meta_tokens, g_mix, w_in, g_attn_out, conv_w, conv_b, g_conv_out, w_out, g_ffn,
          w_router, b_router, w_gu, b_gu, w_down, b_down, g_final, out):
    with ExitStack() as ctx:
        def sb(name, shape, dt=F32):
            return ctx.enter_context(nc.sbuf_tensor(name, shape, dt))

        def sem(name):
            return ctx.enter_context(nc.semaphore(name))

        ffn_rows = nc.dram_tensor("ffn_rows", [T, D], F32, kind="Internal").ap()
        choice_rows = nc.dram_tensor("choice_rows", [T * TOPK, D], F32, kind="Internal").ap()

        WIN_SLOTS = 3
        GROUP = KD * 512
        TEMPS = 2 * GROUP
        ROWS_AT = WIN_SLOTS * GROUP
        MIX = ROWS_AT + 3 * D + P
        HEADS_AT = MIX + KD * TM
        PAIR = 2 * FF
        LATE_AT = 12 * PAIR
        RING = LATE_AT + 3450
        ring = sb("ring", [P, RING])
        MISC = KD * T + NC_ * UT
        misc = sb("misc", [P, MISC])
        res = sb("res", [P, NT, D])

        def view(t, start, *shape, rows=P):
            n = 1
            for s in shape:
                n *= s
            v = t[0:rows, start:start + n]
            if len(shape) == 2:
                v = v.rearrange("p (a b) -> p a b", b=shape[1])
            elif len(shape) == 3:
                v = v.rearrange("p (a b c) -> p a b c", b=shape[1], c=shape[2])
            return v

        gu_pair = [view(ring, (6 + g if g < 6 else g - 6) * PAIR, 2, FF) for g in range(KD)]
        dn_pair = [view(ring, (2 + g) * PAIR, 2, D) for g in range(NF // 2)]
        parts = sb("parts", [P, STAGES * 2 * FF + 4 * KD * SLOTS], F32R)
        stage = view(parts, 0, STAGES, 2, FF)

        win = [view(ring, slot * GROUP, KD, 512) for slot in (0, 1, 2, 0, 1, 0)]
        at = HEADS_AT
        qT = view(ring, at, NC_, T); at += NC_ * T
        kT = view(ring, at, NC_, TM); at += NC_ * TM
        vN = view(ring, at, NT + 1, AW); at += (NT + 1) * AW
        neg_tri = view(ring, at, P); at += P
        neg_one = view(ring, at, P); at += P
        causal = view(ring, at, P); at += P
        assert at <= RING
        at = TEMPS
        NA, NSP, NW = 2, 3, 3
        za = [view(ring, at + i * T, T) for i in range(NA)]; at += NA * T
        sp = [view(ring, at + i * T, T) for i in range(NSP)]; at += NSP * T
        wT = [view(ring, at + i * T, T) for i in range(NW)]; at += NW * T
        later = [view(ring, at + i * T, T) for i in range(2)]; at += 2 * T
        assert at <= ROWS_AT + D
        sq = [[view(ring, ROWS_AT + D + c * T, T) for c in range(NC_)], [za[0], za[1], sp[0], sp[1]]]
        root, rstd = [wT[0], sp[2]], [wT[1], wT[2]]
        at = TEMPS
        rows2 = [view(ring, at + i * D, D) for i in range(2)]; at += 2 * D
        rowsT = [view(ring, at + i * D, KD, P) for i in range(2)]; at += 2 * D
        assert at <= 6 * PAIR
        at = LATE_AT
        g_ffn_b = view(ring, at, D); at += D
        w_router_sb = view(ring, at, KD, E); at += KD * E
        b_router_b = view(ring, at, E); at += E
        dense = view(ring, at, NT, E); at += NT * E
        b_down_sb = view(ring, at, D, rows=E); at += D
        gates_T = view(ring, LATE_AT + KEYS * E, NT, P, rows=E)
        assert KEYS * E + NT * P <= D + KD * E
        LATE = at
        wo = view(ring, 0, KD, D)
        xn = [view(ring, ROWS_AT + i * D, D) for i in range(2)]
        squared = [view(ring, HEADS_AT + i * D, D) for i in range(2)]
        meta_rows = view(ring, ROWS_AT + 2 * D, D, rows=META)
        scaled = [view(ring, MIX + i * D, KD, P) for i in range(2)]
        hT = [view(parts, i * KD * TM, KD, TM) for i in range(2)]
        wpart = [[view(parts, 2 * KD * TM + (2 * i + half) * 512, 512) for half in range(2)] for i in range(2)]
        assert 2 * KD * TM + 2048 <= STAGES * 2 * FF + 4 * KD * SLOTS
        vec_rows = view(ring, ROWS_AT + 3 * D, P, rows=32)
        bgu_rows = view(misc, 0, 2 * FF, rows=2 * E)
        slot_int = misc[:, 2 * FF:2 * FF + SLOTS].bitcast(I32)
        mixT = view(misc, 0, KD, T)
        uT = view(misc, KD * T, NC_, UT)
        at = 0
        xs = view(misc, at, D, rows=SLOTS); at += D
        hid = view(misc, at, FF, rows=SLOTS); at += FF
        ys = view(misc, at, D, rows=SLOTS); at += D
        gate_t = view(misc, at, FF, rows=SLOTS); at += FF
        lin_t = view(misc, at, FF, rows=SLOTS); at += FF
        sig_t = view(misc, at, FF, rows=SLOTS); at += FF
        assert at <= MISC
        picked = [view(ring, i * TOPK * D, TOPK, D) for i in range(NT)]
        g_final_b = view(ring, NT * TOPK * D, D)
        final_junk = view(ring, (NT * TOPK + 1) * D, D)
        final_rows = [view(ring, (NT * TOPK + 2 + i) * D, D) for i in range(NT)]

        ident = sb("ident", [P, P])
        ones = sb("ones", [P, P])
        eps_t = sb("eps_t", [P, 1])
        before = sb("before", [P, P], BF16)
        ones_h = sb("ones_h", [P, P], BF16)
        vecT = sb("vecT", [P, 32])
        G_MIX, G_ATT, G_CONV, CONV_W, CONV_B = 0, 8, 12, 16, 28
        bgu = sb("bgu", [P, 2 * FF], F32R)
        bgu_row = sb("bgu_row", [P, 1])
        bgu_past = view(misc, 2 * FF + SLOTS, 1)
        sel = sb("sel", [P, SLOTS], F32R)
        xsT, hidT = (view(parts, STAGES * 2 * FF + i * 2 * KD * SLOTS, 2, KD, SLOTS) for i in range(2))
        ss = sb("ss", [P, 8])
        rs = sb("rs", [P, 8])
        logits = sb("logits", [P, NT, E])
        top = sb("top", [P, NT, 8])
        top_e = sb("top_e", [P, NT, 8], U32)
        gates = sb("gates", [P, NT, TOPK])
        place = sb("place", [P, NT, E])
        choice = sb("choice", [P, NT, E])
        shift = sb("shift", [P, ITEMS])
        item_e = sb("item_e", [1, ITEMS], I32)
        item_all = sb("item_all", [P, ITEMS])
        trips = sb("trips", [1, 2], I32)
        slot_no = sb("slot_no", [P, SLOTS])
        onehot = sb("onehot", [P, NT, SLOTS], BF16)
        place_i = sb("place_i", [P, NT])
        ids = sb("ids", [P, NT, 4], BF16)
        slot_f = sb("slot_f", [SLOTS, 4])
        slot_g = sb("slot_g", [SLOTS, 4])
        tok_idx = sb("tok_idx", [SLOTS, 1], U32)
        row_tab = sb("row_tab", [SLOTS, ITEMS + 1], U32)
        row_idx = sb("row_idx", [SLOTS, 1], U32)

        banks = [ctx.enter_context(nc.psum_tensor(f"bank{i}", [P, 512], F32)) for i in range(8)]

        x_in = [sem(f"x_in{i}") for i in range(NT + 1)]
        vec_in, bgu_in, late_in, wo_in = sem("vec_in"), sem("bgu_in"), sem("late_in"), sem("wo_in")
        win_in = [sem(f"win_in{g}") for g in range(6)]
        gu_in = [sem(f"gu_in{g}") for g in range(KD)]
        dn_in = [sem(f"dn_in{g}") for g in range(NF // 2)]
        rows_ready = sem("rows_ready")
        first_items = sem("first_items")
        hi_done, lo_dve, lo_pool, unit_used = sem("hi_done"), sem("lo_dve"), sem("lo_pool"), sem("unit_used")
        ident_ready, ones_ready, masks_ready, slots_ready, eps_ready = (
            sem("ident_ready"), sem("ones_ready"), sem("masks_ready"), sem("slots_ready"), sem("eps_ready"))
        const_step, glu_part, glu_read, row_moved, final_step = sem("const_step"), sem("glu_part"), sem("glu_read"), sem("row_moved"), sem("final_step")
        squares, sq_dve, rms_act = sem("squares"), sem("sq_dve"), sem("rms_act")
        xn_ready, xn_turned = sem("xn_ready"), sem("xn_turned")
        vec_turned, vec_ready, bgu_hi, bgu_ready = sem("vec_turned"), sem("vec_ready"), sem("bgu_hi"), sem("bgu_ready")
        w_hi, w_lo, w_used, proj_act, proj_dve = sem("w_hi"), sem("w_lo"), sem("w_used"), sem("proj_act"), sem("proj_dve")
        scaled_ready, hT_hi = sem("scaled_ready"), sem("hT_hi")
        hT_lo = [sem(f"hT_lo{i}") for i in range(2)]
        conv_step = sem("conv_step")
        z_done, abs_done, exp_done, ln_done, sp_done, masked = (sem("z_done"), sem("abs_done"), sem("exp_done"), sem("ln_done"), sem("sp_done"), sem("masked"))
        later_done, logw_done, w_done, w_masked, av_done, att_copied = (sem("later_done"), sem("logw_done"), sem("w_done"), sem("w_masked"), sem("av_done"), sem("att_copied"))
        nsq, nsum, nroot, nscaled = sem("nsq"), sem("nsum"), sem("nroot"), sem("nscaled")
        outp, res_added, row_sq, row_var, row_root, row_ready, row_turned, rowT_ready = (
            sem("outp"), sem("res_added"), sem("row_sq"), sem("row_var"), sem("row_root"), sem("row_ready"), sem("row_turned"), sem("rowT_ready"))
        row_stored = [sem(f"row_stored{i}") for i in range(NT)]
        logit_done, route, gate_exp, mask_ready, pos_done, dense_turned, dense_ready, bias_done, base_ready = (
            sem("logit_done"), sem("route"), sem("gate_exp"), sem("mask_ready"), sem("pos_done"), sem("dense_turned"), sem("dense_ready"), sem("bias_done"), sem("base_ready"))
        table_ready, bufs_clear = sem("table_ready"), sem("bufs_clear")
        onehot_ready, idx_summed, idx_copied, idx_step, idx_ready, prep_step = (
            sem("onehot_ready"), sem("idx_summed"), sem("idx_copied"), sem("idx_step"), sem("idx_ready"), sem("prep_step"))
        xs_in, xs_turned, xsT_hi, xsT_lo = sem("xs_in"), sem("xs_turned"), sem("xsT_hi"), sem("xsT_lo")
        hid_turned, hidT_hi, hidT_lo = sem("hid_turned"), sem("hidT_hi"), sem("hidT_lo")
        gate_ready, sig_done, hid_ready, sel_ready = (
            sem("gate_ready"), sem("sig_done"), sem("hid_ready"), sem("sel_ready"))
        ys_ready, y_out = sem("ys_ready"), sem("y_out")
        picked_in = [sem(f"picked_in{i}") for i in range(2 * NT)]
        final_in, final_sum, final_sq, final_rt, final_ready, stored = (
            sem("final_in"), sem("final_sum"), sem("final_sq"), sem("final_rt"), sem("final_ready"), sem("stored"))

        assert TM // 2 <= META + 2 * P
        HALF_K, HALF_U = TM // 2, UT // 2 + 1

        def cols_of(kind, h):
            if kind == "k":
                return h * HALF_K, HALF_K
            return (0, HALF_U) if h == 0 else (HALF_U, UT - HALF_U)

        jobs = [("k", c, h) for c in range(NC_) for h in range(2)]
        jobs += [("q", c, 0) for c in range(NC_)]
        jobs += [("v", m, 0) for m in range(NT + 1)]
        HEAD_JOBS = len(jobs)
        jobs += [(kind, c, h) for kind in ("cx", "cc") for c in range(NC_) for h in range(2)]
        jobs += [("cb", c, 0) for c in range(NC_)]
        GROUP_OF = {"q": 0, "k": 1, "v": 2, "cb": 3, "cc": 4, "cx": 5}
        LOADS = ["k", "q", "v", "cx", "cc", "cb"]
        SLOT_OF = {kind: n for n, kind in enumerate(LOADS)}
        HEAD_UNITS = [(kind, c, kh) for kind in ("k", "q") for c in range(NC_) for kh in range(2)] + [("v", k, 0) for k in range(KD)]
        CONV_UNITS = [(kind, c, kh) for kind in ("cx", "cc", "cb") for c in range(NC_) for kh in range(2)]
        w_units = HEAD_UNITS + CONV_UNITS

        def jobs_of(t):
            kind, c, _ = w_units[t]
            return [n for n, j in enumerate(jobs) if j[0] == kind and (kind == "v" or j[1] == c)]

        def last_unit(n):
            return max(t for t in range(len(w_units)) if n in jobs_of(t))

        def bank_no(n):
            kind, c, h = jobs[n]
            return {"k": 2 * (c % 2) + h, "q": 4 + c % 2, "v": (0, 1, 2, 3, 6)[c] if kind == "v" else 0,
                    "cx": 4 + h, "cc": 4 + h, "cb": 4 + c % 2}[kind]

        def bank_holder(n):
            return max([m for m in range(n) if bank_no(m) == bank_no(n)], default=None)

        def job_bank(n):
            return banks[bank_no(n)]

        def evac_by_act(n):
            return (n < HEAD_JOBS and n % 2 == 0) or jobs[n][0] == "cx"

        def evac_wait(eng, n):
            by = [evac_by_act(m) for m in range(n + 1)]
            if by[n]:
                eng.wait_ge(proj_act, sum(by))
            else:
                eng.wait_ge(proj_dve, n + 1 - sum(by))

        def last_job(kind):
            return max(n for n, j in enumerate(jobs) if j[0] == kind)

        att_items = [(2 * c + hh, b) for c in range(HEADS // 2) for b in (3, 2, 1, 0, -1) for hh in range(2)]
        NI = len(att_items)
        LB = 4
        OB = 6

        H0 = len(HEAD_UNITS)
        unit_at = {3 * (m // 2) + 1 + m % 2: H0 + m for m in range(len(CONV_UNITS))}
        SPLIT_EARLY = H0 + 2
        split_at = {step - 1: t for step, t in unit_at.items() if t >= SPLIT_EARLY}
        read_step = {}
        for step, t in unit_at.items():
            for n in jobs_of(t):
                read_step[n] = step + 1
        tap_step = {}
        for m in range(NC_):
            u_there = read_step[jobs.index(("cc", m, 1))]
            tap_step[u_there + 1] = [(0, m)]
            tap_step[u_there + 2] = [(1, m), (2, m)]
            assert u_there + 2 < read_step[jobs.index(("cb", m, 0))]
        assert max(read_step.values()) + 1 < NI

        def span(b):
            return (P * b, P) if b >= 0 else (0, META)

        masks_before = [sum(1 for h, b in att_items[:i] if b >= 0) for i in range(NI + 1)]

        block = ctx.enter_context(nc.Block())

        @block.sync
        def _(sp_):
            def load_gu(e, g):
                src = w_gu[0, e, g * P:(g + 1) * P, :] if isinstance(e, int) else \
                    w_gu[0, bass.ds(e, 1), g * P:(g + 1) * P, :].rearrange("o r f -> (o r) f")
                sp_.dma_start(gu_pair[g], src.rearrange("p (s f) -> p s f", s=2)).then_inc(gu_in[g], 16)

            def load_dn(e, g, place=None, landed=None):
                src = w_down[0, e, 2 * g * P:2 * (g + 1) * P, :] if isinstance(e, int) else \
                    w_down[0, bass.ds(e, 1), 2 * g * P:2 * (g + 1) * P, :].rearrange("o r d -> (o r) d")
                sp_.dma_start(dn_pair[g] if place is None else place, src.rearrange("(f p) d -> p f d", p=P)).then_inc(dn_in[g] if landed is None else landed, 16)

            sp_.dma_start(meta_rows, meta_tokens[:, :]).then_inc(x_in[NT], 16)
            for i in range(NT):
                sp_.dma_start(res[:, i, :], x[0, i * P:(i + 1) * P, :]).then_inc(x_in[i], 16)
            for src, at_, n in ((g_mix[0], G_MIX, 8), (g_attn_out[0], G_ATT, 4), (g_conv_out[0], G_CONV, 4), (conv_b[0], CONV_B, 4)):
                sp_.dma_start(vec_rows[at_:at_ + n, :], src.rearrange("(a b) -> a b", b=P)).then_inc(vec_in, 16)
            sp_.dma_start(vec_rows[CONV_W:CONV_W + 12, :], conv_w[0].rearrange("t (a b) -> (t a) b", b=P)).then_inc(vec_in, 16)
            for n, kind in enumerate(LOADS):
                g = GROUP_OF[kind]
                if n >= WIN_SLOTS:
                    sp_.wait_ge(w_used, last_unit(last_job({"cx": "k", "cc": "q", "cb": "cx"}[kind])) + 1)
                sp_.dma_start(win[n], w_in[0, :, g * 512:(g + 1) * 512].rearrange("(k p) f -> p k f", p=P)).then_inc(win_in[n], 16)
                if n == 1:
                    for r in range(2):
                        sp_.dma_start(bgu_rows[r * E:(r + 1) * E, :], b_gu[0]).then_inc(bgu_in, 16)
            sp_.wait_ge(w_used, len(w_units))
            sp_.dma_start(wo, w_out[0].rearrange("(k p) f -> p k f", p=P)).then_inc(wo_in, 16)
            sp_.wait_ge(nscaled, 2 * NC_)
            sp_.dma_start(g_ffn_b, g_ffn[0:1, :].to_broadcast([P, D])).then_inc(late_in, 16)
            sp_.dma_start(b_router_b, b_router[0:1, :].to_broadcast([P, E])).then_inc(late_in, 16)
            sp_.dma_start(w_router_sb, w_router[0].rearrange("(k p) e -> p k e", p=P)).then_inc(late_in, 16)
            sp_.dma_start(b_down_sb, b_down[0]).then_inc(late_in, 16)
            for g in range(6):
                load_gu(0, g)
            for i in range(NT):
                sp_.wait_ge(row_ready, i + 1)
                sp_.dma_start(ffn_rows[i * P:(i + 1) * P, :], rows2[i % 2]).then_inc(row_stored[i], 16)
            sp_.wait_ge(outp, 2 * NT)
            for g in range(6, KD):
                load_gu(0, g)
            for g in range(2):
                load_dn(0, g)
            sp_.wait_ge(logit_done, NT)
            sp_.wait_ge(xs_in, 16)
            for i in range(NT):
                sp_.wait_ge(row_stored[i], 16)
            for g in range(2, NF // 2):
                load_dn(0, g)
            for g in range(KD):
                sp_.wait_ge(unit_used, 2 * g + 2)
                load_gu(1, g)
            sp_.wait_ge(table_ready, 2)
            but_two = sp_.value_load(trips[0:1, 1:2], min_val=E - 2, max_val=E - 2 + EXTRA)
            with sp_.Fori(0, but_two) as it:
                e2 = sp_.value_load(item_e[0:1, bass.ds(it + 2, 1)], min_val=0, max_val=E - 1)
                e1 = sp_.value_load(item_e[0:1, bass.ds(it + 1, 1)], min_val=0, max_val=E - 1)
                for g in range(KD):
                    sp_.wait_ge(unit_used, it * UNITS + (UNITS + 2 * g + 2))
                    load_gu(e2, g)
                for g in range(NF // 2):
                    sp_.wait_ge(unit_used, it * UNITS + (UNITS + GU_UNITS + 2 * g + 2))
                    load_dn(e1, g)
            e1 = sp_.value_load(item_e[0:1, bass.ds(but_two + 1, 1)], min_val=0, max_val=E - 1)
            for g in range(NF // 2):
                sp_.wait_ge(unit_used, but_two * UNITS + (UNITS + 2 * g + 2))
                load_dn(e1, g, gu_pair[g], gu_in[g])
            full = sp_.value_load(trips[0:1, 0:1], min_val=E - 1, max_val=E - 1 + EXTRA)
            sp_.wait_ge(unit_used, through(BY_ALL, full, UNITS - 1, GU_UNITS))
            sp_.dma_start(g_final_b, g_final.rearrange("(a d) -> a d", a=1).to_broadcast([P, D])).then_inc(final_in, 16)
            sp_.wait_ge(y_out, full * 16 + 48)
            for i in range(NT):
                for half in range(2):
                    sp_.dma_start(picked[i][:, 2 * half:2 * half + 2, :],
                                  choice_rows[i * P * TOPK:(i + 1) * P * TOPK, :].rearrange("(p k) d -> p k d", k=TOPK)[:, 2 * half:2 * half + 2, :]).then_inc(picked_in[2 * i + half], 16)
            for i in range(NT):
                sp_.wait_ge(final_ready, i + 1)
                sp_.dma_start(out[0, i * P:(i + 1) * P, :], final_rows[i]).then_inc(stored, 16)
            sp_.wait_ge(stored, 16 * NT)

        @block.tensor
        def _(pe):
            pe.wait_ge(ident_ready, 1)
            pe.wait_ge(vec_in, 5 * 16)
            pe.transpose(banks[4][:, 0:32], vec_rows[:, :], ident[0:32, 0:32]).then_inc(vec_turned, 1)
            for n in range(NT + 1):
                rows = META if n == 0 else P
                pe.wait_ge(xn_ready, n + 1)
                if n == 0:
                    pe.wait_ge(vec_ready, 1)
                if n >= 2:
                    pe.wait_ge(scaled_ready, n - 1)
                src = xn[n % 2]
                for c in range(KD):
                    b = banks[4 + 2 * (n % 2) + c // 4]
                    mm = pe.transpose(b[:, (c % 4) * P:(c % 4) * P + rows], src[0:rows, c * P:(c + 1) * P], ident[0:rows, 0:rows])
                mm.then_inc(xn_turned, 1)
            def project(t):
                kind, c, kh = w_units[t]
                first, last = (c == 0, c == KD - 1) if kind == "v" else (kh == 0, kh == 1)
                pe.wait_ge(w_lo, t + 1)
                for n in jobs_of(t):
                    _, m, h = jobs[n]
                    if t == 0:
                        pe.wait_ge(hT_lo[0], NT // 2 + h)
                        pe.wait_ge(hT_lo[1], NT // 2 - 1 + h)
                    b = job_bank(n)
                    if first:
                        held = bank_holder(n)
                        if held is not None:
                            evac_wait(pe, held)
                        elif bank_no(n) == 4:
                            pe.wait_ge(vec_ready, 1)
                    for r in range(1 if kind == "v" else 4):
                        if kind == "v":
                            k = c
                            lo, rows = (0, META) if m == 0 else (META + (m - 1) * P, P)
                            o = b[0:rows, :]
                        else:
                            k = 4 * kh + r
                            if kind == "k":
                                lo, cols = cols_of(kind, h)
                            elif kind in ("cx", "cc"):
                                lo, cols = cols_of(kind, h)
                                lo += TM - UT
                            else:
                                lo, cols = META, T
                            o = b[:, 0:cols]
                        for p_, (x_half, w_half) in enumerate(((0, 0), (1, 0), (0, 1))):
                            w = wpart[t % 2][w_half]
                            lhs, rhs = (hT[x_half][:, k, lo:lo + rows], w) if kind == "v" else \
                                (w[:, r * P:(r + 1) * P], hT[x_half][:, k, lo:lo + cols])
                            mm = pe.matmul(o, lhs, rhs, start=(first and r == 0 and p_ == 0),
                                           stop=(last and (kind == "v" or r == 3) and p_ == 2))
                mm.then_inc(w_used, 1)

            for t in range(len(HEAD_UNITS)):
                project(t)

            def width_norm(part):
                for c in range(NC_):
                    pe.wait_ge(nsq, part * NC_ + c + 1)
                    mm = pe.matmul(banks[4 + part][:, :], ones[:, :], sq[part][c], start=(c == 0), stop=(c == NC_ - 1))
                mm.then_inc(nsum, 1)

            for n in range(HEAD_JOBS - 2, HEAD_JOBS):
                evac_wait(pe, n)
            pe.wait_ge(ones_ready, 1)
            pe.wait_ge(masks_ready, 3)
            for s in range(NI + 4):
                if s < NI:
                    h, b = att_items[s]
                    t0, keys = span(b)
                    k0 = META + t0 if b >= 0 else 0
                    r = HD * (h % 2)
                    if s >= LB:
                        pe.wait_ge(w_done, s - LB + 1)
                    pe.matmul(banks[s % LB][0:keys, 0:T - t0], kT[r:r + HD, h // 2, k0:k0 + keys],
                              qT[r:r + HD, h // 2, t0:T], start=True, stop=True).then_inc(z_done, 1)
                if 2 <= s < NI + 2:
                    i = s - 2
                    h, b = att_items[i]
                    t0, keys = span(b)
                    L = banks[i % LB]
                    if b >= 0:
                        pe.wait_ge(masked, masks_before[i + 1])
                    else:
                        pe.wait_ge(sp_done, i + 1)
                    mm = pe.matmul(L[0:keys, 0:T - t0], neg_tri[0:keys, 0:keys], sp[i % NSP][0:keys, 0:T - t0],
                                   start=False, stop=True, skip_group_check=True)
                    if b != 3:
                        t1 = P * (b + 1)
                        pe.wait_ge(later_done, masks_before[i - 1])
                        mm = pe.matmul(L[0:keys, t1 - t0:T - t0], neg_one[:, 0:keys], later[h % 2][:, t1:T],
                                       start=False, stop=True, skip_group_check=True)
                    mm.then_inc(logw_done, 1)
                if s in unit_at:
                    project(unit_at[s])
                if s == NI + 3:
                    for n in range(len(jobs) - 2, len(jobs)):
                        evac_wait(pe, n)
                    width_norm(0)
                if 4 <= s < NI + 4:
                    i = s - 4
                    h, b = att_items[i]
                    t0, keys = span(b)
                    r = HD * (h % 2)
                    if b >= 0:
                        pe.wait_ge(w_masked, masks_before[i + 1])
                    else:
                        pe.wait_ge(w_done, i + 1)
                    if b == 3 and h % 2 == 0 and h >= 4:
                        pe.wait_ge(att_copied, h // 2 - 1)
                    pe.matmul(banks[OB + (h // 2) % 2][r:r + HD, t0:T], vN[0:keys, b + 1, HD * h:HD * (h + 1)],
                              wT[i % NW][0:keys, 0:T - t0], start=(b == 3), stop=True,
                              skip_group_check=True).then_inc(av_done, 1)
            width_norm(1)
            pe.wait_ge(wo_in, 16)
            def turn_row_tile(i):
                pe.wait_ge(row_ready, i + 1)
                if i >= 1:
                    pe.wait_ge(rowT_ready, 2 * i)
                for c in range(KD):
                    mm = pe.transpose(banks[4 + c // 4][:, (c % 4) * P:(c % 4 + 1) * P], rows2[i % 2][:, c * P:(c + 1) * P], ident[:, :])
                mm.then_inc(row_turned, 1)

            def router(i):
                pe.wait_ge(rowT_ready, 2 * (i + 1))
                if i == 0:
                    pe.wait_ge(late_in, 64)
                if i >= 1:
                    pe.wait_ge(route, i)
                for k in range(KD):
                    mm = pe.matmul(banks[6][:, 0:E], rowsT[i % 2][:, k, :], w_router_sb[:, k, :], start=(k == 0), stop=(k == KD - 1))
                mm.then_inc(logit_done, 1)

            for i in range(NT):
                for n in range(2):
                    m = 2 * i + n
                    if m >= 4:
                        pe.wait_ge(res_added, m - 3)
                    for r, k in enumerate((4, 5, 6, 7, 0, 1, 2, 3)):
                        if m == 0:
                            pe.wait_ge(nscaled, r + 1)
                        mm = pe.matmul(banks[m % 4][:, :], mixT[:, k, i * P:(i + 1) * P], wo[:, k, n * 512:(n + 1) * 512],
                                       start=(r == 0), stop=(r == KD - 1))
                    mm.then_inc(outp, 1)
                    if i >= 1:
                        if n == 0:
                            turn_row_tile(i - 1)
                        else:
                            router(i - 1)
            turn_row_tile(NT - 1)
            router(NT - 1)
            pe.wait_ge(mask_ready, 1)
            pe.wait_ge(slots_ready, 1)
            for i in range(NT):
                for m in range(i + 1):
                    pe.matmul(banks[5][:, i * E:(i + 1) * E], (before if m == i else ones_h)[:, :], onehot[:, m, 0:E],
                              start=(m == 0), stop=(m == i))
            for m in range(NT):
                mm = pe.matmul(banks[5][:, NT * E:(NT + 1) * E], ones_h[:, :], onehot[:, m, 0:E], start=(m == 0), stop=(m == NT - 1))
            mm.then_inc(pos_done, 1)
            def sum_ids(n):
                pe.wait_ge(onehot_ready, n + 1)
                for m in range(NT):
                    mm = pe.matmul(banks[7][0:SLOTS, 504:508], onehot[:, m, :], ids[:, m, :], start=(m == 0), stop=(m == NT - 1))
                mm.then_inc(idx_summed, 1)

            def turn(src, turned):
                for c in range(KD):
                    mm = pe.transpose(banks[6 + c // 4][:, (c % 4) * SLOTS:(c % 4 + 1) * SLOTS], src[:, c * P:(c + 1) * P], ident[0:SLOTS, 0:SLOTS])
                mm.then_inc(turned, 1)

            def lower_ready(it, u, skip=0):
                by, done = (BY_POOL, lo_pool) if u in BY_POOL else (BY_DVE, lo_dve)
                pe.wait_ge(done, through(by, it, u, skip))

            def split_product(out_bank, lhs, k, s, q, start, stop):
                for n, (x_half, w_half) in enumerate(((0, 0), (0, 1), (1, 0))):
                    mm = pe.matmul(out_bank[0:SLOTS, :], lhs[:, x_half, k, :], stage[:, s, w_half, q * 512:(q + 1) * 512],
                                   start=(start and n == 0), stop=(stop and n == 2))
                return mm

            def gu_unit(it, u):
                k, s = u // 2, u % 2
                lower_ready(it, u)
                for q in range(2):
                    mm = split_product(banks[2 * s + q], xsT, k, u % STAGES, q, False, k == KD - 1)
                mm.then_inc(unit_used, step_of(BY_ALL, it, u))

            def gate_and_up_biases():
                for b in range(4):
                    pe.matmul(banks[b][0:SLOTS, :], sel[:, :], bgu[:, b * 512:(b + 1) * 512], start=True, stop=False)

            def down_units(it, skip=0):
                for v in range(NF):
                    u = GU_UNITS + v
                    lower_ready(it, u, skip)
                    for q in range(2):
                        mm = split_product(banks[4 + q], hidT, v, u % STAGES, q, v == 0, v == NF - 1)
                    mm.then_inc(unit_used, 1)
                    if v == TURN_AFTER and not skip:
                        pe.wait_ge(xs_in, it * 16 + 48)
                        turn(xs, xs_turned)

            sum_ids(0)
            pe.wait_ge(idx_copied, 1)
            pe.wait_ge(xs_in, 16)
            turn(xs, xs_turned)
            pe.wait_ge(bgu_ready, 1)
            pe.wait_ge(xsT_hi, 1)
            pe.wait_ge(xsT_lo, 1)
            gate_and_up_biases()
            for u in range(GU_UNITS):
                gu_unit(None, u)
                if u == 8:
                    sum_ids(1)
                if u == 11:
                    pe.wait_ge(mask_ready, 2)
                    for i in range(NT):
                        mm = pe.transpose(banks[6][0:E, i * P:(i + 1) * P], dense[:, i, :], ident[:, :])
                    mm.then_inc(dense_turned, 1)
            pe.wait_ge(dense_ready, 1)
            pe.wait_ge(xs_in, 32)
            turn(xs, xs_turned)
            pe.wait_ge(idx_copied, 2)
            pe.wait_ge(table_ready, 2)
            trip = pe.value_load(trips[0:1, 0:1], min_val=E - 1, max_val=E - 1 + EXTRA)
            with pe.Fori(0, trip) as it:
                pe.wait_ge(sel_ready, it + 2)
                pe.wait_ge(xsT_hi, it + 2)
                pe.wait_ge(xsT_lo, it + 2)
                pe.wait_ge(glu_read, it * 2 + 2)
                pe.wait_ge(gate_ready, it * 2 + 2)
                gate_and_up_biases()
                for u in range(GU_UNITS):
                    gu_unit(it, u)
                    if u == 0:
                        sum_ids(it + 2)
                    if u == 5:
                        pe.wait_ge(idx_copied, it + 3)
                        pe.wait_ge(hid_ready, it * 2 + 2)
                        turn(hid, hid_turned)
                pe.wait_ge(hidT_hi, it + 1)
                pe.wait_ge(hidT_lo, it + 1)
                pe.wait_ge(ys_ready, it + 1)
                down_units(it)
            pe.wait_ge(xsT_hi, trip + 2)
            pe.wait_ge(xsT_lo, trip + 2)
            pe.wait_ge(hid_ready, trip * 2 + 2)
            turn(hid, hid_turned)
            pe.wait_ge(hidT_hi, trip + 1)
            pe.wait_ge(hidT_lo, trip + 1)
            pe.wait_ge(ys_ready, trip + 1)
            down_units(trip, GU_UNITS)
            pe.wait_ge(glu_read, trip * 2 + 2)
            pe.wait_ge(gate_ready, trip * 2 + 2)
            for m in range(2 * NT):
                if m >= 4:
                    pe.wait_ge(base_ready, m - 3)
                pe.matmul(banks[m % 4][:, :], gates_T[:, m // 2, :], b_down_sb[:, (m % 2) * 512:(m % 2 + 1) * 512],
                          start=True, stop=True).then_inc(bias_done, 1)

        @block.scalar
        def _(act):
            def w_upper(t):
                kind, c, kh = w_units[t]
                act.wait_ge(win_in[SLOT_OF[kind]], 16)
                if t >= 2:
                    act.wait_ge(w_used, t - 1)
                w, dst = win[SLOT_OF[kind]], wpart[t % 2][0]
                if kind == "v":
                    ins = act.activation(dst, w[:, c, :], ACT.Copy)
                else:
                    ins = act.activation(dst.rearrange("p (a b) -> p a b", b=P), w[:, 4 * kh:4 * kh + 4, c * P:(c + 1) * P], ACT.Copy)
                ins.then_inc(w_hi, 1)

            act.wait_ge(eps_ready, 1)
            for n in range(NT + 1):
                act.wait_ge(x_in[NT if n == 0 else n - 1], 16)
                src = meta_rows if n == 0 else res[:, n - 1, :]
                rows = META if n == 0 else P
                if n >= 2:
                    act.wait_ge(squares, n - 1)
                act.activation(squared[n % 2][0:rows, :], src, ACT.Square, accum_out=ss[0:rows, n:n + 1]).then_inc(squares, 1)
                act.wait_ge(squares, n + 1)
                act.activation(rs[0:rows, n:n + 1], ss[0:rows, n:n + 1], ACT.Sqrt, scale=1.0 / D, bias=eps_t[0:rows, :]).then_inc(rms_act, 1)
            for n in range(NT + 1):
                lo, rows = (0, META) if n == 0 else (META + (n - 1) * P, P)
                act.wait_ge(scaled_ready, n + 1)
                act.activation(hT[0][:, :, lo:lo + rows], scaled[n % 2][:, :, 0:rows], ACT.Copy).then_inc(hT_hi, 1)
                if n in (2, 3):
                    w_upper(n - 2)
            for t in range(2, len(HEAD_UNITS) + 2):
                w_upper(t)
                if t == len(HEAD_UNITS) // 2:
                    act.wait_ge(bgu_in, 32)
                    act.activation(bgu[0:2 * E, :], bgu_rows, ACT.Copy).then_inc(bgu_hi, 1)
                for n in range(HEAD_JOBS):
                    if evac_by_act(n) and last_unit(n) == t - 2:
                        kind, c, h = jobs[n]
                        b = job_bank(n)
                        act.wait_ge(w_used, t - 1)
                        if kind == "k":
                            ins = act.activation(kT[:, c, h * HALF_K:(h + 1) * HALF_K], b[:, 0:HALF_K], ACT.Copy)
                        elif kind == "q":
                            ins = act.activation(qT[:, c, :], b[:, :], ACT.Copy, scale=HD ** -0.5)
                        else:
                            rows = META if c == 0 else P
                            ins = act.activation(vN[0:rows, c, :], b[0:rows, :], ACT.Copy)
                        ins.then_inc(proj_act, 1)

            act.preload_act_table_set("natural_log_exp_and_others")
            for s in range(NI + 3):
                if s >= 3:
                    i = s - 3
                    h, b = att_items[i]
                    t0, keys = span(b)
                    act.wait_ge(logw_done, i + 1)
                    if i >= NW:
                        act.wait_ge(av_done, i - NW + 1)
                    act.activation(wT[i % NW][0:keys, 0:T - t0], banks[i % LB][0:keys, 0:T - t0], ACT.Exp).then_inc(w_done, 1)
                if s < NI:
                    h, b = att_items[s]
                    t0, keys = span(b)
                    a = za[s % NA][0:keys, 0:T - t0]
                    act.wait_ge(abs_done, s + 1)
                    act.activation(a, a, ACT.Exp, scale=-1.0).then_inc(exp_done, 1)
                    act.wait_ge(exp_done, s + 1)
                    act.activation(a, a, ACT.Ln, bias=1.0).then_inc(ln_done, 1)
                if s in split_at:
                    w_upper(split_at[s])
                for n in range(HEAD_JOBS, len(jobs)):
                    kind, c, h = jobs[n]
                    if kind == "cx" and read_step[n] == s:
                        lo, cols = cols_of(kind, h)
                        act.wait_ge(w_used, last_unit(n) + 1)
                        act.activation(uT[:, c, lo:lo + cols], job_bank(n)[:, 0:cols], ACT.Copy).then_inc(proj_act, 1)
                    if kind == "cb" and read_step[n] + 1 == s:
                        evac_wait(act, n)
                        act.activation(sq[0][c], mixT[:, NC_ + c, :], ACT.Square).then_inc(nsq, 1)
            def one_over_root(part):
                act.wait_ge(nsum, part + 1)
                act.activation(root[part], banks[4 + part][:, :], ACT.Ln, scale=1.0 / AW, bias=eps_t[:, :]).then_inc(nroot, 1)
                act.wait_ge(nroot, 2 * part + 1)
                act.activation(rstd[part], root[part], ACT.Exp, scale=-0.5).then_inc(nroot, 1)

            act.wait_ge(av_done, NI)
            act.wait_ge(att_copied, NC_)
            for c in range(NC_):
                act.activation(sq[1][c], mixT[:, c, :], ACT.Square).then_inc(nsq, 1)
                if c == 0:
                    one_over_root(0)
            one_over_root(1)
            for i in range(NT):
                act.wait_ge(res_added, 2 * (i + 1))
                if i >= 1:
                    act.wait_ge(row_ready, i)
                if i >= 2:
                    act.wait_ge(row_stored[i - 2], 16)
                    act.wait_ge(row_turned, i - 1)
                act.activation(rows2[i % 2], res[:, i, :], ACT.Square, accum_out=ss[:, i:i + 1]).then_inc(row_sq, 1)
                act.wait_ge(row_sq, i + 1)
                act.activation(rs[:, i:i + 1], ss[:, i:i + 1], ACT.Ln, scale=1.0 / D, bias=eps_t[:, :]).then_inc(row_var, 1)
                act.wait_ge(row_var, i + 1)
                act.activation(rs[:, i:i + 1], rs[:, i:i + 1], ACT.Exp, scale=-0.5).then_inc(row_root, 1)
                act.wait_ge(row_turned, i + 1)
                if i >= 2:
                    act.wait_ge(logit_done, i - 1)
                for c in range(2):
                    act.activation(rowsT[i % 2][:, 4 * c:4 * c + 4, :], banks[4 + c][:, :].rearrange("p (a b) -> p a b", b=P), ACT.Copy).then_inc(rowT_ready, 1)
            act.wait_ge(gate_exp, 1)
            act.activation(gates[:, :, :], gates[:, :, :], ACT.Exp).then_inc(gate_exp, 1)

            def upper(it, u, skip=0):
                if u < GU_UNITS or skip:
                    m = u - skip
                    act.wait_ge(gu_in[m // 2], 16 if it is None else it * 16 + 32)
                    src = gu_pair[m // 2][:, m % 2, :]
                else:
                    act.wait_ge(dn_in[(u - GU_UNITS) // 2], it * 16 + 16)
                    src = dn_pair[(u - GU_UNITS) // 2][:, u % 2, :]
                free = free_again(it, u, skip)
                if free is not None:
                    act.wait_ge(unit_used, free)
                act.activation(stage[:, u % STAGES, 0, :], src, ACT.Copy).then_inc(hi_done, step_of(BY_ALL, it, u))

            def upper_turned(dst, done):
                for c in range(2):
                    ins = act.activation(dst[:, 0, 4 * c:4 * c + 4, :], banks[6 + c][:, 0:4 * SLOTS].rearrange("p (a b) -> p a b", b=SLOTS), ACT.Copy)
                ins.then_inc(done, 1)

            def sigmoid(n, q):
                act.wait_ge(gate_ready, n * 2 + (q + 1))
                act.activation(sig_t[:, q * 512:(q + 1) * 512], gate_t[:, q * 512:(q + 1) * 512], ACT.Sigmoid, scale=ALPHA).then_inc(sig_done, 1)

            def outputs_out(it):
                act.wait_ge(unit_used, it * UNITS + UNITS)
                act.wait_ge(y_out, it * 16 + 16)
                for c in range(2):
                    ins = act.activation(ys[:, 512 * c:512 * (c + 1)], banks[4 + c][0:SLOTS, :], ACT.Copy)
                ins.then_inc(ys_ready, 1)

            act.wait_ge(xs_turned, 1)
            upper_turned(xsT, xsT_hi)
            for u in range(GU_UNITS):
                upper(None, u)
            act.wait_ge(table_ready, 2)
            trip = act.value_load(trips[0:1, 0:1], min_val=E - 1, max_val=E - 1 + EXTRA)
            act.wait_ge(xs_turned, 2)
            act.wait_ge(unit_used, GU_UNITS)
            upper_turned(xsT, xsT_hi)
            for q in range(2):
                sigmoid(0, q)
            with act.Fori(0, trip) as it:
                for u in range(UNITS):
                    upper(it, u)
                    if u == 11:
                        outputs_out(it)
                    if u == 9:
                        act.wait_ge(hid_turned, it + 1)
                        act.wait_ge(unit_used, it * UNITS + UNITS)
                        upper_turned(hidT, hidT_hi)
                    if u in (20, 21):
                        q = u - 20
                        act.wait_ge(hid_ready, it * 2 + (q + 1))
                        sigmoid(it + 1, q)
                    if u == GU_UNITS + TURN_AFTER + 4:
                        act.wait_ge(xs_turned, it + 3)
                        act.wait_ge(unit_used, it * UNITS + (UNITS + GU_UNITS))
                        upper_turned(xsT, xsT_hi)
            for u in range(GU_UNITS, UNITS):
                if u == GU_UNITS + 2:
                    outputs_out(trip)
                    act.wait_ge(hid_turned, trip + 1)
                    upper_turned(hidT, hidT_hi)
                upper(trip, u, GU_UNITS)
            act.wait_ge(unit_used, through(BY_ALL, trip, UNITS - 1, GU_UNITS))
            act.wait_ge(y_out, trip * 16 + 32)
            for c in range(2):
                ins = act.activation(ys[:, 512 * c:512 * (c + 1)], banks[4 + c][0:SLOTS, :], ACT.Copy)
            ins.then_inc(ys_ready, 1)
            for i in range(NT):
                act.wait_ge(final_sum, TOPK * (i + 1))
                if i >= 1:
                    act.wait_ge(final_sq, i)
                act.activation(final_junk, res[:, i, :], ACT.Square, accum_out=ss[:, i:i + 1]).then_inc(final_sq, 1)
                act.wait_ge(final_sq, i + 1)
                act.activation(rs[:, i:i + 1], ss[:, i:i + 1], ACT.Sqrt, scale=1.0 / D, bias=eps_t[:, :]).then_inc(final_rt, 1)

        @block.vector
        def _(v):
            v.memset(eps_t[:, :], EPS)
            v.memset(ss[:, :], 1.0).then_inc(eps_ready, 1)
            def scale_rows(n):
                src = meta_rows if n == 0 else res[:, n - 1, :]
                rows = META if n == 0 else P
                v.wait_ge(rms_act, n + 1)
                v.reciprocal(rs[0:rows, n:n + 1], rs[0:rows, n:n + 1]).then_inc(sq_dve, 1)
                v.wait_ge(sq_dve, n + 1)
                v.tensor_scalar(xn[n % 2][0:rows, :], src, rs[0:rows, n:n + 1], None, ALU.mult).then_inc(xn_ready, 1)

            def gain_rows(n):
                lo, rows = (0, META) if n == 0 else (META + (n - 1) * P, P)
                v.wait_ge(xn_turned, n + 1)
                if n >= 2:
                    v.wait_ge(hT_lo[n % 2], n // 2)
                for c in range(2):
                    src = banks[4 + 2 * (n % 2) + c][:, :].rearrange("p (a b) -> p a b", b=P)[:, :, 0:rows]
                    gain = vecT[:, G_MIX + 4 * c:G_MIX + 4 * c + 4].rearrange("p (a b) -> p a b", b=1).to_broadcast([P, 4, rows])
                    ins = v.tensor_tensor(scaled[n % 2][:, 4 * c:4 * c + 4, 0:rows], src, gain, ALU.mult)
                ins.then_inc(scaled_ready, 1)

            def input_lower(n):
                lo, rows = (0, META) if n == 0 else (META + (n - 1) * P, P)
                v.wait_ge(hT_hi, n + 1)
                v.tensor_tensor(hT[1][:, :, lo:lo + rows], scaled[n % 2][:, :, 0:rows], hT[0][:, :, lo:lo + rows].bitcast(F32), ALU.subtract).then_inc(hT_lo[0], 1)

            def w_lower(t):
                kind, c, kh = w_units[t]
                v.wait_ge(w_hi, t + 1)
                w, (hi, dst) = win[SLOT_OF[kind]], wpart[t % 2]
                if kind == "v":
                    ins = v.tensor_tensor(dst, w[:, c, :], hi.bitcast(F32), ALU.subtract)
                else:
                    ins = v.tensor_tensor(dst.rearrange("p (a b) -> p a b", b=P), w[:, 4 * kh:4 * kh + 4, c * P:(c + 1) * P],
                                          hi.bitcast(F32).rearrange("p (a b) -> p a b", b=P), ALU.subtract)
                ins.then_inc(w_lo, 1)

            scale_rows(0)
            v.wait_ge(vec_turned, 1)
            v.tensor_copy(vecT[:, :], banks[4][:, 0:32]).then_inc(vec_ready, 1)
            v.wait_ge(vec_ready, 1)
            for n in range(NT + 1):
                if n < NT:
                    scale_rows(n + 1)
                gain_rows(n)
                if n % 2 == 1:
                    input_lower(n - 1)
                if n == 3:
                    w_lower(0)
            input_lower(NT)
            w_lower(1)

            def vec(col):
                return vecT[:, col:col + 1]

            steps = [0]

            def conv(ins):
                steps[0] += 1
                ins.then_inc(conv_step, 1)

            def read_out(n):
                kind, c, h = jobs[n]
                b = job_bank(n)
                v.wait_ge(w_used, last_unit(n) + 1)
                if kind == "k":
                    ins = v.tensor_copy(kT[:, c, h * HALF_K:(h + 1) * HALF_K], b[:, 0:HALF_K])
                elif kind == "q":
                    ins = v.tensor_scalar(qT[:, c, :], b[:, :], HD ** -0.5, None, ALU.mult)
                elif kind == "v":
                    rows = META if c == 0 else P
                    ins = v.tensor_copy(vN[0:rows, c, :], b[0:rows, :])
                elif kind == "cc":
                    lo, cols = cols_of(kind, h)
                    u = uT[:, c, lo:lo + cols]
                    evac_wait(v, jobs.index(("cx", c, h)))
                    ins = v.tensor_tensor(u, b[:, 0:cols], u, ALU.mult)
                else:
                    o = mixT[:, NC_ + c, :]
                    v.wait_ge(conv_step, TAPS * (c + 1))
                    ins = v.tensor_tensor(o, b[:, :], o, ALU.mult)
                ins.then_inc(proj_dve, 1)

            def conv_tap(tap, m):
                o = mixT[:, NC_ + m, :]
                if tap == 0:
                    evac_wait(v, jobs.index(("cc", m, 1)))
                    conv(v.tensor_scalar(o, uT[:, m, 0:T], vec(CONV_W + m), vec(CONV_B + m), ALU.mult, ALU.add))
                else:
                    v.wait_ge(conv_step, TAPS * m + tap)
                    conv(v.scalar_tensor_tensor(out=o, in0=uT[:, m, tap:tap + T], scalar=vec(CONV_W + 4 * tap + m),
                                                in1=o, op0=ALU.mult, op1=ALU.add))

            for t in range(2, len(HEAD_UNITS) + 2):
                w_lower(t)
                for n in range(HEAD_JOBS):
                    if not evac_by_act(n) and last_unit(n) == t - 2:
                        read_out(n)
            v.memset(bgu[2 * E:P, :].bitcast(F32), 0.0)
            v.wait_ge(bgu_hi, 1)
            v.tensor_tensor(bgu[E:2 * E, :], bgu_rows[E:2 * E, :], bgu[E:2 * E, :].bitcast(F32), ALU.subtract).then_inc(bgu_ready, 1)
            v.wait_ge(bgu_ready, 1)
            v.wait_ge(slots_ready, 1)
            v.wait_ge(rows_ready, 1)

            def width_norm(part):
                v.wait_ge(nroot, 2 * part + 2)
                for c in range(NC_):
                    o = mixT[:, c + (0 if part else NC_), :]
                    g = vec((G_ATT if part else G_CONV) + c)
                    v.scalar_tensor_tensor(out=o, in0=o, scalar=g, in1=rstd[part], op0=ALU.mult, op1=ALU.mult).then_inc(nscaled, 1)

            v.wait_ge(masks_ready, 3)
            for s in range(NI + 1):
                if s < NI:
                    h, b = att_items[s]
                    t0, keys = span(b)
                    v.wait_ge(z_done, s + 1)
                    if s >= NA:
                        v.wait_ge(sp_done, s - NA + 1)
                    v.tensor_scalar(za[s % NA][0:keys, 0:T - t0].bitcast(I32), banks[s % LB][0:keys, 0:T - t0].bitcast(I32),
                                    0x7FFFFFFF, None, ALU.bitwise_and).then_inc(abs_done, 1)
                if s >= 1:
                    i = s - 1
                    h, b = att_items[i]
                    t0, keys = span(b)
                    v.wait_ge(ln_done, i + 1)
                    if i >= NSP:
                        v.wait_ge(logw_done, i - NSP + 1)
                        v.wait_ge(later_done, masks_before[i - NSP + 1])
                    v.scalar_tensor_tensor(out=sp[i % NSP][0:keys, 0:T - t0], in0=banks[i % LB][0:keys, 0:T - t0], scalar=0.0,
                                           in1=za[i % NA][0:keys, 0:T - t0], op0=ALU.max, op1=ALU.add).then_inc(sp_done, 1)
                    if b >= 0:
                        v.wait_ge(sp_done, i + 1)
                        v.tensor_tensor(sp[i % NSP][:, 0:P], sp[i % NSP][:, 0:P], causal, ALU.mult).then_inc(masked, 1)
                if s >= 15 and (s - 15) % 10 == 0 and s < NI:
                    c = (s - 15) // 10
                    v.wait_ge(av_done, 10 * (c + 1))
                    v.tensor_copy(mixT[:, c, :], banks[OB + c % 2][:, :]).then_inc(att_copied, 1)
                if s in split_at:
                    w_lower(split_at[s])
                for tap, m in tap_step.get(s, ()):
                    conv_tap(tap, m)
                for n in range(HEAD_JOBS, len(jobs)):
                    if not evac_by_act(n) and read_step[n] == s:
                        read_out(n)
            v.wait_ge(av_done, NI)
            v.tensor_copy(mixT[:, NC_ - 1, :], banks[OB + (NC_ - 1) % 2][:, :]).then_inc(att_copied, 1)
            v.wait_ge(att_copied, NC_)
            width_norm(0)
            width_norm(1)
            at_ = LATE

            def late(*shape, dt=None):
                nonlocal at_
                n = 1
                for q in shape:
                    n *= q
                r = view(ring, at_, *shape)
                at_ += n
                return r

            v.tensor_copy(item_all[:, 0:E], slot_no[:, 0:E]).then_inc(first_items, 1)
            v.memset(shift[:, 0:E], 0.0).then_inc(first_items, 1)
            v.memset(row_idx[:, :], int(SKIP)).then_inc(bufs_clear, 1)
            v.memset(row_tab[:, 0:1], int(SKIP)).then_inc(bufs_clear, 1)
            v.wait_ge(late_in, 64)
            for i in range(NT):
                for n in range(2):
                    v.wait_ge(outp, 2 * i + n + 1)
                    o = res[:, i, n * 512:(n + 1) * 512]
                    v.tensor_tensor(o, banks[(2 * i + n) % 4][:, :], o, ALU.add).then_inc(res_added, 1)
                v.wait_ge(row_root, i + 1)
                v.wait_ge(res_added, 2 * (i + 1))
                v.scalar_tensor_tensor(out=rows2[i % 2], in0=res[:, i, :], scalar=rs[:, i:i + 1], in1=g_ffn_b,
                                       op0=ALU.mult, op1=ALU.mult).then_inc(row_ready, 1)
                if i >= 1:
                    v.wait_ge(logit_done, i)
                    v.tensor_tensor(logits[:, i - 1, :], banks[6][:, 0:E], b_router_b, ALU.add).then_inc(route, 1)
            v.wait_ge(logit_done, NT)
            v.tensor_tensor(logits[:, NT - 1, :], banks[6][:, 0:E], b_router_b, ALU.add).then_inc(route, 1)
            v.wait_ge(route, NT)
            chain = [NT]

            def step(ins):
                chain[0] += 1
                ins.then_inc(route, 1)
                v.wait_ge(route, chain[0])

            for i in range(NT):
                v.max(top[:, i, :], logits[:, i, :]).then_inc(route, 1)
            chain[0] += NT
            v.wait_ge(route, chain[0])
            for i in range(NT):
                v.max_index(top_e[:, i, :], top[:, i, :], logits[:, i, :]).then_inc(route, 1)
            chain[0] += NT
            v.wait_ge(route, chain[0])
            v.tensor_tensor(gates[:, :, :], top[:, :, 0:TOPK], top[:, :, 0:1].to_broadcast([P, NT, TOPK]), ALU.subtract).then_inc(gate_exp, 1)
            chosen = late(NT, 8)
            step(v.tensor_copy(chosen, top_e[:, :, :]))
            e_no = late(E)
            v.wait_ge(slots_ready, 1)
            step(v.tensor_copy(e_no, slot_no[:, 0:E]))
            picks = [late(NT, E) for _ in range(TOPK)]
            e_all = e_no.rearrange("p (a e) -> p a e", a=1).to_broadcast([P, NT, E])
            for k in range(TOPK):
                ins = v.tensor_tensor(picks[k], e_all, chosen[:, :, k:k + 1].to_broadcast([P, NT, E]), ALU.is_equal)
                ins.then_inc(route, 1)
            chain[0] += TOPK
            v.wait_ge(route, chain[0])
            mask = late(NT, E)
            step(v.tensor_tensor(mask, picks[0], picks[1], ALU.add))
            step(v.tensor_tensor(mask, mask, picks[2], ALU.add))
            step(v.tensor_tensor(mask, mask, picks[3], ALU.add))
            v.tensor_copy(onehot[:, :, 0:E], mask).then_inc(mask_ready, 1)
            step(v.scalar_tensor_tensor(out=choice[:, :, :], in0=picks[2], scalar=2.0, in1=picks[1], op0=ALU.mult, op1=ALU.add))
            step(v.scalar_tensor_tensor(out=choice[:, :, :], in0=picks[3], scalar=3.0, in1=choice[:, :, :], op0=ALU.mult, op1=ALU.add))
            v.wait_ge(pos_done, 1)
            step(v.scalar_tensor_tensor(out=place[:, :, :], in0=banks[5][:, 0:NT * E].rearrange("p (a e) -> p a e", e=E), scalar=4096.0,
                                        in1=mask, op0=ALU.add, op1=ALU.mult))
            step(v.tensor_scalar(place[:, :, :], place[:, :, :], -4096.0, None, ALU.add))
            def select_bias(number):
                v.tensor_scalar(sel[:, :], item_all[:, number].to_broadcast([P, SLOTS]), bgu_row[:, 0:1], None, ALU.is_equal).then_inc(sel_ready, 1)

            def prepare(n, number):
                e = n if isinstance(n, int) else v.value_load(item_e[0:1, number], min_val=0, max_val=E - 1)
                if not isinstance(n, int) or n > 0:
                    v.wait_ge(idx_summed, n)
                v.tensor_copy(ids[:, :, 3:4], choice[:, :, bass.ds(e, 1)]).then_inc(prep_step, 1)
                v.tensor_scalar(place_i[:, :].rearrange("p (a b) -> p a b", b=1), place[:, :, bass.ds(e, 1)], shift[:, number], None, ALU.add).then_inc(prep_step, 1)
                v.wait_ge(prep_step, n * 2 + 2)
                v.tensor_tensor(onehot[:, :, :], slot_no[:, :].rearrange("p (a s) -> p a s", a=1).to_broadcast([P, NT, SLOTS]),
                                place_i[:, :].rearrange("p (a b) -> p a b", b=1).to_broadcast([P, NT, SLOTS]), ALU.is_equal).then_inc(onehot_ready, 1)

            def indices(n, column):
                v.wait_ge(idx_summed, n + 1)
                v.tensor_copy(slot_f[:, :], banks[7][0:SLOTS, 504:508]).then_inc(idx_copied, 1)
                v.wait_ge(idx_copied, n + 1)
                v.tensor_scalar(slot_g[:, 0:1], slot_f[:, 2:3], -SKIP, SKIP, ALU.mult, ALU.add).then_inc(idx_step, 1)
                v.wait_ge(idx_step, n * 3 + 1)
                v.scalar_tensor_tensor(out=slot_g[:, 1:2], in0=slot_f[:, 0:1], scalar=slot_f[:, 1:2], in1=slot_g[:, 0:1], op0=ALU.add, op1=ALU.add).then_inc(idx_step, 1)
                v.wait_ge(idx_step, n * 3 + 2)
                v.tensor_tensor(row_tab[:, column], slot_g[:, 1:2], slot_f[:, 3:4], ALU.add).then_inc(idx_step, 1)
                if not isinstance(n, int) or n > 0:
                    v.wait_ge(xs_in, n * 16)
                v.tensor_scalar(tok_idx[:, :], slot_g[:, 1:2], 0.25, None, ALU.mult).then_inc(idx_ready, 1)

            v.wait_ge(first_items, 2)
            prepare(0, slice(0, 1))
            select_bias(slice(0, 1))
            indices(0, slice(1, 2))
            counts, extra, cum, one_e = late(E), late(E), late(E), late(E)
            step(v.tensor_copy(counts, banks[5][:, NT * E:(NT + 1) * E]))
            step(v.memset(one_e, 1.0))
            step(v.tensor_scalar(extra, counts, float(SLOTS), None, ALU.is_gt))
            for b in range(2, BLOCKS):
                step(v.scalar_tensor_tensor(out=extra, in0=counts, scalar=float(SLOTS * b), in1=extra, op0=ALU.is_gt, op1=ALU.add))
            step(v.tensor_tensor_scan(cum, one_e, extra, 0.0, ALU.mult, ALU.add))
            done = view(ring, LATE_AT, KEYS, E)
            key_e, key_b, key_end, key_no = late(KEYS), late(KEYS), late(KEYS), late(KEYS)
            step(v.tensor_copy(key_no, slot_no[:, 0:KEYS]))
            step(v.tensor_tensor(done, cum.rearrange("p (a e) -> p a e", a=1).to_broadcast([P, KEYS, E]),
                                 key_no.rearrange("p (k a) -> p k a", a=1).to_broadcast([P, KEYS, E]), ALU.is_le))
            step(v.tensor_reduce(key_e, done, AX.X, ALU.add))
            step(v.tensor_tensor(done, done, extra.rearrange("p (a e) -> p a e", a=1).to_broadcast([P, KEYS, E]), ALU.mult))
            step(v.tensor_reduce(key_b, done, AX.X, ALU.add))
            step(v.tensor_scalar(key_end, key_e, float(E), None, ALU.is_equal))
            step(v.tensor_tensor(key_b, key_no, key_b, ALU.subtract))
            step(v.scalar_tensor_tensor(out=key_b, in0=key_end, scalar=float(BLOCKS), in1=key_b, op0=ALU.mult, op1=ALU.add))
            step(v.tensor_scalar(shift[:, E:ITEMS], key_b[:, 0:ITEMS - E], 1.0, -float(SLOTS), ALU.add, ALU.mult))
            step(v.tensor_scalar(key_e, key_e, float(E - 1), None, ALU.min))
            step(v.tensor_copy(item_all[:, E:ITEMS], key_e[:, 0:ITEMS - E]))
            step(v.tensor_copy(item_e[:, 0:E], slot_no[0:1, 0:E]))
            v.tensor_copy(item_e[:, E:ITEMS], key_e[0:1, 0:ITEMS - E]).then_inc(table_ready, 1)
            step(v.tensor_scalar(trips[:, 0:1], cum[0:1, E - 1:E], float(E - 1), None, ALU.add))
            v.tensor_scalar(trips[:, 1:2], cum[0:1, E - 1:E], float(E - 2), None, ALU.add).then_inc(table_ready, 1)
            gsum = late(NT)

            def gate_table():
                v.wait_ge(gate_exp, 2)
                step(v.tensor_reduce(gsum, gates[:, :, :], AX.X, ALU.add))
                step(v.reciprocal(gsum, gsum))
                step(v.tensor_tensor(gates[:, :, :], gates[:, :, :], gsum.rearrange("p (a b) -> p a b", b=1).to_broadcast([P, NT, TOPK]), ALU.mult))
                for k in range(TOPK):
                    v.tensor_tensor(picks[k], picks[k], gates[:, :, k:k + 1].to_broadcast([P, NT, E]), ALU.mult).then_inc(route, 1)
                chain[0] += TOPK
                v.wait_ge(route, chain[0])
                v.wait_ge(logit_done, NT)
                step(v.tensor_tensor(mask, picks[0], picks[1], ALU.add))
                step(v.tensor_tensor(mask, mask, picks[2], ALU.add))
                v.tensor_tensor(dense, mask, picks[3], ALU.add).then_inc(mask_ready, 1)
            assert at_ <= RING

            def lower(it, u, skip=0):
                if u < GU_UNITS or skip:
                    m = u - skip
                    v.wait_ge(gu_in[m // 2], 16 if it is None else it * 16 + 32)
                    src = gu_pair[m // 2][:, m % 2, :]
                else:
                    v.wait_ge(dn_in[(u - GU_UNITS) // 2], it * 16 + 16)
                    src = dn_pair[(u - GU_UNITS) // 2][:, u % 2, :]
                v.wait_ge(hi_done, through(BY_ALL, it, u, skip))
                v.tensor_tensor(stage[:, u % STAGES, 1, :], src, stage[:, u % STAGES, 0, :].bitcast(F32), ALU.subtract).then_inc(lo_dve, step_of(BY_DVE, it, u))

            def lower_turned(dst, upper_done, n, done):
                v.wait_ge(upper_done, n + 1)
                for c in range(2):
                    ins = v.tensor_tensor(dst[:, 1, 4 * c:4 * c + 4, :], banks[6 + c][:, 0:4 * SLOTS].rearrange("p (a b) -> p a b", b=SLOTS),
                                          dst[:, 0, 4 * c:4 * c + 4, :].bitcast(F32), ALU.subtract)
                ins.then_inc(done, 1)

            def half(t, q):
                return t[:, q * 512:(q + 1) * 512]

            def read_gate_and_up(n, used, q):
                v.wait_ge(unit_used, used)
                if not isinstance(n, int):
                    v.wait_ge(hid_ready, n * 2)
                v.tensor_scalar(half(gate_t, q), banks[q][0:SLOTS, :], LIMIT, None, ALU.min).then_inc(gate_ready, 1)
                v.tensor_scalar(half(lin_t, q), banks[2 + q][0:SLOTS, :], LIMIT, -LIMIT, ALU.min, ALU.max).then_inc(glu_read, 1)

            def glu(n, q):
                v.wait_ge(gate_ready, n * 2 + (q + 1))
                v.wait_ge(glu_read, n * 2 + (q + 1))
                v.scalar_tensor_tensor(out=half(lin_t, q), in0=half(lin_t, q), scalar=1.0, in1=half(gate_t, q), op0=ALU.add, op1=ALU.mult).then_inc(glu_part, 1)

            def hidden(n, q):
                v.wait_ge(glu_part, n * 2 + (q + 1))
                v.wait_ge(sig_done, n * 2 + (q + 1))
                if not isinstance(n, int):
                    v.wait_ge(hid_turned, n)
                v.tensor_tensor(half(hid, q), half(lin_t, q), half(sig_t, q), ALU.mult).then_inc(hid_ready, 1)

            lower_turned(xsT, xsT_hi, 0, xsT_lo)
            for u in range(GU_UNITS):
                if u in BY_DVE:
                    lower(None, u)
                if u == 4:
                    v.wait_ge(unit_used, 1)
                    select_bias(slice(1, 2))
                    prepare(1, slice(1, 2))
                if u == 6:
                    gate_table()
                if u == 13:
                    indices(1, slice(2, 3))
                if u == 15:
                    v.wait_ge(dense_turned, 1)
                    v.tensor_copy(gates_T, banks[6][0:E, :].rearrange("p (a b) -> p a b", b=P)).then_inc(dense_ready, 1)
            for q in range(2):
                read_gate_and_up(0, GU_UNITS, q)
            v.wait_ge(table_ready, 2)
            lower_turned(xsT, xsT_hi, 1, xsT_lo)
            for q in range(2):
                glu(0, q)
            for q in range(2):
                hidden(0, q)
            prepare(2, slice(2, 3))
            v.wait_ge(table_ready, 2)
            trip = v.value_load(trips[0:1, 0:1], min_val=E - 1, max_val=E - 1 + EXTRA)
            with v.Fori(0, trip) as it:
                for u in range(UNITS):
                    if u in BY_DVE:
                        lower(it, u)
                    if u == 10:
                        v.wait_ge(y_out, it * 16 + 16)
                        v.wait_ge(idx_step, it * 3 + 3)
                        v.wait_ge(bufs_clear, 4)
                        v.tensor_copy(row_idx[:, :], row_tab[:, bass.ds(it, 1)]).then_inc(row_moved, 1)
                    if u == 4:
                        v.wait_ge(unit_used, it * UNITS + (UNITS + 1))
                        indices(it + 2, bass.ds(it + 3, 1))
                        select_bias(bass.ds(it + 2, 1))
                    if u == 9:
                        lower_turned(hidT, hidT_hi, it, hidT_lo)
                    if u == 14:
                        prepare(it + 3, bass.ds(it + 3, 1))
                    if u == 19:
                        for q in range(2):
                            read_gate_and_up(it + 1, it * UNITS + (UNITS + GU_UNITS), q)
                        for q in range(2):
                            glu(it + 1, q)
                    if u == 21:
                        for q in range(2):
                            hidden(it + 1, q)
                    if u == GU_UNITS + TURN_AFTER + 4:
                        lower_turned(xsT, xsT_hi, it + 2, xsT_lo)
            v.wait_ge(y_out, trip * 16 + 16)
            v.wait_ge(idx_step, trip * 3 + 3)
            v.tensor_copy(row_idx[:, :], row_tab[:, bass.ds(trip, 1)]).then_inc(row_moved, 1)
            lower_turned(hidT, hidT_hi, trip, hidT_lo)
            for u in range(GU_UNITS, UNITS):
                if u in BY_DVE:
                    lower(trip, u, GU_UNITS)
            v.wait_ge(y_out, trip * 16 + 32)
            v.tensor_copy(row_idx[:, :], row_tab[:, bass.ds(trip + 1, 1)]).then_inc(row_moved, 1)
            for m in range(2 * NT):
                v.wait_ge(bias_done, m + 1)
                o = res[:, m // 2, (m % 2) * 512:(m % 2 + 1) * 512]
                v.tensor_tensor(o, banks[m % 4][:, :], o, ALU.add).then_inc(base_ready, 1)
            v.wait_ge(base_ready, 2 * NT)
            def combine(i):
                for k in range(TOPK):
                    if k % 2 == 0:
                        v.wait_ge(picked_in[2 * i + k // 2], 16)
                    if k:
                        v.wait_ge(final_sum, TOPK * i + k)
                    v.scalar_tensor_tensor(out=res[:, i, :], in0=picked[i][:, k, :], scalar=gates[:, i, k:k + 1], in1=res[:, i, :],
                                           op0=ALU.mult, op1=ALU.add).then_inc(final_sum, 1)

            def finish(i):
                v.wait_ge(final_rt, i + 1)
                v.reciprocal(rs[:, i:i + 1], rs[:, i:i + 1]).then_inc(final_step, 1)
                v.wait_ge(final_step, i + 1)
                v.scalar_tensor_tensor(out=final_rows[i], in0=res[:, i, :], scalar=rs[:, i:i + 1], in1=g_final_b,
                                       op0=ALU.mult, op1=ALU.mult).then_inc(final_ready, 1)

            v.wait_ge(final_in, 16)
            for i in range(NT):
                combine(i)
                if i >= 1:
                    finish(i - 1)
            finish(NT - 1)

        @block.gpsimd
        def _(g):
            steps = [0]

            def step(ins):
                steps[0] += 1
                ins.then_inc(const_step, 1)
                g.wait_ge(const_step, steps[0])

            def triangle(t, compare, base, fill):
                return g.affine_select(out=t, in_=t, compare_op=compare, fill=fill, base=base, pattern=[[1, P]], channel_multiplier=-1)

            step(g.memset(ident[:, :], 0.0))
            triangle(ident[:, :], ALU.not_equal, 0, 1.0).then_inc(ident_ready, 1)
            g.memset(ones[:, :], 1.0).then_inc(ones_ready, 1)
            step(g.memset(ones_h[:, :], 1.0))
            step(g.memset(before[:, :], 1.0))
            step(triangle(before[:, :], ALU.is_gt, 0, 0.0))
            step(g.iota(slot_int, pattern=[[1, SLOTS]], base=0, channel_multiplier=0))
            step(g.tensor_copy(slot_no[:, :], slot_int))
            step(g.memset(ids[:, :, :], 1.0))
            step(g.iota(slot_int[:, 0:NT], pattern=[[0, NT]], base=0, channel_multiplier=TOPK))
            step(g.tensor_copy(ids[:, :, 0:1], slot_int[:, 0:NT].rearrange("p (a b) -> p a b", b=1)))
            step(g.iota(slot_int[:, 0:NT], pattern=[[TOPK * P, NT]], base=0, channel_multiplier=0))
            g.tensor_copy(ids[:, :, 1:2], slot_int[:, 0:NT].rearrange("p (a b) -> p a b", b=1)).then_inc(slots_ready, 1)
            row_no = slot_int[:, 8:9]
            step(g.iota(row_no, pattern=[[0, 1]], base=0, channel_multiplier=1))
            step(g.tensor_copy(bgu_row[:, :], row_no))
            step(g.tensor_scalar(bgu_past, bgu_row[:, :], float(E), -float(E), ALU.is_ge, ALU.mult))
            g.tensor_tensor(bgu_row[:, :], bgu_row[:, :], bgu_past, ALU.add).then_inc(rows_ready, 1)
            step(g.memset(neg_tri, -1.0))
            g.affine_select(out=neg_tri, in_=neg_tri, compare_op=ALU.is_ge, fill=0.0, base=0, pattern=[[-1, P]], channel_multiplier=1).then_inc(masks_ready, 1)
            g.memset(neg_one, -1.0).then_inc(masks_ready, 1)
            step(g.memset(causal, 1.0))
            triangle(causal, ALU.is_gt, 0, 0.0).then_inc(masks_ready, 1)
            for n in range(1, NT + 1, 2):
                lo = META + (n - 1) * P
                g.wait_ge(hT_hi, n + 1)
                g.tensor_tensor(hT[1][:, :, lo:lo + P], scaled[1], hT[0][:, :, lo:lo + P].bitcast(F32), ALU.subtract).then_inc(hT_lo[1], 1)
            g.wait_ge(masks_ready, 3)
            for s in range(NI + 2):
                if s < NI:
                    h, b = att_items[s]
                    t0, keys = span(b)
                    acc = later[h % 2]
                    if b >= 0:
                        g.wait_ge(masked, masks_before[s + 1])
                        if b == 3:
                            if s >= 2:
                                g.wait_ge(logw_done, s - 1)
                            g.memset(acc[:, 0:t0], 0.0)
                            g.tensor_copy(acc[:, t0:T], sp[s % NSP][:, 0:T - t0]).then_inc(later_done, 1)
                        else:
                            g.wait_ge(logw_done, s + 1)
                            g.wait_ge(later_done, masks_before[s - 1])
                            g.tensor_tensor(acc[:, t0:T], acc[:, t0:T], sp[s % NSP][:, 0:T - t0], ALU.add).then_inc(later_done, 1)
                if s >= 2:
                    i = s - 2
                    if att_items[i][1] >= 0:
                        g.wait_ge(w_done, i + 1)
                        w = wT[i % NW][:, 0:P]
                        g.affine_select(out=w, in_=w, compare_op=ALU.is_gt, fill=0.0, base=0, pattern=[[1, P]], channel_multiplier=-1).then_inc(w_masked, 1)

            last_token, last_row = g.to_reg(T - 1), g.to_reg(T * TOPK - 1)

            def gather(turned, ready):
                g.wait_ge(bufs_clear, 4)
                g.wait_ge(idx_ready, ready)
                g.wait_ge(xs_turned, turned)
                g.indirect_dma_start(xs, None, ffn_rows, bass.IndirectOffsetOnAxis(ap=tok_idx[:, 0:1], axis=0),
                                     bounds_check=last_token, oob_is_err=False).then_inc(xs_in, 16)

            def scatter(ready):
                g.wait_ge(bufs_clear, 4)
                g.wait_ge(ys_ready, ready)
                g.wait_ge(row_moved, ready)
                g.indirect_dma_start(choice_rows, bass.IndirectOffsetOnAxis(ap=row_idx[:, 0:1], axis=0), ys, None,
                                     bounds_check=last_row, oob_is_err=False).then_inc(y_out, 16)

            def lower(it, u, skip=0):
                if u < GU_UNITS or skip:
                    m = u - skip
                    g.wait_ge(gu_in[m // 2], 16 if it is None else it * 16 + 32)
                    src = gu_pair[m // 2][:, m % 2, :]
                else:
                    g.wait_ge(dn_in[(u - GU_UNITS) // 2], it * 16 + 16)
                    src = dn_pair[(u - GU_UNITS) // 2][:, u % 2, :]
                g.wait_ge(hi_done, through(BY_ALL, it, u, skip))
                g.tensor_tensor(stage[:, u % STAGES, 1, :], src, stage[:, u % STAGES, 0, :].bitcast(F32), ALU.subtract).then_inc(lo_pool, step_of(BY_POOL, it, u))

            one, two, three = (g.alloc_register(n) for n in ("one_more", "two_more", "three_more"))
            g.wait_ge(outp, 2 * NT)
            g.memset(ys, 0.0).then_inc(bufs_clear, 1)
            g.memset(xs, 0.0).then_inc(bufs_clear, 1)
            g.wait_ge(bufs_clear, 4)
            for i in range(NT):
                g.wait_ge(row_stored[i], 16)
            g.wait_ge(idx_ready, 1)
            g.indirect_dma_start(xs, None, ffn_rows, bass.IndirectOffsetOnAxis(ap=tok_idx[:, 0:1], axis=0),
                                 bounds_check=last_token, oob_is_err=False).then_inc(xs_in, 16)
            g.indirect_dma_start(choice_rows, bass.IndirectOffsetOnAxis(ap=row_idx[:, 0:1], axis=0), ys, None,
                                 bounds_check=last_row, oob_is_err=False).then_inc(y_out, 16)
            for u in BY_POOL:
                if u < GU_UNITS:
                    lower(None, u)
                if u == 11:
                    gather(1, 2)
            g.wait_ge(table_ready, 2)
            trip = g.value_load(trips[0:1, 0:1], min_val=E - 1, max_val=E - 1 + EXTRA)
            g.reg_mov(one, 1)
            g.reg_mov(two, 2)
            g.reg_mov(three, 3)
            with g.Fori(0, trip) as it:
                for u in BY_POOL:
                    lower(it, u)
                    if u == 3:
                        gather(two, three)
                    if u == 15:
                        scatter(one)
                g.reg_add(one, one, 1)
                g.reg_add(two, two, 1)
                g.reg_add(three, three, 1)
            scatter(one)
            for u in BY_POOL:
                if u >= GU_UNITS:
                    lower(trip, u, GU_UNITS)
            scatter(two)


_INS = ['x', 'meta_tokens', 'g_mix', 'w_in', 'g_attn_out', 'conv_w', 'conv_b', 'g_conv_out', 'w_out', 'g_ffn',
        'w_router', 'b_router', 'w_gu', 'b_gu', 'w_down', 'b_down', 'g_final']


def kernel(**inputs):
    import numpy as _np
    import concourse.bacc as _bacc
    from concourse import mybir as _mybir
    from concourse.bass_utils import run_bass_kernel_spmd as _run

    nc = _bacc.Bacc("TRN2", target_bir_lowering=False, num_devices=1)
    arrays, args = {}, []
    for name in _INS:
        a = _np.ascontiguousarray(inputs[name])
        arrays[f"in_{name}_dram"] = a
        args.append(nc.dram_tensor(f"in_{name}_dram", a.shape, _mybir.dt.from_np(a.dtype), kind="ExternalInput").ap())
    args.append(nc.dram_tensor("out_dram", (1, T, D), F32, kind="ExternalOutput").ap())
    build(nc, *args)
    r = _run(nc, [arrays], core_ids=[0])
    return r.results[0]["out_dram"]
```
